# Optimizing a Trainium2 kernel written in Bass

```python
import jax, jax.numpy as jnp
from jax import lax
import numpy as np
import math

D_MODEL = 1024
BATCH = 1
SEQ = 512
DEPTH = 1

DILATED_GROUPS = ((128, 1), (512, 4), (2048, 16))
N_ATT_GROUPS = 3
ATT_HEADS_PER_GROUP = 4
ATT_HEAD_DIM = 128
ATT_WIDTH = N_ATT_GROUPS * ATT_HEADS_PER_GROUP * ATT_HEAD_DIM
ATT_OUT_WIDTH = ATT_HEADS_PER_GROUP * ATT_HEAD_DIM
ATT_Q_BLOCK = 128
ROPE_THETA = 500000.0
ROPE_DIMS = ATT_HEAD_DIM // 4
MLSTM_HEADS = 4
MLSTM_WIDTH = D_MODEL
MLSTM_HEAD_DIM = MLSTM_WIDTH // MLSTM_HEADS
MLSTM_CHUNK = 64
CONV_WIDTH = 4
D_FF = ((8 * D_MODEL // 3 + 127) // 128) * 128
RMS_EPS = 1e-6
COL_SIZES = (ATT_WIDTH, ATT_WIDTH, ATT_WIDTH, 2 * MLSTM_WIDTH, MLSTM_WIDTH, MLSTM_WIDTH,
             MLSTM_HEADS, MLSTM_HEADS, D_MODEL, D_MODEL)
IN_WIDTH = 3 * ATT_WIDTH + 4 * MLSTM_WIDTH + 2 * MLSTM_HEADS + 2 * D_MODEL


def rmsnorm(x, g):
    xf = x.astype(jnp.float32)
    y = xf * lax.rsqrt(jnp.mean(xf * xf, axis=-1, keepdims=True) + RMS_EPS)
    return (y * g.astype(jnp.float32)).astype(x.dtype)

def swiglu(x, w_gate, w_up, w_down):
    return (jax.nn.silu(x @ w_gate) * (x @ w_up)) @ w_down

def partial_rope(x, positions):
    half = ROPE_DIMS // 2
    inv_freq = jnp.power(ROPE_THETA, -(jnp.arange(half, dtype=jnp.float32) * 2.0 / ROPE_DIMS))
    ang = positions.astype(jnp.float32)[:, None] * inv_freq[None, :]
    cos, sin = jnp.cos(ang)[:, None, :], jnp.sin(ang)[:, None, :]
    xf = x.astype(jnp.float32)
    x1, x2, xp = xf[..., :half], xf[..., half:ROPE_DIMS], xf[..., ROPE_DIMS:]
    out = jnp.concatenate([x1 * cos - x2 * sin, x2 * cos + x1 * sin, xp], axis=-1)
    return out.astype(x.dtype)

def dilated_window_attention(q, k, v, window, dilation):
    B, S, H, dh = q.shape
    L = S // dilation
    span = window // dilation
    bq = ATT_Q_BLOCK
    nblk = -(-L // bq)
    lp = nblk * bq

    def classes(t, front):
        t = t.reshape(B, L, dilation, H, dh)
        return jnp.pad(t, ((0, 0), (front, lp - L), (0, 0), (0, 0), (0, 0)))

    qb = classes(q, 0).reshape(B, nblk, bq, dilation, H, dh)
    idx = np.arange(nblk)[:, None] * bq + np.arange(bq + span)[None, :]
    kw = classes(k, span)[:, idx]
    vw = classes(v, span)[:, idx]
    s = jnp.einsum('bnirhc,bnjrhc->bnrhij', qb, kw).astype(jnp.float32) * (dh ** -0.5)
    qpos = np.arange(nblk)[:, None, None] * bq + np.arange(bq)[None, :, None]
    kpos = np.arange(nblk)[:, None, None] * bq - span + np.arange(bq + span)[None, None, :]
    dist = qpos - kpos
    valid = (dist >= 0) & (dist <= span) & (kpos >= 0)
    s = jnp.where(valid[None, :, None, None], s, -jnp.inf)
    m = jnp.max(s, axis=-1)
    p = jnp.exp(s - m[..., None])
    l = jnp.sum(p, axis=-1)
    o = jnp.einsum('bnrhij,bnjrhc->bnirhc', p, vw.astype(jnp.float32))
    o = o / jnp.moveaxis(l, -1, 2)[..., None]
    lse = jnp.moveaxis(m + jnp.log(l), -1, 2)
    o = o.reshape(B, lp, dilation, H, dh)[:, :L].reshape(B, S, H, dh)
    lse = lse.reshape(B, lp, dilation, H)[:, :L].reshape(B, S, H)
    return o, lse

def causal_depthwise_conv(x, w, b):
    S, K = x.shape[1], w.shape[0]
    xp = jnp.pad(x, ((0, 0), (K - 1, 0), (0, 0)))
    y = b + w[0] * xp[:, 0:S]
    for j in range(1, K):
        y = y + w[j] * xp[:, j:j + S]
    return y

def mlstm_chunkwise(q, k, v, i_pre, log_f):
    B, S, H, dh = q.shape
    lc = MLSTM_CHUNK
    nc = S // lc

    def chunks(t):
        return t.astype(jnp.float32).reshape(B, nc, lc, H, dh).transpose(1, 0, 3, 2, 4)

    def gchunks(t):
        return t.reshape(B, nc, lc, H).transpose(1, 0, 3, 2)

    qc, kc, vc = chunks(q), chunks(k) * (dh ** -0.5), chunks(v)
    ic, fc = gchunks(i_pre), gchunks(log_f)
    causal = np.tril(np.ones((lc, lc), dtype=bool))

    def step(carry, inp):
        C, n, m = carry
        qt, kt, vt, it, ft = inp
        b = jnp.cumsum(ft, axis=-1)
        D = jnp.where(causal, b[..., :, None] - b[..., None, :] + it[..., None, :], -jnp.inf)
        m_inter = b + m[..., None]
        m_t = jnp.maximum(m_inter, jnp.max(D, axis=-1))
        w = jnp.exp(D - m_t[..., None]) * jnp.einsum('bhtk,bhsk->bhts', qt, kt)
        inter = jnp.exp(m_inter - m_t)
        num = jnp.einsum('bhts,bhsv->bhtv', w, vt) + inter[..., None] * jnp.einsum('bhvk,bhtk->bhtv', C, qt)
        den = jnp.sum(w, axis=-1) + inter * jnp.einsum('bhk,bhtk->bht', n, qt)
        h = num / jnp.maximum(jnp.abs(den), jnp.exp(-m_t))[..., None]
        bl = b[..., -1]
        g = bl[..., None] - b + it
        m_new = jnp.maximum(bl + m, jnp.max(g, axis=-1))
        a = jnp.exp(g - m_new[..., None])
        decay = jnp.exp(bl + m - m_new)
        C_new = decay[..., None, None] * C + jnp.einsum('bhsv,bhsk->bhvk', a[..., None] * vt, kt)
        n_new = decay[..., None] * n + jnp.einsum('bhs,bhsk->bhk', a, kt)
        return (C_new, n_new, m_new), h

    init = (jnp.zeros((B, H, dh, dh), jnp.float32), jnp.zeros((B, H, dh), jnp.float32),
            jnp.zeros((B, H), jnp.float32))
    _, hs = lax.scan(step, init, (qc, kc, vc, ic, fc))
    return hs.transpose(1, 0, 3, 2, 4).reshape(B, S, H, dh)

def hybrid_mixer(h, positions, w_in, conv_w, conv_b, i_bias, f_bias, head_g,
                 w_att_branch, w_mlstm_branch, w_out):
    B, S, _ = h.shape
    proj = h @ w_in
    points = np.cumsum(np.array(COL_SIZES))[:-1].tolist()
    q_a, k_a, v_a, qk_m, v_m, o_m, i_pre, f_pre, g_a, g_m = jnp.split(proj, points, axis=-1)

    nh = N_ATT_GROUPS * ATT_HEADS_PER_GROUP
    q_a = partial_rope(q_a.reshape(B, S, nh, ATT_HEAD_DIM), positions)
    k_a = partial_rope(k_a.reshape(B, S, nh, ATT_HEAD_DIM), positions)
    q_a = q_a.reshape(B, S, N_ATT_GROUPS, ATT_HEADS_PER_GROUP, ATT_HEAD_DIM)
    k_a = k_a.reshape(B, S, N_ATT_GROUPS, ATT_HEADS_PER_GROUP, ATT_HEAD_DIM)
    v_a = v_a.reshape(B, S, N_ATT_GROUPS, ATT_HEADS_PER_GROUP, ATT_HEAD_DIM)
    outs, lses = [], []
    for g, (window, dilation) in enumerate(DILATED_GROUPS):
        o, lse = dilated_window_attention(q_a[:, :, g], k_a[:, :, g], v_a[:, :, g], window, dilation)
        outs.append(o)
        lses.append(lse)
    alpha = jax.nn.softmax(jnp.stack(lses, axis=0), axis=0)
    att = jnp.sum(alpha[..., None] * jnp.stack(outs, axis=0), axis=0)
    att = att.reshape(B, S, ATT_OUT_WIDTH).astype(h.dtype)

    qk = jax.nn.silu(causal_depthwise_conv(qk_m, conv_w, conv_b))
    q_m, k_m = jnp.split(qk, 2, axis=-1)
    shp = (B, S, MLSTM_HEADS, MLSTM_HEAD_DIM)
    ig = i_pre.astype(jnp.float32) + i_bias.astype(jnp.float32)
    lf = jax.nn.log_sigmoid(f_pre.astype(jnp.float32) + f_bias.astype(jnp.float32))
    hm = mlstm_chunkwise(q_m.reshape(shp), k_m.reshape(shp), v_m.reshape(shp), ig, lf)
    hm = hm * lax.rsqrt(jnp.mean(hm * hm, axis=-1, keepdims=True) + RMS_EPS)
    hm = hm * head_g.astype(jnp.float32).reshape(MLSTM_HEADS, MLSTM_HEAD_DIM)
    ml = (jax.nn.sigmoid(o_m.astype(jnp.float32)) * hm.reshape(B, S, MLSTM_WIDTH)).astype(h.dtype)

    merged = jax.nn.sigmoid(g_a) * (att @ w_att_branch) + jax.nn.sigmoid(g_m) * (ml @ w_mlstm_branch)
    return merged @ w_out

def first_inputs(seed: int = 0) -> dict:
    key = jax.random.key(seed)
    ks = jax.random.split(key, 24)
    f32 = jnp.float32

    def dense(k, fan_in, shape):
        return jax.random.normal(k, (DEPTH,) + shape, f32) * (fan_in ** -0.5)

    def gain(k, n):
        return 1.0 + 0.05 * jax.random.normal(k, (DEPTH, n), f32)

    return {
        'x': jax.random.normal(ks[0], (BATCH, SEQ, D_MODEL), f32),
        'ffn1_pre_g': gain(ks[1], D_MODEL),
        'ffn1_w_gate': dense(ks[2], D_MODEL, (D_MODEL, D_FF)),
        'ffn1_w_up': dense(ks[3], D_MODEL, (D_MODEL, D_FF)),
        'ffn1_w_down': dense(ks[4], D_FF, (D_FF, D_MODEL)),
        'ffn1_post_g': gain(ks[5], D_MODEL),
        'mix_pre_g': gain(ks[6], D_MODEL),
        'w_in': dense(ks[7], D_MODEL, (D_MODEL, IN_WIDTH)),
        'conv_w': dense(ks[8], CONV_WIDTH, (CONV_WIDTH, 2 * MLSTM_WIDTH)),
        'conv_b': 0.01 * jax.random.normal(ks[9], (DEPTH, 2 * MLSTM_WIDTH), f32),
        'mlstm_i_bias': 0.1 * jax.random.normal(ks[10], (DEPTH, MLSTM_HEADS), f32),
        'mlstm_f_bias': jnp.linspace(3.0, 6.0, MLSTM_HEADS, dtype=f32)[None, :]
                        + 0.1 * jax.random.normal(ks[11], (DEPTH, MLSTM_HEADS), f32),
        'mlstm_head_g': gain(ks[12], MLSTM_WIDTH),
        'w_att_branch': dense(ks[13], ATT_OUT_WIDTH, (ATT_OUT_WIDTH, D_MODEL)),
        'w_mlstm_branch': dense(ks[14], MLSTM_WIDTH, (MLSTM_WIDTH, D_MODEL)),
        'w_out': dense(ks[15], D_MODEL, (D_MODEL, D_MODEL)),
        'mix_post_g': gain(ks[16], D_MODEL),
        'ffn2_pre_g': gain(ks[17], D_MODEL),
        'ffn2_w_gate': dense(ks[18], D_MODEL, (D_MODEL, D_FF)),
        'ffn2_w_up': dense(ks[19], D_MODEL, (D_MODEL, D_FF)),
        'ffn2_w_down': dense(ks[20], D_FF, (D_FF, D_MODEL)),
        'ffn2_post_g': gain(ks[21], D_MODEL),
    }

def first_block(x, ffn1_pre_g, ffn1_w_gate, ffn1_w_up, ffn1_w_down, ffn1_post_g,
              mix_pre_g, w_in, conv_w, conv_b, mlstm_i_bias, mlstm_f_bias, mlstm_head_g,
              w_att_branch, w_mlstm_branch, w_out, mix_post_g,
              ffn2_pre_g, ffn2_w_gate, ffn2_w_up, ffn2_w_down, ffn2_post_g):
    positions = jnp.arange(x.shape[1], dtype=jnp.int32)
    for l in range(DEPTH):
        f = swiglu(rmsnorm(x, ffn1_pre_g[l]), ffn1_w_gate[l], ffn1_w_up[l], ffn1_w_down[l])
        x = x + 0.5 * rmsnorm(f, ffn1_post_g[l])
        y = hybrid_mixer(rmsnorm(x, mix_pre_g[l]), positions, w_in[l], conv_w[l], conv_b[l],
                         mlstm_i_bias[l], mlstm_f_bias[l], mlstm_head_g[l],
                         w_att_branch[l], w_mlstm_branch[l], w_out[l])
        x = x + rmsnorm(y, mix_post_g[l])
        f = swiglu(rmsnorm(x, ffn2_pre_g[l]), ffn2_w_gate[l], ffn2_w_up[l], ffn2_w_down[l])
        x = x + 0.5 * rmsnorm(f, ffn2_post_g[l])
    return x


DEPTH_2 = 2

N_MIXERS = 2
N_HEADS = 16
HEAD_DIM = 64
N_KV_HEADS = 4
GROUP = N_HEADS // N_KV_HEADS
IDX_HEADS = 8
IDX_DIM = 64
TOPK_MAX = 256
Q_BLOCK = 128
ROPE_THETA_2 = 10000.0
CONV_WIDTH_2 = 3
FFN_HIDDEN = int(math.ceil(8 * D_MODEL / 3 / 256) * 256)
NORM_EPS = 1e-6
N_A = (DEPTH_2 + 1) // 2
N_B = DEPTH_2 // 2

Q_COLS = N_HEADS * HEAD_DIM
K_COLS = N_KV_HEADS * HEAD_DIM
V_COLS = N_KV_HEADS * HEAD_DIM
QI_COLS = IDX_HEADS * IDX_DIM
KI_COLS = IDX_DIM
WI_COLS = IDX_HEADS
ATTN_IN_COLS = Q_COLS + K_COLS + V_COLS + QI_COLS + KI_COLS + WI_COLS


def _rmsnorm(x, g):
    xf = x.astype(jnp.float32)
    y = xf * lax.rsqrt(jnp.mean(xf * xf, axis=-1, keepdims=True) + NORM_EPS)
    return (y * g.astype(jnp.float32)).astype(x.dtype)

def _layernorm(x, g, b):
    xf = x.astype(jnp.float32)
    mu = jnp.mean(xf, axis=-1, keepdims=True)
    var = jnp.mean(jnp.square(xf - mu), axis=-1, keepdims=True)
    y = (xf - mu) * lax.rsqrt(var + NORM_EPS)
    return (y * g.astype(jnp.float32) + b.astype(jnp.float32)).astype(x.dtype)

def _rope(x, pos):
    d = x.shape[-1]
    half = d // 2
    inv_freq = ROPE_THETA_2 ** (-(jnp.arange(half, dtype=jnp.float32) * 2.0 / d))
    ang = pos.astype(jnp.float32)[..., None] * inv_freq
    cos = jnp.cos(ang)[:, :, None, :]
    sin = jnp.sin(ang)[:, :, None, :]
    xf = x.astype(jnp.float32)
    x1, x2 = xf[..., :half], xf[..., half:]
    out = jnp.concatenate([x1 * cos - x2 * sin, x2 * cos + x1 * sin], axis=-1)
    return out.astype(x.dtype)

def _dsa_mixer(h, positions, w_in, q_norm_g, k_norm_g, idx_k_ln_g, idx_k_ln_b, w_out):
    Bn, T, _ = h.shape
    proj = h @ w_in
    o0 = 0
    q = proj[..., o0:o0 + Q_COLS].reshape(Bn, T, N_HEADS, HEAD_DIM); o0 += Q_COLS
    k = proj[..., o0:o0 + K_COLS].reshape(Bn, T, N_KV_HEADS, HEAD_DIM); o0 += K_COLS
    v = proj[..., o0:o0 + V_COLS].reshape(Bn, T, N_KV_HEADS, HEAD_DIM); o0 += V_COLS
    qi = proj[..., o0:o0 + QI_COLS].reshape(Bn, T, IDX_HEADS, IDX_DIM); o0 += QI_COLS
    ki = proj[..., o0:o0 + KI_COLS]; o0 += KI_COLS
    wi = proj[..., o0:o0 + WI_COLS]

    q = _rope(_rmsnorm(q, q_norm_g), positions)
    k = _rope(_rmsnorm(k, k_norm_g), positions)
    qi = _rope(qi, positions)
    ki = _rope(_layernorm(ki, idx_k_ln_g, idx_k_ln_b)[:, :, None, :], positions)[:, :, 0, :]
    wi = wi * (IDX_HEADS ** -0.5 * IDX_DIM ** -0.5)

    topk = min(TOPK_MAX, T // 4)
    n_blk = T // Q_BLOCK
    key_idx = jnp.arange(T)
    scale = HEAD_DIM ** -0.5

    def to_blocks(a):
        return jnp.moveaxis(a.reshape(Bn, n_blk, Q_BLOCK, *a.shape[2:]), 1, 0)

    def block_fn(args):
        qb, qib, wib, start = args
        t_idx = start + jnp.arange(Q_BLOCK)
        s = jnp.einsum('bqhd,bsd->bqhs', qib, ki)
        score = jnp.einsum('bqhs,bqh->bqs', jax.nn.relu(s), wib).astype(jnp.float32)
        causal = key_idx[None, :] <= t_idx[:, None]
        score = jnp.where(causal[None], score, -jnp.inf)
        _, sel = lax.top_k(score, topk)
        sel_ok = sel <= t_idx[None, :, None]
        kg = jax.vmap(lambda a, i: a[i])(k, sel)
        vg = jax.vmap(lambda a, i: a[i])(v, sel)
        qg = qb.reshape(Bn, Q_BLOCK, N_KV_HEADS, GROUP, HEAD_DIM)
        logits = jnp.einsum('bqgrd,bqkgd->bqgrk', qg, kg).astype(jnp.float32) * scale
        logits = jnp.where(sel_ok[:, :, None, None, :], logits, -1e30)
        p = jax.nn.softmax(logits, axis=-1).astype(vg.dtype)
        o = jnp.einsum('bqgrk,bqkgd->bqgrd', p, vg)
        return o.reshape(Bn, Q_BLOCK, N_HEADS * HEAD_DIM)

    starts = jnp.arange(n_blk) * Q_BLOCK
    o = lax.map(block_fn, (to_blocks(q), to_blocks(qi), to_blocks(wi), starts))
    o = jnp.moveaxis(o, 0, 1).reshape(Bn, T, N_HEADS * HEAD_DIM)
    return o @ w_out

def _short_conv_mixer(h, w_in, conv_w, w_out):
    proj = h @ w_in
    b_gate, c_gate, u = jnp.split(proj, 3, axis=-1)
    z = c_gate * u
    z = lax.conv_general_dilated(
        z, conv_w[:, None, :].astype(z.dtype),
        window_strides=(1,), padding=[(CONV_WIDTH_2 - 1, 0)],
        dimension_numbers=('NWC', 'WIO', 'NWC'),
        feature_group_count=z.shape[-1])
    return (b_gate * z) @ w_out

def _swiglu(h, w_gate, w_up, w_down):
    return (jax.nn.silu(h @ w_gate) * (h @ w_up)) @ w_down

def second_inputs(seed: int = 0) -> dict:
    key = jax.random.key(seed)
    ks = jax.random.split(key, 20)
    D = D_MODEL

    def nrm(k, shape, s):
        return jax.random.normal(k, shape, dtype=jnp.float32) * s

    x = nrm(ks[0], (BATCH, SEQ, D), 1.0)
    c = nrm(ks[1], (BATCH, D), 1.0)
    positions = (jnp.arange(SEQ, dtype=jnp.int32)[None, :]
                 + jax.random.randint(ks[2], (BATCH, 1), 0, 1024, dtype=jnp.int32))
    ada_w = nrm(ks[3], (DEPTH_2, D, 6 * D), 0.5 * D ** -0.5)
    ada_b = nrm(ks[4], (DEPTH_2, 6 * D), 0.02)
    norm1_g = 1.0 + nrm(ks[5], (DEPTH_2, D), 0.02)
    norm2_g = 1.0 + nrm(ks[6], (DEPTH_2, D), 0.02)
    attn_w_in = nrm(ks[7], (N_A, D, ATTN_IN_COLS), D ** -0.5)
    attn_q_norm_g = 1.0 + nrm(ks[8], (N_A, HEAD_DIM), 0.02)
    attn_k_norm_g = 1.0 + nrm(ks[9], (N_A, HEAD_DIM), 0.02)
    idx_k_ln_g = 1.0 + nrm(ks[10], (N_A, IDX_DIM), 0.02)
    idx_k_ln_b = nrm(ks[11], (N_A, IDX_DIM), 0.02)
    attn_w_out = nrm(ks[12], (N_A, N_HEADS * HEAD_DIM, D), (N_HEADS * HEAD_DIM) ** -0.5)
    conv_w_in = nrm(ks[13], (N_B, D, 3 * D), D ** -0.5)
    conv_w = nrm(ks[14], (N_B, CONV_WIDTH_2, D), CONV_WIDTH_2 ** -0.5)
    conv_w_out = nrm(ks[15], (N_B, D, D), D ** -0.5)
    ffn_w_gate = nrm(ks[16], (DEPTH_2, D, FFN_HIDDEN), D ** -0.5)
    ffn_w_up = nrm(ks[17], (DEPTH_2, D, FFN_HIDDEN), D ** -0.5)
    ffn_w_down = nrm(ks[18], (DEPTH_2, FFN_HIDDEN, D), FFN_HIDDEN ** -0.5)
    return {"x": x, "c": c, "positions": positions,
            "ada_w": ada_w, "ada_b": ada_b, "norm1_g": norm1_g, "norm2_g": norm2_g,
            "attn_w_in": attn_w_in, "attn_q_norm_g": attn_q_norm_g,
            "attn_k_norm_g": attn_k_norm_g, "idx_k_ln_g": idx_k_ln_g,
            "idx_k_ln_b": idx_k_ln_b, "attn_w_out": attn_w_out,
            "conv_w_in": conv_w_in, "conv_w": conv_w, "conv_w_out": conv_w_out,
            "ffn_w_gate": ffn_w_gate, "ffn_w_up": ffn_w_up, "ffn_w_down": ffn_w_down}

def second_block(x, c, positions, ada_w, ada_b, norm1_g, norm2_g,
              attn_w_in, attn_q_norm_g, attn_k_norm_g, idx_k_ln_g, idx_k_ln_b, attn_w_out,
              conv_w_in, conv_w, conv_w_out, ffn_w_gate, ffn_w_up, ffn_w_down):
    c_act = jax.nn.silu(c)
    for i in range(DEPTH_2):
        mod = c_act @ ada_w[i] + ada_b[i]
        sh1, sc1, g1, sh2, sc2, g2 = [m[:, None, :] for m in jnp.split(mod, 6, axis=-1)]
        h = _rmsnorm(x, norm1_g[i]) * (1.0 + sc1) + sh1
        if i % N_MIXERS == 0:
            j = i // N_MIXERS
            y = _dsa_mixer(h, positions, attn_w_in[j], attn_q_norm_g[j], attn_k_norm_g[j],
                           idx_k_ln_g[j], idx_k_ln_b[j], attn_w_out[j])
        else:
            j = i // N_MIXERS
            y = _short_conv_mixer(h, conv_w_in[j], conv_w[j], conv_w_out[j])
        x = x + g1 * y
        h = _rmsnorm(x, norm2_g[i]) * (1.0 + sc2) + sh2
        x = x + g2 * _swiglu(h, ffn_w_gate[i], ffn_w_up[i], ffn_w_down[i])
    return x


def setup_inputs(seed=0):
    out = dict(first_inputs(seed))
    for name, value in second_inputs(seed + 1).items():
        if name != "x":
            out[name + "_2"] = value
    return out


def reference(
    x, ffn1_pre_g, ffn1_w_gate, ffn1_w_up, ffn1_w_down, ffn1_post_g, mix_pre_g, w_in, conv_w,
    conv_b, mlstm_i_bias, mlstm_f_bias, mlstm_head_g, w_att_branch, w_mlstm_branch, w_out,
    mix_post_g, ffn2_pre_g, ffn2_w_gate, ffn2_w_up, ffn2_w_down, ffn2_post_g, c_2, positions_2,
    ada_w_2, ada_b_2, norm1_g_2, norm2_g_2, attn_w_in_2, attn_q_norm_g_2, attn_k_norm_g_2,
    idx_k_ln_g_2, idx_k_ln_b_2, attn_w_out_2, conv_w_in_2, conv_w_2, conv_w_out_2, ffn_w_gate_2,
    ffn_w_up_2, ffn_w_down_2,
):
    x = first_block(
        x, ffn1_pre_g, ffn1_w_gate, ffn1_w_up, ffn1_w_down, ffn1_post_g, mix_pre_g, w_in,
        conv_w, conv_b, mlstm_i_bias, mlstm_f_bias, mlstm_head_g, w_att_branch, w_mlstm_branch,
        w_out, mix_post_g, ffn2_pre_g, ffn2_w_gate, ffn2_w_up, ffn2_w_down, ffn2_post_g,
    )
    return second_block(
        x, c_2, positions_2, ada_w_2, ada_b_2, norm1_g_2, norm2_g_2, attn_w_in_2,
        attn_q_norm_g_2, attn_k_norm_g_2, idx_k_ln_g_2, idx_k_ln_b_2, attn_w_out_2, conv_w_in_2,
        conv_w_2, conv_w_out_2, ffn_w_gate_2, ffn_w_up_2, ffn_w_down_2,
    )


_drawn_inputs = setup_inputs


def setup_inputs(seed=0):
    import zlib

    import numpy as np

    out = dict(_drawn_inputs(seed))
    spreads = {}
    factors = {'conv_b': 8.0,
     'mlstm_i_bias': 64.0,
     'ffn2_post_g': 3.201,
     'norm1_g_2': 6.359,
     'norm2_g_2': 8.0,
     'attn_q_norm_g_2': 8.0,
     'attn_k_norm_g_2': 8.0,
     'idx_k_ln_g_2': 8.0,
     'idx_k_ln_b_2': 8.0}
    for name, (base, spread) in spreads.items():
        noise = np.random.default_rng([zlib.crc32(name.encode()), seed]).standard_normal(out[name].shape)
        drawn = base * np.exp(spread * noise) if base else spread * noise
        out[name] = __import__('jax').numpy.asarray(drawn.astype(out[name].dtype))
    for name, factor in factors.items():
        out[name] = (out[name] * factor).astype(out[name].dtype)
    return out
```

```python
from contextlib import ExitStack

import numpy as np

import concourse.bass as bass
from concourse import mybir

F32 = mybir.dt.float32
F32R = mybir.dt.float32r
I32 = mybir.dt.int32
ALU = mybir.AluOpType
ACT = mybir.ActivationFunctionType
AX = mybir.AxisListType

P = 128
T = 512
D = 1024
DK = D // P
FF = 2816
FK = FF // P
EPS = 1e-6
NEG = -3.0e38
MASKED = -1.0e30

NRAW = 4
NSPL = 3

INV_2PI = 0.15915494309189535
PI_A = 6.28125
PI_B = 1.9350051879882812e-03
PI_C = 3.0199157663446332e-07
PI = 3.141592653589793
ROUND = 12582912.0
SIN_MAX = 3.1415925

C_ID, C_ONE, C_FM, C_LOW, C_TRI, C_B64, C_R1, C_R2, C_SEL, C_INVF, C_EPS = (
    0, 128, 256, 1792, 1920, 2048, 2176, 2208, 2336, 2848, 2849)
C_N = 2850


def constants():
    c = np.zeros((P, C_N), np.float32)
    i = np.arange(P)
    c[:, C_ID:C_ID + P] = np.eye(P)
    c[:, C_ONE:C_ONE + P] = 1.0
    t, s = 384 + i[:, None], np.arange(T)[None, :]
    d = t - s
    for g, ok in enumerate(((d >= 0) & (d <= 128), (d >= 0) & (d % 4 == 0), (d >= 0) & (d % 16 == 0))):
        c[:, C_FM + g * T:C_FM + (g + 1) * T] = np.where(ok, 0.0, MASKED)
    c[:, C_LOW:C_LOW + P] = i[:, None] <= i[None, :]
    c[:, C_TRI:C_TRI + P] = np.where(i[None, :] <= i[:, None], 0.0, NEG)
    c[:, C_B64:C_B64 + P] = i[:, None] // 64 == i[None, :] // 64
    for m in range(16):
        c[m + 16, C_R1 + m] = -1.0
        c[m, C_R1 + m + 16] = 1.0
    for b in (0, 64):
        for m in range(32):
            c[b + m + 32, C_R2 + b + m] = -1.0
            c[b + m, C_R2 + b + m + 32] = 1.0
    for h in range(4):
        c[h, C_SEL + h * P:C_SEL + (h + 1) * P] = 1.0
    f2 = np.float32(10000.0) ** (-(np.arange(32, dtype=np.float32) * np.float32(2.0) / np.float32(64.0)))
    c[:, C_INVF] = f2[i % 32]
    c[:, C_EPS] = EPS
    f1 = np.float32(500000.0) ** (-(np.arange(16, dtype=np.float32) * np.float32(2.0) / np.float32(32.0)))
    ang = (np.arange(T, dtype=np.float32)[None, :] * f1[np.arange(32) % 16][:, None]).astype(np.float32)
    cs = np.concatenate([np.cos(ang), np.sin(ang)], axis=1).astype(np.float32)
    return c, cs


class Ring:

    def __init__(self, aps):
        self.aps, self.free, self.n = list(aps), [None] * len(aps), 0

    def take(self):
        i = self.n % len(self.aps)
        self.n += 1
        return i, self.aps[i], self.free[i]


class Queues:

    def __init__(self, sems):
        self.sems = sems
        self.ops = {e: [] for e in ("pe", "act", "dve", "pool", "sp")}
        self.count = {s: 0 for s in sems}
        self.seen = {e: {} for e in self.ops}

    def put(self, eng, fn, a, k, w, sem, step):
        q, seen = self.ops[eng], self.seen[eng]
        for t in w:
            if t is not None and seen.get(t[0], 0) < t[1]:
                seen[t[0]] = t[1]
                q.append(("wait", self.sems[t[0]], t[1]))
        if sem is None:
            q.append(("op", fn, a, k, None, 0))
            return None
        self.count[sem] += step
        q.append(("op", fn, a, k, self.sems[sem], step))
        return (sem, self.count[sem])

    def now(self):
        return [(s, self.count[s]) for s in ("pe", "act", "dve", "pool")]

    def run(self, eng, e):
        for op in self.ops[eng]:
            if op[0] == "wait":
                e.wait_ge(op[1], op[2])
            else:
                ins = op[1](*op[2], **op[3])
                if op[4] is not None:
                    ins.then_inc(op[4], op[5])


class Split:

    def __init__(self, hi, lo):
        self.hi, self.lo, self.tok = hi, lo, {}


def program(nc, q, mem, A, out, cst, cs_tab, plan):
    chunks = []
    V, S, G, PE, SP = nc.vector, nc.scalar, nc.gpsimd, nc.tensor, nc.sync

    def dve(fn, *a, w=(), **k):
        return q.put("dve", fn, a, k, w, "dve", 1)

    def act(fn, *a, w=(), **k):
        return q.put("act", fn, a, k, w, "act", 1)

    def pool(fn, *a, w=(), **k):
        return q.put("pool", fn, a, k, w, "pool", 1)

    def mm(o, l, r, start, stop, w=(), done=False):
        return q.put("pe", PE.matmul, (o, l, r), dict(start=start, stop=stop), w, "pe" if done else None, 1)

    def tr(o, i, ident, w=(), done=False):
        return q.put("pe", PE.transpose, (o, i, ident), {}, w, "pe" if done else None, 1)

    def load(o, i, sem, w=(), eng="sp"):
        fn = SP.dma_start if eng == "sp" else G.dma_start
        return q.put(eng, fn, (o, i), {}, w, sem, 16)

    C = mem["C"]
    ident, ones = C[:, C_ID:C_ID + P], C[:, C_ONE:C_ONE + P]
    eps = C[:, C_EPS:C_EPS + 1]
    X, HH, HL, F16 = mem["X"], mem["HH"], mem["HL"], mem["F16"]
    TS = mem["TS"]
    PS = mem["PS"]
    VT, MOD, SM = mem["VT"], mem["MOD"], mem["SM"]
    bfree = [None] * 8

    def bank(b):
        return PS[:, b, :]

    st = dict(use=0, dma=0, spl=0, nspl=0)
    raw_done, raw_tok, spl_tok, pe_done = {}, {}, {}, {}
    spl_index = {}
    if plan is not None:
        for i, c in enumerate(plan):
            if c[2]:
                spl_index[i] = len(spl_index)
    spl_list = sorted(spl_index)
    RAW, WH, WL = mem["RAW"], mem["WH"], mem["WL"]

    def issue_dma(j):
        pieces, nk, _ = plan[j]
        r = j % NRAW
        for c0, ap in pieces:
            n = ap.shape[1]
            tok = load(RAW[:, r, 0:nk, c0:c0 + n], ap.rearrange("(k p) n -> p k n", p=P), f"raw{r}",
                       w=[raw_done.get(j - NRAW)])
        raw_tok[j] = tok

    def issue_split(j):
        pieces, nk, _ = plan[j]
        r, i = j % NRAW, spl_index[j]
        s = i % NSPL
        wd = max(c0 + ap.shape[1] for c0, ap in pieces)
        prev = pe_done[spl_list[i - NSPL]] if i >= NSPL else None
        t = act(S.activation, WH[:, s, 0:nk, 0:wd], RAW[:, r, 0:nk, 0:wd], ACT.Copy, w=[raw_tok[j], prev])
        t = dve(V.tensor_tensor, WL[:, s, 0:nk, 0:wd], RAW[:, r, 0:nk, 0:wd],
                WH[:, s, 0:nk, 0:wd].bitcast(F32), ALU.subtract, w=[t, raw_tok[j], prev])
        spl_tok[j] = raw_done[j] = t

    def advance(i):
        while True:
            j = st["dma"]
            if j < len(plan) and j <= i + NRAW and (j < NRAW or j - NRAW in raw_done):
                issue_dma(j)
                st["dma"] += 1
                continue
            j = st["spl"]
            if j < st["dma"] and j <= i + 3:
                if not plan[j][2]:
                    st["spl"] += 1
                    continue
                n = spl_index[j]
                if n < NSPL or spl_list[n - NSPL] in pe_done:
                    issue_split(j)
                    st["spl"] += 1
                    continue
            break

    def use(pieces, nk, split=True):
        i = st["use"]
        st["use"] += 1
        chunks.append((pieces, nk, split))
        if plan is None:
            return i, RAW[:, 0], None, None, None
        advance(i)
        if split:
            s = spl_index[i] % NSPL
            return i, None, WH[:, s], WL[:, s], spl_tok[i]
        return i, RAW[:, i % NRAW], None, None, raw_tok[i]

    def used(i, split, tok):
        pe_done[i] = tok
        if not split:
            raw_done[i] = tok

    def wslice(w, r0, nk, c0, n):
        return [(0, w[r0:r0 + nk * P, c0:c0 + n])]

    jobs = []
    background = []

    def pump():
        while jobs and jobs[0][0] > 0:
            jobs[0][1]()
            jobs[0][0] -= 1
            break
        if background:
            try:
                next(background[0])
            except StopIteration:
                background.pop(0)

    def drain():
        while background:
            try:
                next(background[0])
            except StopIteration:
                background.pop(0)

    def fm(pieces, nk, x, kt0, b, first=True, last=True, n=P):
        if plan is None:
            use(pieces, nk)
            return None
        i, _, wh, wl, wt = use(pieces, nk)
        o = PS[0:n, b, :]
        for k in range(nk):
            kk = kt0 + k
            w = [wt, x.tok[kk]] + ([bfree[b]] if first and k == 0 else [])
            end = last and k == nk - 1
            mm(o, wh[:, k, 0:n], x.hi[:, kk, :], first and k == 0, False, w=w)
            mm(o, wh[:, k, 0:n], x.lo[:, kk, :], False, False)
            t = mm(o, wl[:, k, 0:n], x.hi[:, kk, :], False, end, done=k == nk - 1)
        used(i, True, t)
        return t

    def tm(pieces, x, b, n, c0=0):
        if plan is None:
            use(pieces, DK)
            return None
        i, _, wh, wl, wt = use(pieces, DK)
        for tb in range(4):
            o = PS[:, b, tb * n:(tb + 1) * n]
            ts = slice(tb * P, (tb + 1) * P)
            for k in range(DK):
                w = [wt, x.tok[k]] + ([bfree[b]] if tb == 0 and k == 0 else [])
                mm(o, x.hi[:, k, ts], wh[:, k, c0:c0 + n], k == 0, False, w=w)
                mm(o, x.lo[:, k, ts], wh[:, k, c0:c0 + n], False, False)
                t = mm(o, x.hi[:, k, ts], wl[:, k, c0:c0 + n], False, k == DK - 1, done=tb == 3 and k == DK - 1)
        used(i, True, t)
        return t

    t_c = load(C[:, :], cst, "c")
    XR, VS = mem["XR"], mem["VS"]
    for tb in range(4):
        t_x = load(XR[:, tb, :], A["x"][0, tb * P:(tb + 1) * P, :], "x")

    def rows(ap, n):
        return ap.rearrange("a (r c) -> (a r) c", c=P) if len(ap.shape) == 2 else ap.rearrange("a j (r c) -> (a j r) c", c=P)

    stage = [
        [("ffn1_pre_g", 8), ("ffn1_post_g", 8), ("mix_pre_g", 8), ("mix_post_g", 8), ("ffn2_pre_g", 8),
         ("ffn2_post_g", 8), ("mlstm_head_g", 8), ("conv_b", 16), ("attn_q_norm_g_2", 1), ("attn_k_norm_g_2", 1),
         ("idx_k_ln_g_2", 1), ("idx_k_ln_b_2", 1), ("c_2", 8)],
        [("conv_w", 64), ("norm1_g_2", 16), ("norm2_g_2", 16), ("conv_w_2", 24)],
        [("ada_b_2", 96)],
    ]
    col, n_all, sizes = {}, 0, []
    for g, names in enumerate(stage):
        r = 0
        for name, n in names:
            col[name] = n_all + r
            if n == 1:
                for half in (0, 64):
                    t_vs = load(VS[r:r + 1, g, half:half + 64], A[name], "vs")
            elif name == "ada_b_2":
                t_vs = load(VS[r:r + n, g, :], A[name].rearrange("l (r c) -> (l r) c", c=P), "vs")
            elif name in ("norm1_g_2", "norm2_g_2"):
                t_vs = load(VS[r:r + n, g, :], A[name].rearrange("l (r c) -> (l r) c", c=P), "vs")
            else:
                t_vs = load(VS[r:r + n, g, :], rows(A[name], n), "vs")
            r += n
        sizes.append((n_all, r))
        n_all += r
    IB, FB = mem["IB"], mem["FB"]
    t_vs = load(IB[:, :], A["mlstm_i_bias"].rearrange("a h -> h a"), "vs")
    t_vs = load(FB[:, :], A["mlstm_f_bias"].rearrange("a h -> h a"), "vs")

    def vec(name, k=0):
        c = col[name] + k
        return VT[:, c:c + 1]

    if plan is not None:
        advance(-1)

    t_v = None
    for g, (c0, n) in enumerate(sizes):
        t = tr(PS[:, 7, c0:c0 + n], VS[0:n, g, :], C[0:n, C_ID:C_ID + n], w=[t_vs, t_c], done=True)
    t_v = dve(V.tensor_copy, VT[:, 0:n_all], PS[:, 7, 0:n_all], w=[t])
    bfree[7] = t_v
    HG = mem["HG"]
    t_hg = dve(V.tensor_scalar, HG[:, 0:8], VT[:, col["ffn1_post_g"]:col["ffn1_post_g"] + 8], 0.5, None, ALU.mult, w=[t_v])
    t_hg = dve(V.tensor_scalar, HG[:, 8:16], VT[:, col["ffn2_post_g"]:col["ffn2_post_g"] + 8], 0.5, None, ALU.mult, w=[t_v])

    lring = Ring(range(8))
    x_tok = [None] * DK
    acc, rstd = TS[:, 6, :], TS[:, 7, :]
    sq = Ring([TS[:, 4, :], TS[:, 5, :]])
    nt = Ring([TS[:, i, :] for i in range(4)])
    ss = dict(tok=None, n=0, free=None)

    def sumsq(src, w):
        if ss["n"] == 0:
            t0 = act(S.activation, acc, src, ACT.Square, w=list(w) + [ss["free"]])
            ss["tok"] = t0
        else:
            i, ap, fr = sq.take()
            t0 = act(S.activation, ap, src, ACT.Square, w=list(w) + [fr])
            ss["tok"] = sq.free[i] = dve(V.tensor_tensor, acc, acc, ap, ALU.add, w=[t0, ss["tok"]])
        ss["n"] += 1
        return t0

    def finish_rstd(b):
        t = mm(bank(b), ones, acc, True, True, w=[ss["tok"], bfree[b], t_c], done=True)
        ss["free"], ss["n"] = t, 0
        t = act(S.activation, rstd, bank(b), ACT.Sqrt, bias=eps, scale=1.0 / D, w=[t] + q.now())
        bfree[b] = t
        return dve(V.reciprocal, rstd, rstd, w=[t])

    H = Split(HH, HL)

    def write_h(t_r, gain, shift=None):
        for k in range(DK):
            i, ap, fr = nt.take()
            t = dve(V.scalar_tensor_tensor, ap, X[:, k, :], gain(k), rstd, ALU.mult, ALU.mult, w=[t_r, x_tok[k], fr])
            if shift is None:
                t2 = act(S.activation, HH[:, k, :], ap, ACT.Copy, w=[t])
                t3 = dve(V.tensor_tensor, HL[:, k, :], ap, HH[:, k, :].bitcast(F32), ALU.subtract, w=[t2, t])
            else:
                t2 = act(S.activation, HH[:, k, :], ap, ACT.Identity, bias=shift(k), w=[t])
                t3 = dve(V.scalar_tensor_tensor, HL[:, k, :], ap, shift(k), HH[:, k, :].bitcast(F32),
                         ALU.add, ALU.subtract, w=[t2, t])
            nt.free[i] = t3
            H.tok[k] = t3

    def split_to(x, k, src, w, cols=slice(0, T), rows_=slice(0, P)):
        hi, lo = x.hi[rows_, k, cols], x.lo[rows_, k, cols]
        t = act(S.activation, hi, src, ACT.Copy, w=w)
        t = dve(V.tensor_tensor, lo, src, hi.bitcast(F32), ALU.subtract, w=[t] + list(w))
        x.tok[k] = t
        return t

    for k in range(DK):
        b = k % 4
        for tb in range(4):
            t = tr(PS[:, b, tb * P:(tb + 1) * P], XR[:, tb, k * P:(k + 1) * P], ident,
                   w=[t_x, t_c, bfree[b]], done=tb == 3)
        x_tok[k] = dve(V.tensor_copy, X[:, k, :], bank(b), w=[t])
        bfree[b] = sumsq(bank(b), [t, x_tok[k]])

    CA = mem["CA"]
    t_ca = act(S.activation, CA[:, :], VT[:, col["c_2"]:col["c_2"] + 8], ACT.Silu, w=[t_v])
    mod = dict(n=0, tok=None)

    def ada_job():
        n = mod["n"]
        mod["n"] += 1
        pieces = wslice(A["ada_w_2"][n // 48], 0, DK, (n % 48) * P, P)
        if plan is None:
            use(pieces, DK, False)
            return
        i, raw, _, _, wt = use(pieces, DK, False)
        for k in range(DK):
            t = mm(PS[:, 7, n:n + 1], raw[:, k, :], CA[:, k:k + 1], k == 0, k == DK - 1,
                   w=[wt, t_ca, bfree[7]], done=k == DK - 1)
        used(i, False, t)
        mod["tok"] = t

    U = Split(mem["UH"], mem["UL"])
    silu_r = Ring([TS[:, 0, :], TS[:, 1, :]])
    prod_r = Ring([TS[:, 2, :], TS[:, 3, :]])

    def ffn_up(wg, wu):
        for n in range(FK):
            bg, bu = (2 * n) % 4, (2 * n) % 4 + 1
            tg = fm(wslice(wg, 0, DK, n * P, P), DK, H, 0, bg)
            pump()
            tu = fm(wslice(wu, 0, DK, n * P, P), DK, H, 0, bu)
            pump()
            i, s_ap, fr = silu_r.take()
            ts_ = act(S.activation, s_ap, bank(bg), ACT.Silu, w=[tg, fr])
            bfree[bg] = ts_
            j, p_ap, fr = prod_r.take()
            tp = dve(V.tensor_tensor, p_ap, s_ap, bank(bu), ALU.mult, w=[ts_, tu, fr])
            silu_r.free[i] = bfree[bu] = tp
            prod_r.free[j] = split_to(U, n, p_ap, [tp])

    def ffn_down(wd, n, b):
        for c, nk in ((0, 8), (8, 8), (16, 6)):
            t = fm(wslice(wd, c * P, nk, n * P, P), nk, U, c, b, first=c == 0, last=c == 16)
            pump()
        return t

    def residual(t_r, gain):
        for k in range(DK):
            i, ap, fr = nt.take()
            t = dve(V.scalar_tensor_tensor, ap, F16[:, k, :], gain(k), rstd, ALU.mult, ALU.mult, w=[t_r, fr, t_hg])
            x_tok[k] = dve(V.tensor_tensor, X[:, k, :], X[:, k, :], ap, ALU.add, w=[t])
            nt.free[i] = x_tok[k]
            sumsq(X[:, k, :], [x_tok[k]])

    def keep_f(n, b, t):
        act(S.activation, F16[:, n, :], bank(b), ACT.Copy, w=[t])
        bfree[b] = sumsq(bank(b), [t])

    def ffn_first(pre, wg, wu, wd, post):
        t_r = finish_rstd(4)
        write_h(t_r, lambda k: vec(pre, k))
        ffn_up(wg, wu)
        for n in range(DK):
            keep_f(n, n % 4, ffn_down(wd, n, n % 4))
        t_r = finish_rstd(4)
        residual(t_r, lambda k: HG[:, post + k:post + k + 1])

    jobs.append([96, ada_job])
    ffn_first("ffn1_pre_g", A["ffn1_w_gate"][0], A["ffn1_w_up"][0], A["ffn1_w_down"][0], 0)
    while jobs and jobs[0][0] > 0:
        jobs[0][1]()
        jobs[0][0] -= 1
    jobs.clear()
    b0 = col["ada_b_2"]
    t_mod = dve(V.tensor_tensor, MOD[:, 0:96], PS[:, 7, 0:96], VT[:, b0:b0 + 96], ALU.add, w=[mod["tok"]])
    bfree[7] = t_mod
    for l in range(2):
        for j, name in enumerate(("norm1_g_2", "norm2_g_2")):
            o = 96 + 16 * l + 8 * j
            sc = 48 * l + 24 * j + 8
            g0 = col[name] + 8 * l
            dve(V.scalar_tensor_tensor, MOD[:, o:o + 8], MOD[:, sc:sc + 8], 1.0, VT[:, g0:g0 + 8],
                ALU.add, ALU.mult, w=[t_mod])

    t_r = finish_rstd(4)
    CS1 = mem["CS1"]
    t_cs = load(CS1[0:32, :], cs_tab, "cs", w=q.now(), eng="pool")
    write_h(t_r, lambda k: vec("mix_pre_g", k))
    w_in = A["w_in"][0]
    SETS = mem["SETS"]
    set_free = [[], []]
    AT, ML, MG = Split(mem["ATH"], mem["ATL"]), Split(mem["MLH"], mem["MLL"]), Split(mem["MGH"], mem["MGL"])

    lb = Ring([0, 1])

    def lbank():
        i, b, _ = lb.take()
        return b

    xb = Ring([5, 6])

    def xbank():
        i, b, _ = xb.take()
        return b

    b = lbank()
    ti = fm(wslice(w_in, 0, DK, 8704, P), DK, H, 0, b)
    ig, xf, nz, lf, cb, av = (TS[0:4, i, :] for i in range(6))
    MX, EM = TS[0:4, 7, :], TS[0:4, 8, :]
    t_ig = dve(V.tensor_scalar, ig, PS[0:4, b, :], IB[:, 0:1], None, ALU.add, w=[ti, t_vs] + q.now())
    bfree[b] = t_ig
    b = lbank()
    tf = fm(wslice(w_in, 0, DK, 8708, P), DK, H, 0, b)
    t = dve(V.tensor_scalar, xf, PS[0:4, b, :], FB[:, 0:1], None, ALU.add, w=[tf, t_vs] + q.now())
    bfree[b] = t
    t1 = act(S.activation, nz, xf, ACT.Abs, w=[t])
    t1 = act(S.activation, nz, nz, ACT.Exp, scale=-1.0, w=[t1])
    t1 = act(S.activation, nz, nz, ACT.Ln, bias=C[0:4, C_ONE:C_ONE + 1], w=[t1])
    t = dve(V.scalar_tensor_tensor, lf, xf, 0.0, nz, ALU.min, ALU.subtract, w=[t1, t])
    t = dve(V.memset, xf, 1.0, w=[t])
    t = dve(V.tensor_tensor_scan, cb, xf, lf, 0.0, ALU.mult, ALU.add, w=[t])
    t = dve(V.tensor_tensor, av, ig, cb, ALU.subtract, w=[t, t_ig])
    t_av = t
    t = dve(V.tensor_tensor_scan, MX, av, av, 0.0, ALU.max, ALU.max, w=[t])
    t_mx = t
    t = dve(V.tensor_tensor, EM, cb, MX, ALU.add, w=[t])
    t_em = act(S.activation, EM, EM, ACT.Exp, scale=-1.0, w=[t])
    AVT = mem["AVT"]
    b = xbank()
    for sb in range(4):
        t = tr(PS[:, b, sb * 4:sb * 4 + 4], av[:, sb * P:(sb + 1) * P], C[0:4, C_ID:C_ID + 4],
               w=[t_av, bfree[b]], done=sb == 3)
    t_avt = dve(V.tensor_copy, AVT[:, :], PS[:, b, 0:16], w=[t])
    bfree[b] = t_avt

    rope_t = Ring([TS[:, 5, :], TS[:, 6, :]])

    def att_project(hd, s):
        free = set_free[s]
        tok = {}
        for g in range(3):
            for which, base in ((0, 0), (1, 1536)):
                dst = SETS[:, s, 2 * g + which, :]
                b = lbank()
                t = fm(wslice(w_in, 0, DK, base + (4 * g + hd) * P, P), DK, H, 0, b)
                pump()
                t = act(S.activation, dst, bank(b), ACT.Copy, w=[t] + free)
                bfree[b] = t
                x = xbank()
                t2 = mm(PS[0:32, x, :], C[0:32, C_R1:C_R1 + 32], dst[0:32, :], True, True, w=[t, bfree[x]], done=True)
                i, ap, fr = rope_t.take()
                t3 = dve(V.tensor_tensor, ap[0:32, :], PS[0:32, x, :], CS1[0:32, T:2 * T], ALU.mult, w=[t2, fr, t_cs, t_avt])
                bfree[x] = t3
                t4 = dve(V.tensor_tensor, dst[0:32, :], dst[0:32, :], CS1[0:32, 0:T], ALU.mult, w=[t, t2])
                t4 = dve(V.tensor_tensor, dst[0:32, :], dst[0:32, :], ap[0:32, :], ALU.add, w=[t4, t3])
                rope_t.free[i] = t4
                tok[2 * g + which] = [t, t4]
            b = lbank()
            t = tm(wslice(w_in, 0, DK, 3072 + (4 * g + hd) * P, P), H, b, P)
            pump()
            t = act(S.activation, SETS[:, s, 6 + g, :], bank(b), ACT.Copy, w=[t] + free)
            bfree[b] = t
            tok[6 + g] = [t]
        return tok

    sm_n = [0]

    def small():
        c = sm_n[0] % 32
        sm_n[0] += 1
        return SM[:, 2 * c:2 * c + 1]

    pt_r = Ring([TS[:, 3, :], TS[:, 4, :]])
    att = dict(s_free=None, p_free=None)
    SCALE = float(P) ** -0.5

    def attention(hd, s, tok):
        yield
        for tb in range(4):
            W = (tb + 1) * P
            ts = slice(tb * P, (tb + 1) * P)
            for g in range(3):
                t = mm(PS[:, 2 + g, 0:W], SETS[:, s, 2 * g, ts], SETS[:, s, 2 * g + 1, 0:W], True, True,
                       w=tok[2 * g] + tok[2 * g + 1] + [att["s_free"]], done=g == 2)
            pr = TS[:, 0:3, 0:W]
            t = dve(V.scalar_tensor_tensor, pr, PS[:, 2:5, 0:W], SCALE,
                    C[:, C_FM:C_FM + 3 * T].rearrange("p (g t) -> p g t", g=3)[:, :, T - W:T],
                    ALU.mult, ALU.add, w=[t, att["p_free"]] + (q.now() if hd == 0 and tb == 0 else []))
            att["s_free"] = t
            mx, l = small(), small()
            t = dve(V.tensor_reduce, mx, pr, AX.XY, ALU.max, negate=True, w=[t])
            t = act(S.activation, pr, pr, ACT.Exp, bias=mx, accum_out=l, w=[t])
            t = dve(V.reciprocal, l, l, w=[t])
            t_p = dve(V.tensor_scalar, pr, pr, l, None, ALU.mult, w=[t])
            yield
            blocks = [(g, sb) for g in range(3) for sb in range(tb + 1) if g > 0 or sb >= tb - 1]
            done = 0
            while done < len(blocks):
                part = blocks[done:done + 4]
                b = xbank()
                for j, (g, sb) in enumerate(part):
                    t = tr(PS[:, b, j * P:(j + 1) * P], TS[:, g, sb * P:(sb + 1) * P], ident,
                           w=[t_p, bfree[b]], done=j == len(part) - 1)
                att["p_free"] = t
                i, ap, fr = pt_r.take()
                n = len(part) * P
                t = act(S.activation, ap[:, 0:n], PS[:, b, 0:n], ACT.Copy, w=[t, fr])
                bfree[b] = t
                for j, (g, sb) in enumerate(part):
                    m = done + j
                    t2 = mm(PS[:, 7, 0:P], SETS[:, s, 6 + g, sb * P:(sb + 1) * P], ap[:, j * P:(j + 1) * P],
                            m == 0, m == len(blocks) - 1, w=[t, bfree[7]] + tok[6 + g], done=j == len(part) - 1)
                pt_r.free[i] = t2
                done += len(part)
            bfree[7] = split_to(AT, hd, PS[:, 7, 0:P], [t2], cols=ts)
            set_free[s] = [t2, att["s_free"]]
            yield

    def ml_project(hd, s):
        free = set_free[s]
        tok = {}
        for which in range(2):
            for c in range(2):
                cc = which * 8 + hd * 2 + c
                dst = SETS[:, s, 2 * which + c, :]
                b = lbank()
                t = fm(wslice(w_in, 0, DK, 4608 + cc * P, P), DK, H, 0, b)
                pump()
                wv = [vec("conv_w", j * 16 + cc) for j in range(4)]
                t2 = dve(V.tensor_scalar, dst, bank(b), wv[3], vec("conv_b", cc), ALU.mult, ALU.add, w=[t] + free)
                for d in range(1, 4):
                    t2 = dve(V.scalar_tensor_tensor, dst[:, d:T], PS[:, b, 0:T - d], wv[3 - d], dst[:, d:T],
                             ALU.mult, ALU.add, w=[t2])
                bfree[b] = t2
                tok[2 * which + c] = [act(S.activation, dst, dst, ACT.Silu, w=[t2])]
        for c in range(2):
            b = lbank()
            t = tm(wslice(w_in, 0, DK, 6656 + hd * 256 + c * P, P), H, b, P)
            pump()
            t = act(S.activation, SETS[:, s, 4 + c, :], bank(b), ACT.Copy, w=[t] + free)
            bfree[b] = t
            tok[4 + c] = [t]
        for c in range(2):
            b = lbank()
            t = fm(wslice(w_in, 0, DK, 7680 + hd * 256 + c * P, P), DK, H, 0, b)
            pump()
            t = act(S.activation, SETS[:, s, 6 + c, :], bank(b), ACT.Sigmoid, w=[t] + free)
            bfree[b] = t
            tok[6 + c] = [t]
        return tok

    sfree = [None] * 3

    def mlstm(hd, s, tok):
        yield
        start = q.now()
        sel = C[0:4, C_SEL + hd * P:C_SEL + (hd + 1) * P]
        b = xbank()
        t = mm(bank(b), sel, MX, True, True, w=[t_mx, bfree[b]], done=True)
        gt = []
        for sb in range(4):
            o = TS[:, sb, sb * P:T]
            c = sb * 4 + hd
            t2 = dve(V.tensor_scalar, o, PS[:, b, sb * P:T], AVT[:, c:c + 1], 0.0, ALU.subtract, ALU.max, w=[t] + start)
            gt.append(t2)
        bfree[b] = t2
        gt = [act(S.activation, TS[:, sb, sb * P:T], TS[:, sb, sb * P:T], ACT.Exp, scale=-1.0, w=[gt[sb]]) for sb in range(4)]
        yield
        wt = []
        for sb in range(4):
            z = sb % 2
            ns = slice(sb * P, T)
            for c in range(2):
                t = mm(PS[:, 2 + z, ns], SETS[:, s, 2 + c, sb * P:(sb + 1) * P], SETS[:, s, c, ns], c == 0, c == 1,
                       w=tok[c] + tok[2 + c] + [sfree[z], att["s_free"]], done=c == 1)
            t = dve(V.scalar_tensor_tensor, TS[:, sb, ns], PS[:, 2 + z, ns], 1.0 / 16.0, TS[:, sb, ns],
                    ALU.mult, ALU.mult, w=[t, gt[sb]])
            sfree[z] = t
            dg = TS[:, sb, sb * P:(sb + 1) * P]
            wt.append(dve(V.tensor_tensor, dg, dg, C[:, C_LOW:C_LOW + P], ALU.mult, w=[t]))
            if sb % 2:
                yield
        bd, be = xbank(), xbank()
        nb = [7, 4]
        for sb in range(4):
            ns = slice(sb * P, T)
            td = mm(PS[:, bd, ns], ones, TS[:, sb, ns], sb == 0, sb == 3, w=[wt[sb], bfree[bd]], done=sb == 3)
        te = mm(bank(be), sel, EM, True, True, w=[t_em, bfree[be]], done=True)
        tn = []
        for c in range(2):
            for sb in range(4):
                ns = slice(sb * P, T)
                t = mm(PS[:, nb[c], ns], SETS[:, s, 4 + c, sb * P:(sb + 1) * P], TS[:, sb, ns], sb == 0, sb == 3,
                       w=tok[4 + c] + [bfree[nb[c]], att["s_free"]], done=sb == 3)
            tn.append(t)
        dn = TS[:, 4, :]
        t = act(S.activation, dn, bank(bd), ACT.Abs, w=[td] + start)
        bfree[bd] = t
        t = dve(V.tensor_tensor, dn, dn, bank(be), ALU.max, w=[t, te])
        bfree[be] = t
        t = dve(V.reciprocal, dn, dn, w=[t])
        hm, sqt = [TS[:, 5, :], TS[:, 6, :]], [TS[:, 0, :], TS[:, 1, :]]
        th, tq = [], []
        for c in range(2):
            t2 = dve(V.tensor_tensor, hm[c], dn, bank(nb[c]), ALU.mult, w=[t, tn[c]] + start)
            bfree[nb[c]] = t2
            th.append(t2)
            tq.append(act(S.activation, sqt[c], hm[c], ACT.Square, w=[t2, tn[1]]))
        t_dn = th[1]
        t = dve(V.tensor_tensor, sqt[0], sqt[0], sqt[1], ALU.add, w=tq)
        yield
        b = xbank()
        t = mm(bank(b), ones, sqt[0], True, True, w=[t, bfree[b]], done=True)
        t = act(S.activation, dn, bank(b), ACT.Sqrt, bias=eps, scale=1.0 / 256.0, w=[t, t_dn])
        bfree[b] = t
        t = dve(V.reciprocal, dn, dn, w=[t])
        for c in range(2):
            t2 = dve(V.scalar_tensor_tensor, hm[c], hm[c], vec("mlstm_head_g", 2 * hd + c), dn, ALU.mult, ALU.mult, w=[t] + tq)
            t2 = dve(V.tensor_tensor, hm[c], hm[c], SETS[:, s, 6 + c, :], ALU.mult, w=[t2] + tok[6 + c])
            t2 = split_to(ML, 2 * hd + c, hm[c], [t2])
        set_free[s] = [t2, tn[1]]
        yield

    n_head = 0
    for hd in range(4):
        tok = att_project(hd, n_head % 2)
        drain()
        background.append(attention(hd, n_head % 2, tok))
        n_head += 1
    for hd in range(4):
        tok = ml_project(hd, n_head % 2)
        drain()
        background.append(mlstm(hd, n_head % 2, tok))
        n_head += 1
    drain()

    before = q.now()
    wa, wm = A["w_att_branch"][0], A["w_mlstm_branch"][0]
    gate_r = Ring([TS[:, 0, :], TS[:, 1, :], TS[:, 2, :], TS[:, 3, :]])
    for n in range(DK):
        parts = []
        for j, (gc, w, x, nk) in enumerate(((8712, wa, AT, 4), (9736, wm, ML, 8))):
            b = 2 * j
            t = fm(wslice(w_in, 0, DK, gc + n * P, P), DK, H, 0, b)
            i, ap, fr = gate_r.take()
            t = act(S.activation, ap, bank(b), ACT.Sigmoid, w=[t, fr] + before)
            bfree[b] = t
            t2 = fm(wslice(w, 0, nk, n * P, P), nk, x, 0, b + 1)
            t = dve(V.tensor_tensor, ap, ap, bank(b + 1), ALU.mult, w=[t, t2])
            bfree[b + 1] = t
            parts.append((i, ap, t))
        (i0, a0, t0), (i1, a1, t1) = parts
        t = dve(V.tensor_tensor, a0, a0, a1, ALU.add, w=[t0, t1])
        gate_r.free[i1] = t
        gate_r.free[i0] = split_to(MG, n, a0, [t])
    w_out = A["w_out"][0]
    for n in range(DK):
        keep_f(n, n % 4, fm(wslice(w_out, 0, DK, n * P, P), DK, MG, 0, n % 4))
    t_r = finish_rstd(4)
    residual(t_r, lambda k: vec("mix_post_g", k))
    ffn_first("ffn2_pre_g", A["ffn2_w_gate"][0], A["ffn2_w_up"][0], A["ffn2_w_down"][0], 8)

    def mods(l, j):
        o = 96 + 16 * l + 8 * j
        sh, gt = 48 * l + 24 * j, 48 * l + 24 * j + 16
        return (lambda k: MOD[:, o + k:o + k + 1], lambda k: MOD[:, sh + k:sh + k + 1],
                lambda k: MOD[:, gt + k:gt + k + 1])

    CS2, POSI = mem["CS2"], mem["POSI"]
    before = q.now()
    t_pos = load(POSI[:, :], A["positions_2"][0:1, :].to_broadcast([P, T]), "pos", w=before, eng="pool")
    pf, ang, kr, tmp = (TS[:, i, :] for i in range(4))
    t = dve(V.tensor_copy, pf, POSI[:, :], w=[t_pos] + before)
    t = dve(V.tensor_scalar, ang, pf, C[:, C_INVF:C_INVF + 1], None, ALU.mult, w=[t])
    t = dve(V.tensor_scalar, kr, ang, INV_2PI, ROUND, ALU.mult, ALU.add, w=[t])
    t = dve(V.tensor_scalar, kr, kr, ROUND, None, ALU.subtract, w=[t])
    for p in (PI_A, PI_B, PI_C):
        t = dve(V.scalar_tensor_tensor, ang, kr, -p, ang, ALU.mult, ALU.add, w=[t])
    cosT, sinT = CS2[:, 0, :], CS2[:, 1, :]
    t1 = dve(V.tensor_scalar, sinT, ang, SIN_MAX, -SIN_MAX, ALU.min, ALU.max, w=[t])
    t2 = dve(V.tensor_scalar, ang, ang, PI / 2, None, ALU.add, w=[t1])
    t2 = dve(V.tensor_scalar, tmp, ang, PI, -2.0 * PI, ALU.is_gt, ALU.mult, w=[t2])
    t2 = dve(V.tensor_tensor, ang, ang, tmp, ALU.add, w=[t2])
    t2 = dve(V.tensor_scalar, cosT, ang, SIN_MAX, -SIN_MAX, ALU.min, ALU.max, w=[t2])
    t1 = act(S.activation, sinT, sinT, ACT.Sin, w=[t1, t2])
    t_cs2 = act(S.activation, cosT, cosT, ACT.Sin, w=[t2])
    for i in range(4):
        nt.free[i] = t2

    gain, shift, gate = mods(0, 0)
    t_r = finish_rstd(4)
    write_h(t_r, gain, shift)
    QT, KD, VV, QI, KI = mem["QT"], mem["KD"], mem["VV"], mem["QI"], mem["KI"]
    MASK, WI, SCW = mem["MASK"], mem["WI"], mem["SCW"]
    O = Split(mem["OH"], mem["OL"])
    w_att = A["attn_w_in_2"][0]
    B64 = C[:, C_B64:C_B64 + P]
    before = q.now()
    xr = Ring([TS[:, 0, :], TS[:, 1, :]])
    rr = Ring([TS[:, 3, :], TS[:, 4, :]])

    def rope(x_ap, t_x_, dst, i):
        b = xbank()
        t = mm(bank(b), C[:, C_R2:C_R2 + P], x_ap, True, True, w=[t_x_, bfree[b]], done=True)
        j, ap, fr = rr.take()
        t2 = dve(V.tensor_tensor, ap, bank(b), sinT, ALU.mult, w=[t, fr, t_cs2])
        bfree[b] = t2
        t3 = dve(V.tensor_tensor, dst, x_ap, cosT, ALU.mult, w=[t, t_x_, t_cs2])
        t3 = dve(V.tensor_tensor, dst, dst, ap, ALU.add, w=[t3, t2])
        rr.free[j] = xr.free[i] = t3
        return t3

    b = lbank()
    t = fm([(0, w_att[:, 2048:2112]), (64, w_att[:, 2048:2112])], DK, H, 0, b)
    i, x, fr = xr.take()
    t = act(S.activation, x, bank(b), ACT.Copy, w=[t, fr] + before)
    bfree[b] = t
    xbk = xbank()
    t2 = mm(bank(xbk), B64, x, True, True, w=[t, bfree[xbk]], done=True)
    t = dve(V.scalar_tensor_tensor, x, bank(xbk), -1.0 / 64.0, x, ALU.mult, ALU.add, w=[t2, t] + before)
    bfree[xbk] = t
    s2 = TS[:, 2, :]
    t2 = act(S.activation, s2, x, ACT.Square, w=[t] + before)
    xbk = xbank()
    t2 = mm(bank(xbk), B64, s2, True, True, w=[t2, bfree[xbk]], done=True)
    s2_free = t2
    t2 = act(S.activation, s2, bank(xbk), ACT.Sqrt, bias=eps, scale=1.0 / 64.0, w=[t2])
    bfree[xbk] = t2
    t2 = dve(V.reciprocal, s2, s2, w=[t2])
    t = dve(V.tensor_tensor, x, x, s2, ALU.mult, w=[t, t2])
    t = dve(V.tensor_scalar, x, x, vec("idx_k_ln_g_2"), vec("idx_k_ln_b_2"), ALU.mult, ALU.add, w=[t])
    s2_free = t
    t_ki = rope(x, t, KI[:, :], i)

    b = lbank()
    t = tm(wslice(w_att, 0, DK, 2112, 8), H, b, 8)
    t_wi = dve(V.tensor_scalar, WI[:, :], PS[:, b, 0:32], float(8 ** -0.5 * 64 ** -0.5), None, ALU.mult, w=[t] + before)
    bfree[b] = t_wi
    t_qi = []
    for c in range(4):
        b = lbank()
        t = fm(wslice(w_att, 0, DK, 1536 + c * P, P), DK, H, 0, b)
        i, x, fr = xr.take()
        t = act(S.activation, x, bank(b), ACT.Copy, w=[t, fr])
        bfree[b] = t
        t_qi.append(rope(x, t, QI[:, c, :], i))

    t_mask = [None] * 4
    tri = C[:, C_TRI:C_TRI + P]
    rel = Ring([TS[:, 5, :], TS[:, 6, :]])
    sring = Ring([2, 3, 4])
    M8 = mem["M8"]

    def indexer():
        t_mask[0] = dve(V.tensor_scalar, MASK[:, 0, 0:P], tri, MASKED, None, ALU.max, w=before)
        sc_free, w_free = None, None
        for tb in range(1, 4):
            W = (tb + 1) * P
            ts = slice(tb * P, (tb + 1) * P)
            sc, wk = SCW[:, 0, 0:W], SCW[:, 1, 0:W]
            for h in range(8):
                i, b, _ = sring.take()
                r = slice(64 * (h % 2), 64 * (h % 2) + 64)
                t = mm(PS[:, b, 0:W], QI[r, h // 2, ts], KI[r, 0:W], True, True, w=[t_qi[h // 2], t_ki, bfree[b]], done=True)
                wi = WI[:, tb * 8 + h:tb * 8 + h + 1]
                if h == 0:
                    ta = dve(V.tensor_scalar, sc, PS[:, b, 0:W], 0.0, wi, ALU.max, ALU.mult, w=[t, t_wi] + before)
                    bfree[b] = ta
                else:
                    j, ap, fr = rel.take()
                    t = act(S.activation, ap[:, 0:W], PS[:, b, 0:W], ACT.Relu, w=[t, fr])
                    bfree[b] = t
                    ta = dve(V.scalar_tensor_tensor, sc, ap[:, 0:W], wi, sc, ALU.mult, ALU.add, w=[t, ta])
                    rel.free[j] = ta
                if h % 2:
                    yield
            ta = dve(V.tensor_tensor, sc[:, W - P:W], sc[:, W - P:W], tri, ALU.add, w=[ta])
            src = sc
            for n in range(16):
                ta = dve(V.max, M8[:, :], src, w=[ta])
                if n < 15:
                    ta = dve(V.match_replace, wk, M8[:, :], src, -3.4e38, w=[ta])
                    src = wk
                if n % 4 == 3:
                    yield
            cnt, need = small(), small()
            thr = M8[:, 7:8]
            gt, eq, pf_ = TS[:, 7, 0:W], TS[:, 8, 0:W], wk
            ta = dve(V.tensor_scalar, gt, sc, thr, None, ALU.is_gt, ALU.add, accum_out=cnt, w=[ta])
            tn_ = dve(V.tensor_scalar, need, cnt, -1.0, 128.0, ALU.mult, ALU.add, w=[ta])
            te_ = dve(V.tensor_scalar, eq, sc, thr, None, ALU.is_equal, w=[ta])
            te_ = dve(V.tensor_tensor_scan, pf_, eq, eq, 0.0, ALU.add, ALU.bypass, w=[te_])
            te_ = dve(V.scalar_tensor_tensor, eq, pf_, need, eq, ALU.is_le, ALU.mult, w=[te_, tn_])
            te_ = dve(V.tensor_tensor, gt, gt, eq, ALU.add, w=[te_])
            t_mask[tb] = dve(V.tensor_scalar, MASK[:, tb, 0:W], gt, -1.0, -MASKED, ALU.add, ALU.mult, w=[te_])
            yield

    background.append(indexer())
    s2f = [s2_free]

    def normed(c0, gname, dst, t_dst):
        b = lbank()
        t = fm(wslice(w_att, 0, DK, c0, P), DK, H, 0, b)
        pump()
        i, x, fr = xr.take()
        t = act(S.activation, x, bank(b), ACT.Copy, w=[t, fr])
        t2 = act(S.activation, s2, bank(b), ACT.Square, w=[s2f[0]])
        bfree[b] = t2
        xbk = xbank()
        t2 = mm(bank(xbk), B64, s2, True, True, w=[t2, bfree[xbk]], done=True)
        t2 = act(S.activation, s2, bank(xbk), ACT.Sqrt, bias=eps, scale=1.0 / 64.0, w=[t2])
        bfree[xbk] = t2
        t2 = dve(V.reciprocal, s2, s2, w=[t2])
        t = dve(V.scalar_tensor_tensor, x, x, vec(gname), s2, ALU.mult, ALU.mult, w=[t, t2])
        s2f[0] = t
        pump()
        return rope(x, t, dst, i)

    t_q = [normed(c * P, "attn_q_norm_g_2", QT[:, c, :], None) for c in range(8)]
    t_k = []
    for c in range(2):
        kt = mem["KT"][:, c, :]
        t = normed(1024 + c * P, "attn_k_norm_g_2", kt, None)
        for j in range(2):
            src = kt[64 * j:64 * j + 64, :]
            act(S.activation, KD[0:64, 2 * c + j, :], src, ACT.Copy, w=[t])
            t2 = act(S.activation, KD[64:128, 2 * c + j, :], src, ACT.Copy, w=[t])
            t_k.append(t2)
    t_vv = []
    for c in range(2):
        b = lbank()
        t = tm(wslice(w_att, 0, DK, 1280 + c * P, P), H, b, P)
        pump()
        t = act(S.activation, VV[:, :, c * P:(c + 1) * P], bank(b).rearrange("p (t n) -> p t n", t=4), ACT.Copy, w=[t] + before)
        bfree[b] = t
        t_vv.append(t)
    drain()

    pr_r = Ring([TS[:, i, :] for i in range(4, 9)])
    PT = TS[:, 0:4, :].rearrange("p s (a b t) -> p s a b t", a=2, b=2)
    before = q.now()
    pt_free = None

    def probs(tb, g, i4):
        h = 4 * g + i4
        W = (tb + 1) * P
        r = slice(64 * (h % 2), 64 * (h % 2) + 64)
        _, b, _ = sring.take()
        t = mm(PS[:, b, 0:W], QT[r, h // 2, tb * P:(tb + 1) * P], KD[r, g, 0:W], True, True,
               w=[t_q[h // 2], t_k[g], bfree[b]], done=True)
        j, ap, fr = pr_r.take()
        pr = ap[:, 0:W]
        t = dve(V.scalar_tensor_tensor, pr, PS[:, b, 0:W], 0.125, MASK[:, tb, 0:W], ALU.mult, ALU.add,
                w=[t, fr, t_mask[tb]] + before)
        bfree[b] = t
        mx, l = small(), small()
        t = dve(V.tensor_reduce, mx, pr, AX.X, ALU.max, negate=True, w=[t])
        t = act(S.activation, pr, pr, ACT.Exp, bias=mx, accum_out=l, w=[t])
        t = dve(V.reciprocal, l, l, w=[t])
        t = dve(V.tensor_scalar, pr, pr, l, None, ALU.mult, w=[t])
        return j, ap, t

    def turned(tb, g, i4, j, ap, t, pt_free):
        b = xbank()
        for sb in range(tb + 1):
            t2 = tr(PS[:, b, sb * P:(sb + 1) * P], ap[:, sb * P:(sb + 1) * P], ident, w=[t, bfree[b]], done=sb == tb)
        pr_r.free[j] = t2
        t2 = act(S.activation, PT[:, 0:tb + 1, i4 % 2, i4 // 2, :],
                 PS[:, b, 0:(tb + 1) * P].rearrange("p (s t) -> p s t", t=P), ACT.Copy, w=[t2, pt_free])
        bfree[b] = t2
        return t2

    items = [(tb, g, i4) for tb in range(4) for g in range(4) for i4 in range(4)]
    ready = {}
    AHEAD = 3
    for n in range(len(items) + AHEAD):
        if n < len(items):
            ready[n] = probs(*items[n])
        m = n - AHEAD
        if m < 0:
            continue
        tb, g, i4 = items[m]
        t = turned(tb, g, i4, *ready.pop(m), pt_free)
        if i4 < 3:
            continue
        for par in range(2):
            for sb in range(tb + 1):
                t2 = mm(PS[64 * par:64 * par + 64, 7, 0:256], VV[:, sb, g * 64:(g + 1) * 64],
                        PT[:, sb, par, :, :].rearrange("p b t -> p (b t)"), sb == 0, sb == tb,
                        w=[t, t_vv[g // 2], bfree[7]], done=par == 1 and sb == tb)
        pt_free = t2
        t = t2
        for i2 in range(2):
            t = split_to(O, 2 * g + i2, PS[:, 7, i2 * P:(i2 + 1) * P], [t2, t], cols=slice(tb * P, (tb + 1) * P))
        bfree[7] = t

    def gated(n, b, t, gate_):
        x_tok[n] = dve(V.scalar_tensor_tensor, X[:, n, :], bank(b), gate_(n), X[:, n, :], ALU.mult, ALU.add, w=[t, x_tok[n]])
        bfree[b] = x_tok[n]
        sumsq(X[:, n, :], [x_tok[n]])

    for n in range(DK):
        gated(n, n % 4, fm(wslice(A["attn_w_out_2"][0], 0, DK, n * P, P), DK, O, 0, n % 4), gate)

    def ffn_second(l):
        gain, shift, gate = mods(l, 1)
        t_r = finish_rstd(4)
        write_h(t_r, gain, shift)
        ffn_up(A["ffn_w_gate_2"][l], A["ffn_w_up_2"][l])
        for n in range(DK):
            t = ffn_down(A["ffn_w_down_2"][l], n, n % 4)
            gated(n, n % 4, t, gate)

    ffn_second(0)

    gain, shift, gate = mods(1, 0)
    t_r = finish_rstd(4)
    write_h(t_r, gain, shift)
    CV = Split(mem["CVH"], mem["CVL"])
    wc = A["conv_w_in_2"][0]
    before = q.now()
    zr = Ring([TS[:, 0, :], TS[:, 1, :]])
    yr = Ring([TS[:, 2, :], TS[:, 3, :]])
    for n in range(DK):
        bs = [0, 1, 2] if n % 2 == 0 else [3, 4, 5]
        tt = [fm(wslice(wc, 0, DK, j * D + n * P, P), DK, H, 0, bs[i]) for i, j in enumerate((1, 2, 0))]
        i, z, fr = zr.take()
        t = act(S.activation, z, bank(bs[0]), ACT.Copy, w=[tt[0], fr] + before)
        bfree[bs[0]] = t
        t = dve(V.tensor_tensor, z, z, bank(bs[1]), ALU.mult, w=[t, tt[1]])
        bfree[bs[1]] = t
        j, y, fr = yr.take()
        w3 = [vec("conv_w_2", m * 8 + n) for m in range(3)]
        t = dve(V.tensor_scalar, y, z, w3[2], None, ALU.mult, w=[t, fr] + before)
        for d in (1, 2):
            t = dve(V.scalar_tensor_tensor, y[:, d:T], z[:, 0:T - d], w3[2 - d], y[:, d:T], ALU.mult, ALU.add, w=[t])
        zr.free[i] = t
        t = dve(V.tensor_tensor, y, y, bank(bs[2]), ALU.mult, w=[t, tt[2]])
        bfree[bs[2]] = t
        yr.free[j] = split_to(CV, n, y, [t])
    for i in range(4):
        nt.free[i] = yr.free[1]
    for n in range(DK):
        gated(n, n % 4, fm(wslice(A["conv_w_out_2"][0], 0, DK, n * P, P), DK, CV, 0, n % 4), gate)
    ffn_second(1)

    OUT = mem["OUT"]
    before = q.now()
    for tb in range(4):
        for half in range(2):
            b = (2 * tb + half) % 4
            for j in range(4):
                k = half * 4 + j
                t = tr(PS[:, b, j * P:(j + 1) * P], X[:, k, tb * P:(tb + 1) * P], ident, w=[x_tok[k], bfree[b]], done=j == 3)
            t = dve(V.tensor_copy, OUT[:, tb, half * 512:(half + 1) * 512], bank(b), w=[t] + before)
            bfree[b] = t
        t_out = load(out[0, tb * P:(tb + 1) * P, :], OUT[:, tb, :], "out", w=[t])
    q.ops["sp"].append(("wait", q.sems["out"], t_out[1]))
    return chunks


def build(nc, A, out, cst, cs_tab):
    with ExitStack() as ctx:
        base = 16512
        top = [base]

        def at(name, shape, dt, off):
            return nc.alloc_sbuf_tensor_at(name, shape, dt, offset=off)

        def new(name, shape, dt=F32):
            n = 4
            for s in shape[1:]:
                n *= s
            off = top[0]
            top[0] += (n + 31) // 32 * 32
            return at(name, shape, dt, off)

        mem = {}
        mem["X"] = new("X", [P, DK, T])
        ho = top[0]
        mem["HH"] = new("HH", [P, DK, T], F32R)
        mem["HL"] = new("HL", [P, DK, T], F32R)
        mem["F16"] = at("F16", [P, DK, T], F32, ho)
        uo = top[0]
        mem["UH"] = new("UH", [P, FK, T], F32R)
        mem["UL"] = new("UL", [P, FK, T], F32R)

        def over(name, shape, dt, off):
            mem[name] = at(name, shape, dt, uo + off)

        over("XR", [P, 4, D], F32, 0)
        over("VS", [P, 3, P], F32, 16384)
        over("ATH", [P, 4, T], F32R, 0)
        over("ATL", [P, 4, T], F32R, 8192)
        over("MLH", [P, 8, T], F32R, 16384)
        over("MLL", [P, 8, T], F32R, 32768)
        over("SETS", [P, 2, 9, T], F32, 49152)
        over("CS1", [P, 2 * T], F32, 86016)
        over("MGH", [P, 8, T], F32R, 49152)
        over("MGL", [P, 8, T], F32R, 65536)
        over("QT", [P, 8, T], F32, 0)
        over("KD", [P, 4, T], F32, 16384)
        over("VV", [P, 4, 256], F32, 24576)
        over("QI", [P, 4, T], F32, 28672)
        over("KI", [P, T], F32, 36864)
        over("MASK", [P, 4, T], F32, 38912)
        over("WI", [P, 32], F32, 47104)
        over("SCW", [P, 2, T], F32, 47232)
        over("OH", [P, 8, T], F32R, 51328)
        over("OL", [P, 8, T], F32R, 67712)
        over("KT", [P, 2, T], F32, 51328)
        over("CS2", [P, 2, T], F32, 84096)
        over("POSI", [P, T], I32, 0)
        over("CVH", [P, 8, T], F32R, 0)
        over("CVL", [P, 8, T], F32R, 16384)
        over("OUT", [P, 4, D], F32, 0)
        mem["RAW"] = new("RAW", [P, NRAW, DK, P])
        mem["WH"] = new("WH", [P, NSPL, DK, P], F32R)
        mem["WL"] = new("WL", [P, NSPL, DK, P], F32R)
        mem["C"] = new("C", [P, C_N])
        mem["TS"] = new("TS", [P, 9, T])
        mem["VT"] = new("VT", [P, 304])
        mem["MOD"] = new("MOD", [P, 128])
        mem["HG"] = new("HG", [P, 16])
        mem["CA"] = new("CA", [P, 8])
        mem["SM"] = new("SM", [P, 64])
        mem["M8"] = new("M8", [P, 8])
        mem["AVT"] = new("AVT", [P, 16])
        mem["IB"] = new("IB", [4, 1])
        mem["FB"] = new("FB", [4, 1])
        mem["PS"] = ctx.enter_context(nc.psum_tensor("PS", [P, 8, 512], F32))

        names = ["pe", "act", "dve", "pool", "c", "x", "vs", "cs", "pos", "out"] + [f"raw{i}" for i in range(NRAW)]
        sems = {n: ctx.enter_context(nc.semaphore(f"s_{n}")) for n in names}
        plan = program(nc, Queues(sems), mem, A, out, cst, cs_tab, None)
        q = Queues(sems)
        program(nc, q, mem, A, out, cst, cs_tab, plan)
        block = ctx.enter_context(nc.Block())

        @block.sync
        def _(e):
            q.run("sp", e)

        @block.gpsimd
        def _(e):
            q.run("pool", e)

        @block.scalar
        def _(e):
            q.run("act", e)

        @block.vector
        def _(e):
            q.run("dve", e)

        @block.tensor
        def _(e):
            q.run("pe", e)


_INS = ['x', 'ffn1_pre_g', 'ffn1_w_gate', 'ffn1_w_up', 'ffn1_w_down', 'ffn1_post_g', 'mix_pre_g', 'w_in', 'conv_w',
        'conv_b', 'mlstm_i_bias', 'mlstm_f_bias', 'mlstm_head_g', 'w_att_branch', 'w_mlstm_branch', 'w_out',
        'mix_post_g', 'ffn2_pre_g', 'ffn2_w_gate', 'ffn2_w_up', 'ffn2_w_down', 'ffn2_post_g', 'c_2', 'positions_2',
        'ada_w_2', 'ada_b_2', 'norm1_g_2', 'norm2_g_2', 'attn_w_in_2', 'attn_q_norm_g_2', 'attn_k_norm_g_2',
        'idx_k_ln_g_2', 'idx_k_ln_b_2', 'attn_w_out_2', 'conv_w_in_2', 'conv_w_2', 'conv_w_out_2', 'ffn_w_gate_2',
        'ffn_w_up_2', 'ffn_w_down_2']


def kernel(**inputs):
    import concourse.bacc as _bacc
    from concourse.bass_utils import run_bass_kernel_spmd as _run

    nc = _bacc.Bacc("TRN2", target_bir_lowering=False, num_devices=1)
    arrays, args = {}, {}
    for name in _INS:
        a = np.ascontiguousarray(inputs[name])
        arrays[f"in_{name}"] = a
        args[name] = nc.dram_tensor(f"in_{name}", a.shape, mybir.dt.from_np(a.dtype), kind="ExternalInput").ap()
    cst, cs_tab = constants()
    extra = []
    for name, a in (("const_tab", cst), ("const_rot", cs_tab)):
        arrays[name] = a
        extra.append(nc.dram_tensor(name, a.shape, F32, kind="ExternalInput").ap())
    out = nc.dram_tensor("out_x", (1, T, D), F32, kind="ExternalOutput").ap()
    build(nc, args, out, *extra)
    r = _run(nc, [arrays], core_ids=[0])
    return r.results[0]["out_x"]
```

```python
from contextlib import ExitStack

import numpy as np

import concourse.bass as bass
from concourse import mybir

F32 = mybir.dt.float32
F32R = mybir.dt.float32r
I32 = mybir.dt.int32
ALU = mybir.AluOpType
ACT = mybir.ActivationFunctionType
AX = mybir.AxisListType

P = 128
T = 512
D = 1024
DK = D // P
FF = 2816
FK = FF // P
EPS = 1e-6
NEG = -3.0e38
MASKED = -1.0e30

NRAW = 4
NSPL = 3

INV_2PI = 0.15915494309189535
PI_A = 6.28125
PI_B = 1.9350051879882812e-03
PI_C = 3.0199157663446332e-07
PI = 3.141592653589793
ROUND = 12582912.0
SIN_MAX = 3.1415925

C_ID, C_ONE, C_LOW, C_TRI, C_B64, C_R1, C_R2, C_SEL, C_INVF, C_EPS = (
    0, 128, 256, 384, 512, 640, 672, 800, 1312, 1313)
C_N = 1314


def constants():
    c = np.zeros((P, C_N), np.float32)
    fm = np.zeros((P, 3 * T), np.float32)
    i = np.arange(P)
    c[:, C_ID:C_ID + P] = np.eye(P)
    c[:, C_ONE:C_ONE + P] = 1.0
    t, s = 384 + i[:, None], np.arange(T)[None, :]
    d = t - s
    for g, ok in enumerate(((d >= 0) & (d <= 128), (d >= 0) & (d % 4 == 0), (d >= 0) & (d % 16 == 0))):
        fm[:, g * T:(g + 1) * T] = np.where(ok, 0.0, MASKED)
    c[:, C_LOW:C_LOW + P] = i[:, None] <= i[None, :]
    c[:, C_TRI:C_TRI + P] = np.where(i[None, :] <= i[:, None], 0.0, NEG)
    c[:, C_B64:C_B64 + P] = i[:, None] // 64 == i[None, :] // 64
    for m in range(16):
        c[m + 16, C_R1 + m] = -1.0
        c[m, C_R1 + m + 16] = 1.0
    for b in (0, 64):
        for m in range(32):
            c[b + m + 32, C_R2 + b + m] = -1.0
            c[b + m, C_R2 + b + m + 32] = 1.0
    for h in range(4):
        c[h, C_SEL + h * P:C_SEL + (h + 1) * P] = 1.0
    f2 = np.float32(10000.0) ** (-(np.arange(32, dtype=np.float32) * np.float32(2.0) / np.float32(64.0)))
    c[:, C_INVF] = f2[i % 32]
    c[:, C_EPS] = EPS
    f1 = np.float32(500000.0) ** (-(np.arange(16, dtype=np.float32) * np.float32(2.0) / np.float32(32.0)))
    ang = (np.arange(T, dtype=np.float32)[None, :] * f1[np.arange(32) % 16][:, None]).astype(np.float32)
    cs = np.concatenate([np.cos(ang), np.sin(ang)], axis=1).astype(np.float32)
    return c, cs, fm


class Ring:

    def __init__(self, aps):
        self.aps, self.free, self.n = list(aps), [None] * len(aps), 0

    def take(self):
        i = self.n % len(self.aps)
        self.n += 1
        return i, self.aps[i], self.free[i]


class Queues:

    def __init__(self, sems):
        self.sems = sems
        self.ops = {e: [] for e in ("pe", "act", "dve", "pool", "sp")}
        self.count = {s: 0 for s in sems}
        self.seen = {e: {} for e in self.ops}

    def put(self, eng, fn, a, k, w, sem, step):
        q, seen = self.ops[eng], self.seen[eng]
        for t in w:
            if t is not None and seen.get(t[0], 0) < t[1]:
                seen[t[0]] = t[1]
                q.append(("wait", self.sems[t[0]], t[1]))
        if sem is None:
            q.append(("op", fn, a, k, None, 0))
            return None
        self.count[sem] += step
        q.append(("op", fn, a, k, self.sems[sem], step))
        return (sem, self.count[sem])

    def now(self):
        return [(s, self.count[s]) for s in ("pe", "act", "dve", "pool")]

    def run(self, eng, e):
        for op in self.ops[eng]:
            if op[0] == "wait":
                e.wait_ge(op[1], op[2])
            else:
                ins = op[1](*op[2], **op[3])
                if op[4] is not None:
                    ins.then_inc(op[4], op[5])


class Split:

    def __init__(self, hi, lo):
        self.hi, self.lo, self.tok = hi, lo, {}


def program(nc, q, mem, A, out, cst, cs_tab, fm_tab, plan):
    chunks = []
    V, S, G, PE, SP = nc.vector, nc.scalar, nc.gpsimd, nc.tensor, nc.sync

    def dve(fn, *a, w=(), **k):
        return q.put("dve", fn, a, k, w, "dve", 1)

    def act(fn, *a, w=(), **k):
        return q.put("act", fn, a, k, w, "act", 1)

    def pool(fn, *a, w=(), **k):
        return q.put("pool", fn, a, k, w, "pool", 1)

    def mm(o, l, r, start, stop, w=(), done=False):
        return q.put("pe", PE.matmul, (o, l, r), dict(start=start, stop=stop), w, "pe" if done else None, 1)

    def tr(o, i, ident, w=(), done=False):
        return q.put("pe", PE.transpose, (o, i, ident), {}, w, "pe" if done else None, 1)

    def load(o, i, sem, w=(), eng="sp"):
        fn = SP.dma_start if eng == "sp" else G.dma_start
        return q.put(eng, fn, (o, i), {}, w, sem, 16)

    C = mem["C"]
    ident, ones = C[:, C_ID:C_ID + P], C[:, C_ONE:C_ONE + P]
    eps = C[:, C_EPS:C_EPS + 1]
    X, HH, HL, F16 = mem["X"], mem["HH"], mem["HL"], mem["F16"]
    TS = mem["TS"]
    PS = mem["PS"]
    VT, MOD, SM = mem["VT"], mem["MOD"], mem["SM"]
    bfree = [None] * 8

    def bank(b):
        return PS[:, b, :]

    st = dict(use=0, dma=0, spl=0)
    raw_tok, spl_tok, pe_done = {}, {}, {}
    RAW, WH, WL = mem["RAW"], mem["WH"], mem["WL"]

    def issue_dma(j):
        pieces, nk = plan[j]
        r = j % NRAW
        for c0, ap in pieces:
            n = ap.shape[1]
            tok = load(RAW[:, r, 0:nk, c0:c0 + n], ap.rearrange("(k p) n -> p k n", p=P), f"raw{r}",
                       w=[spl_tok.get(j - NRAW)])
        raw_tok[j] = tok

    def issue_split(j):
        pieces, nk = plan[j]
        r, s = j % NRAW, j % NSPL
        wd = max(c0 + ap.shape[1] for c0, ap in pieces)
        prev = pe_done.get(j - NSPL)
        t = act(S.activation, WH[:, s, 0:nk, 0:wd], RAW[:, r, 0:nk, 0:wd], ACT.Copy, w=[raw_tok[j], prev])
        spl_tok[j] = dve(V.tensor_tensor, WL[:, s, 0:nk, 0:wd], RAW[:, r, 0:nk, 0:wd],
                         WH[:, s, 0:nk, 0:wd].bitcast(F32), ALU.subtract, w=[t, raw_tok[j], prev])

    def advance(i):
        while True:
            j = st["dma"]
            if j < len(plan) and j <= i + NRAW and (j < NRAW or j - NRAW in spl_tok):
                issue_dma(j)
                st["dma"] += 1
                continue
            j = st["spl"]
            if j < st["dma"] and j < i + NSPL and (j < NSPL or j - NSPL in pe_done):
                issue_split(j)
                st["spl"] += 1
                continue
            break

    def use(pieces, nk):
        i = st["use"]
        st["use"] += 1
        chunks.append((pieces, nk))
        if plan is None:
            return i, WH[:, 0], WL[:, 0], None
        advance(i)
        s = i % NSPL
        return i, WH[:, s], WL[:, s], spl_tok[i]

    def wslice(w, r0, nk, c0, n):
        return [(0, w[r0:r0 + nk * P, c0:c0 + n])]

    background = []

    def pump():
        for g in list(background):
            try:
                next(g)
            except StopIteration:
                background.remove(g)

    def drain():
        while background:
            pump()

    busy = [False] * 8

    def grab(pool_):
        while True:
            for b in pool_:
                if not busy[b]:
                    busy[b] = True
                    pool_.remove(b)
                    pool_.append(b)
                    return b
            yield

    def release(b, t):
        bfree[b] = t
        busy[b] = False

    def fm(pieces, nk, x, kt0, b, first=True, last=True, n=P):
        i, wh, wl, wt = use(pieces, nk)
        o = PS[0:n, b, :]
        for k in range(nk):
            kk = kt0 + k
            w = [wt, x.tok.get(kk)] + ([bfree[b]] if first and k == 0 else [])
            end = last and k == nk - 1
            mm(o, wh[:, k, 0:n], x.hi[:, kk, :], first and k == 0, False, w=w)
            mm(o, wh[:, k, 0:n], x.lo[:, kk, :], False, False)
            t = mm(o, wl[:, k, 0:n], x.hi[:, kk, :], False, end, done=k == nk - 1)
            if k == nk - 1:
                pe_done[i] = t
            if k % 2:
                pump()
        ada_step()
        return t

    def tm(pieces, x, b, n, c0=0):
        i, wh, wl, wt = use(pieces, DK)
        for tb in range(4):
            o = PS[:, b, tb * n:(tb + 1) * n]
            ts = slice(tb * P, (tb + 1) * P)
            for k in range(DK):
                w = [wt, x.tok[k]] + ([bfree[b]] if tb == 0 and k == 0 else [])
                mm(o, x.hi[:, k, ts], wh[:, k, c0:c0 + n], k == 0, False, w=w)
                mm(o, x.lo[:, k, ts], wh[:, k, c0:c0 + n], False, False)
                t = mm(o, x.hi[:, k, ts], wl[:, k, c0:c0 + n], False, k == DK - 1, done=tb == 3 and k == DK - 1)
        pe_done[i] = t
        return t

    XR, VS = mem["XR"], mem["VS"]
    for tb in range(4):
        t_x = load(XR[:, tb, :], A["x"][0, tb * P:(tb + 1) * P, :], "x")
        if tb == 0:
            t_c = load(C[:, :], cst, "c")

    def rows(ap):
        if len(ap.shape) == 2:
            return ap.rearrange("a (r c) -> (a r) c", c=P)
        return ap.rearrange("a j (r c) -> (a j r) c", c=P)

    stage = [
        [("ffn1_pre_g", 8), ("ffn1_post_g", 8), ("mix_pre_g", 8), ("mix_post_g", 8), ("ffn2_pre_g", 8),
         ("ffn2_post_g", 8), ("mlstm_head_g", 8), ("conv_b", 16), ("attn_q_norm_g_2", 1), ("attn_k_norm_g_2", 1),
         ("idx_k_ln_g_2", 1), ("idx_k_ln_b_2", 1), ("c_2", 8)],
        [("conv_w", 64), ("norm1_g_2", 16), ("norm2_g_2", 16), ("conv_w_2", 24)],
        [("ada_b_2", 96)],
    ]
    col, n_all, sizes = {}, 0, []
    for g, names in enumerate(stage):
        r = 0
        for name, n in names:
            col[name] = n_all + r
            if n == 1:
                for half in (0, 64):
                    t_vs = load(VS[r:r + 1, g, half:half + 64], A[name], "vs", eng="pool")
            else:
                t_vs = load(VS[r:r + n, g, :], rows(A[name]), "vs", eng="pool")
            r += n
        sizes.append((n_all, r))
        n_all += r
    IB, FB = mem["IB"], mem["FB"]
    t_vs = load(IB[:, :], A["mlstm_i_bias"].rearrange("a h -> h a"), "vs", eng="pool")
    t_vs = load(FB[:, :], A["mlstm_f_bias"].rearrange("a h -> h a"), "vs", eng="pool")

    def vec(name, k=0):
        c = col[name] + k
        return VT[:, c:c + 1]

    if plan is not None:
        advance(-1)

    CA, ADA, ASUM = mem["CA"], mem["ADA"], mem["ASUM"]
    ada = dict(n=0, sum=None, read=None, ca=None, mod=None)
    ada_in, ada_done = {}, {}

    def ada_load(m):
        if m < 192:
            c, k = (m // 8) % 12, m % 8
            ada_in[m] = load(ADA[:, m % 2, :], A["ada_w_2"][m // 96][k * P:(k + 1) * P, c * 512:(c + 1) * 512],
                             f"ada{m % 2}", w=[ada_done.get(m - 2)])

    def ada_step():
        m = ada["n"]
        if m > 192:
            return
        if m and m % 8 == 0:
            if busy[6]:
                return
            for j in range(4):
                t = mm(PS[:, 6, j:j + 1], ASUM[:, j * P:(j + 1) * P], ones[:, 0:1], True, True,
                       w=[ada["sum"], bfree[6]], done=j == 3)
            ada["read"] = t
            a = m // 2 - 4
            c = col["ada_b_2"] + a
            ada["mod"] = bfree[6] = dve(V.tensor_tensor, MOD[:, a:a + 4], PS[:, 6, 0:4], VT[:, c:c + 4], ALU.add, w=[t])
        if m < 192:
            k = m % 8
            w = [ada_in[m], ada["ca"], ada["read"], ada["sum"]]
            if k == 0:
                t = pool(G.tensor_scalar, ASUM[:, :], ADA[:, m % 2, :], CA[:, 0:1], None, ALU.mult, w=w)
            else:
                src = ADA[:, m % 2, :]
                t = pool(G.tensor_scalar, src, src, CA[:, k:k + 1], None, ALU.mult, w=w)
                t = pool(G.tensor_tensor, ASUM[:, :], ASUM[:, :], src, ALU.add, w=[t])
            ada["sum"] = ada_done[m] = t
            ada_load(m + 2)
        ada["n"] += 1

    for m in range(2):
        ada_load(m)

    sq = Ring([TS[:, 4, :], TS[:, 5, :]])
    nt = Ring([TS[:, i, :] for i in range(4)])
    acc, diag, RC = TS[:, 6, :], TS[:, 7, :], mem["RC"]
    ss = dict(tok=None, n=0, free=None)
    x_tok = [None] * DK
    RB, CB = 4, 5

    def sumsq(src, w):
        if ss["n"] == 0:
            t0 = act(S.activation, acc, src, ACT.Square, w=list(w) + [ss["free"]])
            ss["tok"] = t0
        else:
            i, ap, fr = sq.take()
            t0 = act(S.activation, ap, src, ACT.Square, w=list(w) + [fr])
            ss["tok"] = sq.free[i] = dve(V.tensor_tensor, acc, acc, ap, ALU.add, w=[t0, ss["tok"]])
        ss["n"] += 1
        return t0

    def column_sums(src, first, last, w):
        for tb in range(4):
            t = q.put("pe", PE.matmul, (PS[:, CB, tb:tb + 1], src[:, tb * P:(tb + 1) * P], ones[:, 0:1]),
                      dict(start=first and tb == 0, stop=last, skip_group_check=True),
                      list(w) + ([bfree[CB]] if first else []), "pe" if tb == 3 else None, 1)
        return t

    def finish_rstd():
        if ss["n"]:
            t = column_sums(acc, True, True, [ss["tok"], t_c])
            ss["free"], ss["n"] = t, 0
        else:
            t = ss["sums"]
        t = act(S.activation, RC[:, 0:4], PS[:, CB, 0:4], ACT.Sqrt, bias=eps, scale=1.0 / D, w=[t])
        bfree[CB] = t
        t = dve(V.reciprocal, RC[:, 0:4], RC[:, 0:4], w=[t])
        w = [t] + q.now()
        for tb in range(4):
            t = dve(V.tensor_scalar, diag[:, tb * P:(tb + 1) * P], ident, RC[:, tb:tb + 1], None, ALU.mult, w=w)
        t = mm(bank(RB), ones, diag, True, True, w=[t, bfree[RB]], done=True)
        return t

    H = Split(HH, HL)

    def write_h(t_r, gain, shift=None, t_g=None):
        for k in range(DK):
            i, ap, fr = nt.take()
            t = dve(V.scalar_tensor_tensor, ap, X[:, k, :], gain(k), bank(RB), ALU.mult, ALU.mult, w=[t_r, t_g, x_tok[k], fr])
            bfree[RB] = t
            if shift is None:
                t2 = act(S.activation, HH[:, k, :], ap, ACT.Copy, w=[t])
                lo = pool if k % 3 == 1 else dve
                t3 = lo((G if k % 3 == 1 else V).tensor_tensor, HL[:, k, :], ap, HH[:, k, :].bitcast(F32), ALU.subtract, w=[t2, t])
            else:
                t2 = act(S.activation, HH[:, k, :], ap, ACT.Identity, bias=shift(k), w=[t])
                t3 = dve(V.scalar_tensor_tensor, HL[:, k, :], ap, shift(k), HH[:, k, :].bitcast(F32),
                         ALU.add, ALU.subtract, w=[t2, t])
            nt.free[i] = t3
            H.tok[k] = t3

    def split_to(x, k, src, w, cols=slice(0, T)):
        hi, lo = x.hi[:, k, cols], x.lo[:, k, cols]
        t = act(S.activation, hi, src, ACT.Copy, w=w)
        t = dve(V.tensor_tensor, lo, src, hi.bitcast(F32), ALU.subtract, w=[t] + list(w))
        x.tok[k] = t
        return t

    for k in range(DK):
        b = k % 4
        for tb in range(4):
            t = tr(PS[:, b, tb * P:(tb + 1) * P], XR[:, tb, k * P:(k + 1) * P], ident,
                   w=[t_x, t_c, bfree[b]], done=tb == 3)
        x_tok[k] = dve(V.tensor_copy, X[:, k, :], bank(b), w=[t])
        bfree[b] = sumsq(bank(b), [t, x_tok[k]])

    for g, (c0, n) in enumerate(sizes):
        t = tr(PS[:, 7, c0:c0 + n], VS[0:n, g, :], C[0:n, C_ID:C_ID + n], w=[t_vs, t_c], done=True)
    t_v = dve(V.tensor_copy, VT[:, 0:n_all], PS[:, 7, 0:n_all], w=[t])
    bfree[7] = t_v
    HG = mem["HG"]
    for j, name in enumerate(("ffn1_post_g", "ffn2_post_g")):
        t_hg = dve(V.tensor_scalar, HG[:, 8 * j:8 * j + 8], VT[:, col[name]:col[name] + 8], 0.5, None, ALU.mult, w=[t_v])
    ada["ca"] = act(S.activation, CA[:, :], VT[:, col["c_2"]:col["c_2"] + 8], ACT.Silu, w=[t_v])

    U = Split(mem["UH"], mem["UL"])
    silu_r = Ring([TS[:, 0, :], TS[:, 1, :]])
    prod_r = Ring([TS[:, 2, :], TS[:, 3, :]])

    def ffn_up(wg, wu):
        for i in range(2):
            silu_r.free[i], prod_r.free[i] = nt.free[i], nt.free[2 + i]
        for n in range(FK):
            bg, bu = (2 * n) % 4, (2 * n) % 4 + 1
            tg = fm(wslice(wg, 0, DK, n * P, P), DK, H, 0, bg)
            tu = fm(wslice(wu, 0, DK, n * P, P), DK, H, 0, bu)
            i, s_ap, fr = silu_r.take()
            ts_ = act(S.activation, s_ap, bank(bg), ACT.Silu, w=[tg, fr])
            bfree[bg] = ts_
            j, p_ap, fr = prod_r.take()
            tp = dve(V.tensor_tensor, p_ap, s_ap, bank(bu), ALU.mult, w=[ts_, tu, fr])
            silu_r.free[i] = bfree[bu] = tp
            prod_r.free[j] = split_to(U, n, p_ap, [tp])
        for i in range(2):
            nt.free[i], nt.free[2 + i] = silu_r.free[i], prod_r.free[i]

    def ffn_down(wd, n, b):
        for c, nk in ((0, 8), (8, 8), (16, 6)):
            t = fm(wslice(wd, c * P, nk, n * P, P), nk, U, c, b, first=c == 0, last=c == 16)
        return t

    def keep_f(n, b, t, gain):
        t0 = act(S.activation, F16[:, n, :], bank(b), ACT.Copy, scale=gain(n), w=[t, t_hg])
        bfree[b] = sumsq(bank(b), [t, t0])

    def residual(t_r):
        for k in range(DK):
            i, ap, fr = nt.take()
            t = dve(V.tensor_tensor, ap, F16[:, k, :], bank(RB), ALU.mult, w=[t_r, fr])
            bfree[RB] = t
            e, fn = (pool, G.tensor_tensor) if k % 2 else (dve, V.tensor_tensor)
            x_tok[k] = e(fn, X[:, k, :], X[:, k, :], ap, ALU.add, w=[t])
            nt.free[i] = x_tok[k]
            i, ap, fr = sq.take()
            t = act(S.activation, ap, X[:, k, :], ACT.Square, w=[x_tok[k], fr])
            ss["sums"] = sq.free[i] = column_sums(ap, k == 0, k == DK - 1, [t])

    def ffn_first(t_r, pre, wg, wu, wd, post):
        write_h(t_r, lambda k: vec(pre, k))
        ffn_up(wg, wu)
        for n in range(DK):
            keep_f(n, n % 4, ffn_down(wd, n, n % 4), lambda k: HG[:, post + k:post + k + 1])
        residual(finish_rstd())

    ffn_first(finish_rstd(), "ffn1_pre_g", A["ffn1_w_gate"][0], A["ffn1_w_up"][0], A["ffn1_w_down"][0], 0)

    t_r = finish_rstd()
    CS1, FMT = mem["CS1"], mem["FMT"]
    before = q.now()
    t_cs = load(CS1[0:32, :], cs_tab, "cs", w=before, eng="pool")
    t_fm = load(FMT[:, :], fm_tab, "fm", w=before, eng="pool")
    write_h(t_r, lambda k: vec("mix_pre_g", k))
    w_in = A["w_in"][0]
    SETS = mem["SETS"]
    set_free = [[], []]
    AT, ML, MG = Split(mem["ATH"], mem["ATL"]), Split(mem["MLH"], mem["MLL"]), Split(mem["MGH"], mem["MGL"])

    lb = Ring([0, 1])

    def lbank():
        return lb.take()[1]

    XB = [5, 6]
    gk = {}

    def gates():
        ig, xf, nz, lf, cb = (TS[0:4, i, :] for i in range(5))
        t_ig = dve(V.tensor_scalar, ig, PS[0:4, gk["bi"], :], IB[:, 0:1], None, ALU.add, w=[gk["ti"], t_vs] + before)
        bfree[gk["bi"]] = t_ig
        t = dve(V.tensor_scalar, xf, PS[0:4, gk["bf"], :], FB[:, 0:1], None, ALU.add, w=[gk["tf"], t_vs])
        bfree[gk["bf"]] = t
        t1 = act(S.activation, nz, xf, ACT.Abs, w=[t])
        t1 = act(S.activation, nz, nz, ACT.Exp, scale=-1.0, w=[t1])
        t1 = act(S.activation, nz, nz, ACT.Ln, bias=C[0:4, C_ONE:C_ONE + 1], w=[t1])
        t = dve(V.scalar_tensor_tensor, lf, xf, 0.0, nz, ALU.min, ALU.subtract, w=[t1, t])
        t = dve(V.memset, xf, 1.0, w=[t])
        t = dve(V.tensor_tensor_scan, cb, xf, lf, 0.0, ALU.mult, ALU.add, w=[t])
        t_av = dve(V.tensor_tensor, ig, ig, cb, ALU.subtract, w=[t, t_ig])
        gk["mx"] = dve(V.tensor_tensor_scan, MX, ig, ig, 0.0, ALU.max, ALU.max, w=[t_av])
        t = dve(V.tensor_tensor, EM, cb, MX, ALU.add, w=[gk["mx"]])
        gk["em"] = act(S.activation, EM, EM, ACT.Exp, scale=-1.0, w=[t])
        for _ in range(8):
            yield
        b = yield from grab(XB)
        for sb in range(4):
            t = tr(PS[:, b, sb * 4:sb * 4 + 4], ig[:, sb * P:(sb + 1) * P], C[0:4, C_ID:C_ID + 4],
                   w=[t_av, bfree[b]], done=sb == 3)
        t = dve(V.tensor_copy, AVT[:, :], PS[:, b, 0:16], w=[t])
        release(b, t)
        gk["avt"] = t

    MX, EM = TS[0:4, 7, :], TS[0:4, 8, :]
    AVT = mem["AVT"]
    gk["bi"] = lbank()
    gk["ti"] = fm(wslice(w_in, 0, DK, 8704, P), DK, H, 0, gk["bi"])
    gk["bf"] = lbank()
    gk["tf"] = fm(wslice(w_in, 0, DK, 8708, P), DK, H, 0, gk["bf"])
    background.append(gates())
    pump()
    nt.free[0:4] = [None] * 4

    rope_t = Ring([TS[:, 5, :], TS[:, 6, :]])

    def rope_first(dst, t, tok, key):
        x = yield from grab(XB)
        t2 = mm(PS[0:32, x, :], C[0:32, C_R1:C_R1 + 32], dst[0:32, :], True, True, w=[t, bfree[x]], done=True)
        i, ap, fr = rope_t.take()
        t3 = dve(V.tensor_tensor, ap[0:32, :], PS[0:32, x, :], CS1[0:32, T:2 * T], ALU.mult, w=[t2, fr, t_cs] + before)
        release(x, t3)
        t4 = dve(V.tensor_tensor, dst[0:32, :], dst[0:32, :], CS1[0:32, 0:T], ALU.mult, w=[t, t2])
        t4 = dve(V.tensor_tensor, dst[0:32, :], dst[0:32, :], ap[0:32, :], ALU.add, w=[t4, t3])
        rope_t.free[i] = t4
        tok[key] = [t, t4]

    def to_tokens(dst, t, tok, key):
        b = yield from grab(XB)
        for tb in range(4):
            t2 = tr(PS[:, b, tb * P:(tb + 1) * P], dst[:, tb * P:(tb + 1) * P], ident, w=[t, bfree[b]], done=tb == 3)
        t2 = act(S.activation, dst, bank(b), ACT.Copy, w=[t2])
        release(b, t2)
        tok[key] = [t2]

    def att_project(hd, s, tok):
        free = set_free[s]
        for g in range(3):
            for which, base in ((0, 0), (1, 1536), (2, 3072)):
                key = 2 * g + which if which < 2 else 6 + g
                dst = SETS[:, s, key, :]
                b = lbank()
                t = fm(wslice(w_in, 0, DK, base + (4 * g + hd) * P, P), DK, H, 0, b)
                t = act(S.activation, dst, bank(b), ACT.Copy, w=[t] + free)
                bfree[b] = t
                background.append((rope_first if which < 2 else to_tokens)(dst, t, tok, key))

    sm_n = [0]

    def small():
        c = sm_n[0] % 32
        sm_n[0] += 1
        return SM[:, 2 * c:2 * c + 1]

    pt_r = Ring([TS[:, 3, :], TS[:, 4, :]])
    att = dict(s_free=[bfree[2], bfree[3], bfree[4]], p_free=None)
    SCALE = float(P) ** -0.5

    def attention(hd, s, tok):
        while len(tok) < 9:
            yield
        start = q.now() if hd == 0 else []
        for tb in range(4):
            W = (tb + 1) * P
            ts = slice(tb * P, (tb + 1) * P)
            for g in range(3):
                t = mm(PS[:, 2 + g, 0:W], SETS[:, s, 2 * g, ts], SETS[:, s, 2 * g + 1, 0:W], True, True,
                       w=tok[2 * g] + tok[2 * g + 1] + att["s_free"], done=g == 2)
            pr = TS[:, 0:3, 0:W]
            t = dve(V.scalar_tensor_tensor, pr, PS[:, 2:5, 0:W], SCALE,
                    FMT[:, :].rearrange("p (g t) -> p g t", g=3)[:, :, T - W:T],
                    ALU.mult, ALU.add, w=[t, att["p_free"], t_fm] + start)
            att["s_free"] = [t]
            mx, l = small(), small()
            t = dve(V.tensor_reduce, mx, pr, AX.XY, ALU.max, negate=True, w=[t])
            t = act(S.activation, pr, pr, ACT.Exp, bias=mx, accum_out=l, w=[t])
            t = dve(V.reciprocal, l, l, w=[t])
            t_p = dve(V.tensor_scalar, pr, pr, l, None, ALU.mult, w=[t])
            for _ in range(2 + tb):
                yield
            blocks = [(g, sb) for g in range(3) for sb in range(tb + 1) if g > 0 or sb >= tb - 1]
            done = 0
            while done < len(blocks):
                part = blocks[done:done + 4]
                b = yield from grab(XB)
                for j, (g, sb) in enumerate(part):
                    t = tr(PS[:, b, j * P:(j + 1) * P], TS[:, g, sb * P:(sb + 1) * P], ident,
                           w=[t_p, bfree[b]], done=j == len(part) - 1)
                att["p_free"] = t
                i, ap, fr = pt_r.take()
                n = len(part) * P
                t = act(S.activation, ap[:, 0:n], PS[:, b, 0:n], ACT.Copy, w=[t, fr] + start)
                release(b, t)
                yield
                for j, (g, sb) in enumerate(part):
                    m = done + j
                    t2 = mm(PS[:, 7, 0:P], SETS[:, s, 6 + g, sb * P:(sb + 1) * P], ap[:, j * P:(j + 1) * P],
                            m == 0, m == len(blocks) - 1, w=[t, bfree[7]] + tok[6 + g], done=j == len(part) - 1)
                pt_r.free[i] = t2
                done += len(part)
            bfree[7] = split_to(AT, hd, PS[:, 7, 0:P], [t2], cols=ts)
        set_free[s] = [t2] + att["s_free"]

    def ml_project(hd, s, tok):
        free = set_free[s]
        for which in range(2):
            for c in range(2):
                cc = which * 8 + hd * 2 + c
                dst = SETS[:, s, 2 * which + c, :]
                b = lbank()
                t = fm(wslice(w_in, 0, DK, 4608 + cc * P, P), DK, H, 0, b)
                wv = [vec("conv_w", j * 16 + cc) for j in range(4)]
                t2 = dve(V.tensor_scalar, dst, bank(b), wv[3], vec("conv_b", cc), ALU.mult, ALU.add, w=[t] + free)
                for d in range(1, 4):
                    t2 = dve(V.scalar_tensor_tensor, dst[:, d:T], PS[:, b, 0:T - d], wv[3 - d], dst[:, d:T],
                             ALU.mult, ALU.add, w=[t2])
                bfree[b] = t2
                tok[2 * which + c] = [act(S.activation, dst, dst, ACT.Silu, w=[t2])]
        for c in range(2):
            b = lbank()
            dst = SETS[:, s, 4 + c, :]
            t = fm(wslice(w_in, 0, DK, 6656 + hd * 256 + c * P, P), DK, H, 0, b)
            t = act(S.activation, dst, bank(b), ACT.Copy, w=[t] + free)
            bfree[b] = t
            background.append(to_tokens(dst, t, tok, 4 + c))
        for c in range(2):
            b = lbank()
            t = fm(wslice(w_in, 0, DK, 7680 + hd * 256 + c * P, P), DK, H, 0, b)
            t = act(S.activation, SETS[:, s, 6 + c, :], bank(b), ACT.Sigmoid, w=[t] + free)
            bfree[b] = t
            tok[6 + c] = [t]

    sfree = [None] * 2

    def mlstm(hd, s, tok):
        while len(tok) < 8 or "avt" not in gk:
            yield
        start = q.now()
        sel = C[0:4, C_SEL + hd * P:C_SEL + (hd + 1) * P]
        b = yield from grab(XB)
        t = mm(bank(b), sel, MX, True, True, w=[gk["mx"], bfree[b]], done=True)
        gt = []
        for sb in range(4):
            c = sb * 4 + hd
            t2 = dve(V.tensor_scalar, TS[:, sb, sb * P:T], PS[:, b, sb * P:T], AVT[:, c:c + 1], 0.0,
                     ALU.subtract, ALU.max, w=[t, gk["avt"]] + start)
            gt.append(t2)
        release(b, t2)
        gt = [act(S.activation, TS[:, sb, sb * P:T], TS[:, sb, sb * P:T], ACT.Exp, scale=-1.0, w=[gt[sb]]) for sb in range(4)]
        yield
        wt = []
        for sb in range(4):
            z = sb % 2
            ns = slice(sb * P, T)
            for c in range(2):
                t = mm(PS[:, 2 + z, ns], SETS[:, s, 2 + c, sb * P:(sb + 1) * P], SETS[:, s, c, ns], c == 0, c == 1,
                       w=tok[c] + tok[2 + c] + [sfree[z]] + att["s_free"], done=c == 1)
            t = dve(V.scalar_tensor_tensor, TS[:, sb, ns], PS[:, 2 + z, ns], 1.0 / 16.0, TS[:, sb, ns],
                    ALU.mult, ALU.mult, w=[t, gt[sb]])
            sfree[z] = t
            dg = TS[:, sb, sb * P:(sb + 1) * P]
            wt.append(dve(V.tensor_tensor, dg, dg, C[:, C_LOW:C_LOW + P], ALU.mult, w=[t]))
            yield
        yield
        bd = yield from grab(XB)
        for sb in range(4):
            ns = slice(sb * P, T)
            td = mm(PS[:, bd, ns], ones, TS[:, sb, ns], sb == 0, sb == 3, w=[wt[sb], bfree[bd]], done=sb == 3)
        dn = TS[:, 4, :]
        t = act(S.activation, dn, bank(bd), ACT.Abs, w=[td] + start)
        release(bd, t)
        be = yield from grab(XB)
        te = mm(bank(be), sel, EM, True, True, w=[gk["em"], bfree[be]], done=True)
        t = dve(V.tensor_tensor, dn, dn, bank(be), ALU.max, w=[t, te])
        release(be, t)
        t = dve(V.reciprocal, dn, dn, w=[t])
        nb, tn = [7, 4], []
        for c in range(2):
            for sb in range(4):
                ns = slice(sb * P, T)
                t1 = mm(PS[:, nb[c], ns], SETS[:, s, 4 + c, sb * P:(sb + 1) * P], TS[:, sb, ns], sb == 0, sb == 3,
                        w=tok[4 + c] + [bfree[nb[c]]] + att["s_free"], done=sb == 3)
            tn.append(t1)
            yield
        hm, sqt = [TS[:, 5, :], TS[:, 6, :]], [TS[:, 0, :], TS[:, 1, :]]
        th, tq = [], []
        for c in range(2):
            t2 = dve(V.tensor_tensor, hm[c], dn, bank(nb[c]), ALU.mult, w=[t, tn[c]] + start)
            bfree[nb[c]] = t2
            th.append(t2)
            tq.append(act(S.activation, sqt[c], hm[c], ACT.Square, w=[t2, tn[1]]))
        t = dve(V.tensor_tensor, sqt[0], sqt[0], sqt[1], ALU.add, w=tq)
        for _ in range(3):
            yield
        b = yield from grab(XB)
        t = mm(bank(b), ones, sqt[0], True, True, w=[t, bfree[b]], done=True)
        t = act(S.activation, dn, bank(b), ACT.Sqrt, bias=eps, scale=1.0 / 256.0, w=[t, th[1]])
        release(b, t)
        t = dve(V.reciprocal, dn, dn, w=[t])
        for c in range(2):
            t2 = dve(V.scalar_tensor_tensor, hm[c], hm[c], vec("mlstm_head_g", 2 * hd + c), dn, ALU.mult, ALU.mult, w=[t] + tq)
            t2 = dve(V.tensor_tensor, hm[c], hm[c], SETS[:, s, 6 + c, :], ALU.mult, w=[t2] + tok[6 + c])
            t2 = split_to(ML, 2 * hd + c, hm[c], [t2])
        set_free[s] = [t2, tn[1]]

    tok = None
    for n in range(8):
        todo, tok = tok, {}
        if todo is not None:
            background.append((attention if n <= 4 else mlstm)((n - 1) % 4, (n - 1) % 2, todo))
        (att_project if n < 4 else ml_project)(n % 4, n % 2, tok)
        drain()

    background.append(mlstm(3, 1, tok))
    wa, wm = A["w_att_branch"][0], A["w_mlstm_branch"][0]
    T1 = mem["T1"]
    before = q.now()
    gate_r = Ring([SETS[:, 0, 8, :], CS1[:, 0:T], CS1[:, T:2 * T]])
    t1_tok = []

    def gated_branch(n, gc, w, x, nk, b):
        t = fm(wslice(w_in, 0, DK, gc + n * P, P), DK, H, 0, b)
        i, ap, fr = gate_r.take()
        t = act(S.activation, ap, bank(b), ACT.Sigmoid, w=[t, fr] + before)
        bfree[b] = t
        b2 = lbank()
        t2 = fm(wslice(w, 0, nk, n * P, P), nk, x, 0, b2)
        return i, ap, t, b2, t2

    for n in range(DK):
        i, ap, t, b2, t2 = gated_branch(n, 8712, wa, AT, 4, lbank())
        t = dve(V.tensor_tensor, T1[:, n, :], ap, bank(b2), ALU.mult, w=[t, t2] + set_free[0] + before)
        gate_r.free[i] = bfree[b2] = t
        t1_tok.append(t)
    drain()
    before = q.now()
    gate_r = Ring([TS[:, i, :] for i in range(4)])
    for n in range(DK):
        i, ap, t, b2, t2 = gated_branch(n, 9736, wm, ML, 8, lbank())
        t = dve(V.tensor_tensor, ap, ap, bank(b2), ALU.mult, w=[t, t2])
        bfree[b2] = t
        t = dve(V.tensor_tensor, ap, ap, T1[:, n, :], ALU.add, w=[t, t1_tok[n]])
        gate_r.free[i] = split_to(MG, n, ap, [t] + before)
    w_out = A["w_out"][0]
    for n in range(DK):
        keep_f(n, n % 4, fm(wslice(w_out, 0, DK, n * P, P), DK, MG, 0, n % 4), lambda k: vec("mix_post_g", k))
    nt.free[0:4] = gate_r.free
    residual(finish_rstd())
    ffn_first(finish_rstd(), "ffn2_pre_g", A["ffn2_w_gate"][0], A["ffn2_w_up"][0], A["ffn2_w_down"][0], 8)

    def mods(l, j, t):
        o = 96 + 16 * l + 8 * j
        sh, gt = 48 * l + 24 * j, 48 * l + 24 * j + 16
        g0 = col[("norm1_g_2", "norm2_g_2")[j]] + 8 * l
        t = dve(V.scalar_tensor_tensor, MOD[:, o:o + 8], MOD[:, sh + 8:sh + 16], 1.0, VT[:, g0:g0 + 8],
                ALU.add, ALU.mult, w=[t])
        return (t, lambda k: MOD[:, o + k:o + k + 1], lambda k: MOD[:, sh + k:sh + k + 1],
                lambda k: MOD[:, gt + k:gt + k + 1])

    t_r = finish_rstd()
    while ada["n"] <= 192:
        ada_step()
    t_mod = ada["mod"]
    t_g, gain, shift, gate = mods(0, 0, t_mod)
    write_h(t_r, gain, shift, t_g)

    CS2, POSI = mem["CS2"], mem["POSI"]
    before = q.now()
    t_pos = load(POSI[:, :], A["positions_2"][0:1, :].to_broadcast([P, T]), "pos", w=before, eng="pool")
    pf, ang, kr, tmp = (TS[:, i, :] for i in range(4))
    cosT, sinT = CS2[:, 0, :], CS2[:, 1, :]
    t = dve(V.tensor_copy, pf, POSI[:, :], w=[t_pos] + before)
    t_pf = t
    t = dve(V.tensor_scalar, ang, pf, C[:, C_INVF:C_INVF + 1], None, ALU.mult, w=[t])
    t = dve(V.tensor_scalar, kr, ang, INV_2PI, ROUND, ALU.mult, ALU.add, w=[t])
    t = dve(V.tensor_scalar, kr, kr, ROUND, None, ALU.subtract, w=[t])
    for p in (PI_A, PI_B, PI_C):
        t = dve(V.scalar_tensor_tensor, ang, kr, -p, ang, ALU.mult, ALU.add, w=[t])
    t1 = dve(V.tensor_scalar, sinT, ang, SIN_MAX, -SIN_MAX, ALU.min, ALU.max, w=[t])
    t2 = dve(V.tensor_scalar, ang, ang, PI / 2, None, ALU.add, w=[t1])
    t2 = dve(V.tensor_scalar, tmp, ang, PI, -2.0 * PI, ALU.is_gt, ALU.mult, w=[t2])
    t2 = dve(V.tensor_tensor, ang, ang, tmp, ALU.add, w=[t2])
    t2 = dve(V.tensor_scalar, cosT, ang, SIN_MAX, -SIN_MAX, ALU.min, ALU.max, w=[t2])
    t1 = act(S.activation, sinT, sinT, ACT.Sin, w=[t1, t2])
    t_cs2 = act(S.activation, cosT, cosT, ACT.Sin, w=[t2])
    nt.free[0:4] = [t2] * 4

    QT, KD, VV, QI, KI = mem["QT"], mem["KD"], mem["VV"], mem["QI"], mem["KI"]
    MASK, WI, SCW = mem["MASK"], mem["WI"], mem["SCW"]
    O = Split(mem["OH"], mem["OL"])
    w_att = A["attn_w_in_2"][0]
    B64 = C[:, C_B64:C_B64 + P]
    before = q.now()
    xr = Ring([TS[:, 0, :], TS[:, 1, :]])
    s2r = Ring([TS[:, 2, :], TS[:, 7, :]])
    rr = Ring([TS[:, 3, :], TS[:, 4, :]])
    t_ki, t_qi, t_q, t_k, t_vv = {}, {}, {}, {}, {}

    def rope(x_ap, i, t_x_, dst, toks, key):
        b = yield from grab(XB)
        t = mm(bank(b), C[:, C_R2:C_R2 + P], x_ap, True, True, w=[t_x_, bfree[b]], done=True)
        j, ap, fr = rr.take()
        t2 = dve(V.tensor_tensor, ap, bank(b), sinT, ALU.mult, w=[t, fr, t_cs2])
        release(b, t2)
        t3 = dve(V.tensor_tensor, dst, x_ap, cosT, ALU.mult, w=[t, t_x_, t_cs2] + before)
        t3 = dve(V.tensor_tensor, dst, dst, ap, ALU.add, w=[t3, t2])
        rr.free[j] = xr.free[i] = t3
        xr_busy[i] = False
        toks[key] = t3

    xr_busy = [False, False]

    def take_x():
        while xr_busy[xr.n % 2]:
            pump()
        i, x, fr = xr.take()
        xr_busy[i] = True
        return i, x, fr

    def project(c0, scale=1.0):
        b = lbank()
        t = fm(c0 if isinstance(c0, list) else wslice(w_att, 0, DK, c0, P), DK, H, 0, b)
        i, x, fr = take_x()
        t2 = act(S.activation, x, bank(b), ACT.Copy, scale=scale, w=[t, fr] + before)
        bfree[b] = t2
        return i, x, b, t, t2

    def index_key(i, x, t):
        xbk = yield from grab(XB)
        t2 = mm(bank(xbk), B64, x, True, True, w=[t, bfree[xbk]], done=True)
        t = dve(V.scalar_tensor_tensor, x, bank(xbk), -1.0 / 64.0, x, ALU.mult, ALU.add, w=[t2, t])
        release(xbk, t)
        j, s2, fr = s2r.take()
        t2 = act(S.activation, s2, x, ACT.Square, w=[t, fr] + before)
        yield
        xbk = yield from grab(XB)
        t2 = mm(bank(xbk), B64, s2, True, True, w=[t2, bfree[xbk]], done=True)
        t2 = act(S.activation, s2, bank(xbk), ACT.Sqrt, bias=eps, scale=1.0 / 64.0, w=[t2])
        release(xbk, t2)
        t2 = dve(V.reciprocal, s2, s2, w=[t2])
        t = dve(V.tensor_tensor, x, x, s2, ALU.mult, w=[t, t2])
        s2r.free[j] = t
        t = dve(V.tensor_scalar, x, x, vec("idx_k_ln_g_2"), vec("idx_k_ln_b_2"), ALU.mult, ALU.add, w=[t])
        for _ in range(5):
            yield
        yield from rope(x, i, t, KI[:, :], t_ki, 0)

    i, x, b, _, t = project([(0, w_att[:, 2048:2112]), (64, w_att[:, 2048:2112])])
    background.append(index_key(i, x, t))
    b = lbank()
    t = tm(wslice(w_att, 0, DK, 2112, 8), H, b, 8)
    t_wi = dve(V.tensor_scalar, WI[:, :], PS[:, b, 0:32], float(8 ** -0.5 * 64 ** -0.5), None, ALU.mult, w=[t] + before)
    bfree[b] = t_wi
    for c in range(4):
        i, x, b, _, t = project(1536 + c * P)
        background.append(rope(x, i, t, QI[:, c, :], t_qi, c))

    t_mask = [None] * 4
    tri = C[:, C_TRI:C_TRI + P]
    rel = Ring([TS[:, 5, :], TS[:, 6, :]])
    sring = Ring([2, 3, 4])
    M8 = mem["M8"]
    GT, EQ = TS[:, 8, :], SCW[:, 2, :]

    def indexer():
        while len(t_qi) < 4 or len(t_ki) < 1:
            yield
        t_mask[0] = dve(V.tensor_scalar, MASK[:, 0, 0:P], tri, MASKED, None, ALU.max, w=before)
        for tb in range(1, 4):
            W = (tb + 1) * P
            ts = slice(tb * P, (tb + 1) * P)
            sc, wk = SCW[:, 0, 0:W], SCW[:, 1, 0:W]
            for h in range(8):
                b = sring.take()[1]
                r = slice(64 * (h % 2), 64 * (h % 2) + 64)
                t = mm(PS[:, b, 0:W], QI[r, h // 2, ts], KI[r, 0:W], True, True, w=[t_qi[h // 2], t_ki[0], bfree[b]], done=True)
                wi = WI[:, tb * 8 + h:tb * 8 + h + 1]
                if h == 0:
                    ta = dve(V.tensor_scalar, sc, PS[:, b, 0:W], 0.0, wi, ALU.max, ALU.mult, w=[t, t_wi] + before)
                    bfree[b] = ta
                else:
                    j, ap, fr = rel.take()
                    t = act(S.activation, ap[:, 0:W], PS[:, b, 0:W], ACT.Relu, w=[t, fr] + before)
                    bfree[b] = t
                    ta = dve(V.scalar_tensor_tensor, sc, ap[:, 0:W], wi, sc, ALU.mult, ALU.add, w=[t, ta])
                    rel.free[j] = ta
                yield
            ta = dve(V.tensor_tensor, sc[:, W - P:W], sc[:, W - P:W], tri, ALU.add, w=[ta])
            src = sc
            for n in range(16):
                ta = dve(V.max, M8[:, :], src, w=[ta])
                if n < 15:
                    ta = dve(V.match_replace, wk, M8[:, :], src, -3.4e38, w=[ta])
                    src = wk
                if n % 2:
                    yield
            cnt, need = small(), small()
            thr = M8[:, 7:8]
            gt, eq, pf_ = GT[:, 0:W], EQ[:, 0:W], wk
            ta = dve(V.tensor_scalar, gt, sc, thr, None, ALU.is_gt, ALU.add, accum_out=cnt, w=[ta] + before)
            tn_ = dve(V.tensor_scalar, need, cnt, -1.0, 128.0, ALU.mult, ALU.add, w=[ta])
            te_ = dve(V.tensor_scalar, eq, sc, thr, None, ALU.is_equal, w=[ta])
            te_ = dve(V.tensor_tensor_scan, pf_, eq, eq, 0.0, ALU.add, ALU.bypass, w=[te_])
            te_ = dve(V.scalar_tensor_tensor, eq, pf_, need, eq, ALU.is_le, ALU.mult, w=[te_, tn_])
            te_ = dve(V.tensor_tensor, gt, gt, eq, ALU.add, w=[te_])
            t_mask[tb] = dve(V.tensor_scalar, MASK[:, tb, 0:W], gt, -1.0, -MASKED, ALU.add, ALU.mult, w=[te_])
            yield

    background.append(indexer())

    def q_tile(c, i, x, t, j, s2, t2):
        for tb in range(4):
            o = tb * 16 + 2 * c
            t2 = mm(PS[:, 7, o:o + 2], s2[:, tb * P:(tb + 1) * P], B64[:, 0:P:64], True, True, w=[t2, bfree[7]], done=tb == 3)
        s2r.free[j] = t_rq[0] = t2
        yield from rope(x, i, t, QT[:, c, :], t_q, c)

    def k_tile(c, i, x, t, j, s2, t2):
        xbk = yield from grab(XB)
        t2 = mm(bank(xbk), B64, s2, True, True, w=[t2, bfree[xbk]], done=True)
        t2 = act(S.activation, s2, bank(xbk), ACT.Sqrt, bias=eps, scale=1.0 / 64.0, w=[t2])
        release(xbk, t2)
        t2 = dve(V.reciprocal, s2, s2, w=[t2])
        t = dve(V.tensor_tensor, x, x, s2, ALU.mult, w=[t, t2])
        s2r.free[j] = t
        for _ in range(5):
            yield
        kt, tk = mem["KT"][:, c, :], {}
        yield from rope(x, i, t, kt, tk, 0)
        for j in range(2):
            src = kt[64 * j:64 * j + 64, :]
            act(S.activation, KD[0:64, 2 * c + j, :], src, ACT.Copy, w=[tk[0]])
            t_k[2 * c + j] = act(S.activation, KD[64:128, 2 * c + j, :], src, ACT.Copy, w=[tk[0]])

    def v_tile(c, x, i, t):
        b = yield from grab(XB)
        for tb in range(4):
            t2 = tr(PS[:, b, tb * P:(tb + 1) * P], x[:, tb * P:(tb + 1) * P], ident, w=[t, bfree[b]], done=tb == 3)
        t2 = act(S.activation, VV[:, :, c * P:(c + 1) * P], bank(b).rearrange("p (t n) -> p t n", t=4), ACT.Copy, w=[t2] + before)
        release(b, t2)
        xr.free[i] = t2
        xr_busy[i] = False
        t_vv[c] = t2

    t_rq = [None]
    for c in range(2):
        i, x, b, t, t2 = project(1280 + c * P)
        background.append(v_tile(c, x, i, t2))
    for fn, n, c0, gname in ((k_tile, 2, 1024, "attn_k_norm_g_2"), (q_tile, 8, 0, "attn_q_norm_g_2")):
        for c in range(n):
            i, x, b, t, t2 = project(c0 + c * P, vec(gname))
            j, s2, fr = s2r.take()
            t3 = act(S.activation, s2, bank(b), ACT.Square, w=[t, t2, fr] + before)
            bfree[b] = t3
            background.append(fn(c, i, x, t2, j, s2, t3))
    drain()
    RQ = mem["RQ"]
    t = act(S.activation, RQ[:, :], PS[:, 7, 0:64], ACT.Sqrt, bias=eps, scale=1.0 / 64.0, w=[t_rq[0]])
    bfree[7] = t
    t = dve(V.reciprocal, RQ[:, :], RQ[:, :], w=[t])
    t_rqs = dve(V.tensor_scalar, RQ[:, :], RQ[:, :], 0.125, None, ALU.mult, w=[t])

    pr_r = Ring([TS[:, i, :] for i in range(4, 9)])
    PT = TS[:, 0:4, :].rearrange("p s (a b t) -> p s a b t", a=2, b=2)
    before = q.now()

    def probs(tb, g, i4):
        h = 4 * g + i4
        W = (tb + 1) * P
        r = slice(64 * (h % 2), 64 * (h % 2) + 64)
        b = sring.take()[1]
        t = mm(PS[:, b, 0:W], QT[r, h // 2, tb * P:(tb + 1) * P], KD[r, g, 0:W], True, True,
               w=[t_q[h // 2], t_k[g], bfree[b]], done=True)
        j, ap, fr = pr_r.take()
        pr = ap[:, 0:W]
        c = tb * 16 + h
        t = dve(V.scalar_tensor_tensor, pr, PS[:, b, 0:W], RQ[:, c:c + 1], MASK[:, tb, 0:W], ALU.mult, ALU.add,
                w=[t, fr, t_mask[tb], t_rqs] + before)
        bfree[b] = t
        mx, l = small(), small()
        t = dve(V.tensor_reduce, mx, pr, AX.X, ALU.max, negate=True, w=[t])
        t = act(S.activation, pr, pr, ACT.Exp, bias=mx, accum_out=l, w=[t])
        t = dve(V.reciprocal, l, l, w=[t])
        t = dve(V.tensor_scalar, pr, pr, l, None, ALU.mult, w=[t])
        return j, ap, t

    def turned(tb, g, i4, j, ap, t, pt_free):
        b = xb2.take()[1]
        for sb in range(tb + 1):
            t2 = tr(PS[:, b, sb * P:(sb + 1) * P], ap[:, sb * P:(sb + 1) * P], ident, w=[t, bfree[b]], done=sb == tb)
        pr_r.free[j] = t2
        t2 = act(S.activation, PT[:, 0:tb + 1, i4 % 2, i4 // 2, :],
                 PS[:, b, 0:(tb + 1) * P].rearrange("p (s t) -> p s t", t=P), ACT.Copy, w=[t2, pt_free])
        bfree[b] = t2
        return t2

    def values(tb, g, t):
        for par in range(2):
            for sb in range(tb + 1):
                t2 = mm(PS[64 * par:64 * par + 64, 7, 0:256], VV[:, sb, g * 64:(g + 1) * 64],
                        PT[:, sb, par, :, :].rearrange("p b t -> p (b t)"), sb == 0, sb == tb,
                        w=[t, t_vv[g // 2], bfree[7]], done=par == 1 and sb == tb)
        t = t2
        for i2 in range(2):
            t = split_to(O, 2 * g + i2, PS[:, 7, i2 * P:(i2 + 1) * P], [t2, t], cols=slice(tb * P, (tb + 1) * P))
        bfree[7] = t
        return t2

    xb2 = Ring([5, 6])
    items = [(tb, g, i4) for tb in range(4) for g in range(4) for i4 in range(4)]
    ready, pt_free, pending = {}, before[0], None
    AHEAD = 3
    for n in range(len(items) + AHEAD + 1):
        m = n - AHEAD
        if pending is not None:
            pt_free = values(*pending)
            pending = None
        if 0 <= m < len(items):
            t = turned(*items[m], *ready.pop(m), pt_free)
            if items[m][2] == 3:
                pending = (items[m][0], items[m][1], t)
        if n < len(items):
            ready[n] = probs(*items[n])

    def gated(n, b, t, gate_):
        x_tok[n] = dve(V.scalar_tensor_tensor, X[:, n, :], bank(b), gate_(n), X[:, n, :], ALU.mult, ALU.add, w=[t, x_tok[n]])
        bfree[b] = x_tok[n]
        sumsq(X[:, n, :], [x_tok[n]])

    nt.free[0:4] = [pt_free] * 4
    for n in range(DK):
        gated(n, n % 4, fm(wslice(A["attn_w_out_2"][0], 0, DK, n * P, P), DK, O, 0, n % 4), gate)

    def ffn_second(l):
        t_g, gain, shift, gate = mods(l, 1, t_mod)
        write_h(finish_rstd(), gain, shift, t_g)
        ffn_up(A["ffn_w_gate_2"][l], A["ffn_w_up_2"][l])
        for n in range(DK):
            t = ffn_down(A["ffn_w_down_2"][l], n, n % 4)
            gated(n, n % 4, t, gate)

    ffn_second(0)

    t_g, gain, shift, gate = mods(1, 0, t_mod)
    write_h(finish_rstd(), gain, shift, t_g)
    CV = Split(mem["CVH"], mem["CVL"])
    wc = A["conv_w_in_2"][0]
    before = q.now()
    zr = Ring([TS[:, 0, :], TS[:, 1, :]])
    yr = Ring([TS[:, 2, :], TS[:, 3, :]])
    for n in range(DK):
        bs = [0, 1, 2] if n % 2 == 0 else [3, 6, 7]
        tt = [fm(wslice(wc, 0, DK, j * D + n * P, P), DK, H, 0, bs[i]) for i, j in enumerate((1, 2, 0))]
        i, z, fr = zr.take()
        t = act(S.activation, z, bank(bs[0]), ACT.Copy, w=[tt[0], fr] + before)
        bfree[bs[0]] = t
        t = dve(V.tensor_tensor, z, z, bank(bs[1]), ALU.mult, w=[t, tt[1]])
        bfree[bs[1]] = t
        j, y, fr = yr.take()
        w3 = [vec("conv_w_2", m * 8 + n) for m in range(3)]
        t = dve(V.tensor_scalar, y, z, w3[2], None, ALU.mult, w=[t, fr] + before)
        for d in (1, 2):
            t = dve(V.scalar_tensor_tensor, y[:, d:T], z[:, 0:T - d], w3[2 - d], y[:, d:T], ALU.mult, ALU.add, w=[t])
        zr.free[i] = t
        t = dve(V.tensor_tensor, y, y, bank(bs[2]), ALU.mult, w=[t, tt[2]])
        bfree[bs[2]] = t
        yr.free[j] = split_to(CV, n, y, [t])
    nt.free[0:4] = [yr.free[(DK - 1) % 2]] * 4
    for n in range(DK):
        gated(n, n % 4, fm(wslice(A["conv_w_out_2"][0], 0, DK, n * P, P), DK, CV, 0, n % 4), gate)
    ffn_second(1)

    OUT = mem["OUT"]
    before = q.now()
    for tb in range(4):
        for half in range(2):
            b = (2 * tb + half) % 4
            for j in range(4):
                k = half * 4 + j
                t = tr(PS[:, b, j * P:(j + 1) * P], X[:, k, tb * P:(tb + 1) * P], ident, w=[x_tok[k], bfree[b]], done=j == 3)
            t = dve(V.tensor_copy, OUT[:, tb, half * 512:(half + 1) * 512], bank(b), w=[t] + before)
            bfree[b] = t
        t_out = load(out[0, tb * P:(tb + 1) * P, :], OUT[:, tb, :], "out", w=[t])
    q.ops["sp"].append(("wait", q.sems["out"], t_out[1]))
    return chunks


def build(nc, A, out, cst, cs_tab, fm_tab):
    with ExitStack() as ctx:
        base = 16512
        top = [base]

        def at(name, shape, dt, off):
            return nc.alloc_sbuf_tensor_at(name, shape, dt, offset=off)

        def new(name, shape, dt=F32):
            n = 4
            for s in shape[1:]:
                n *= s
            off = top[0]
            top[0] += (n + 31) // 32 * 32
            return at(name, shape, dt, off)

        mem = {}
        mem["X"] = new("X", [P, DK, T])
        ho = top[0]
        mem["HH"] = new("HH", [P, DK, T], F32R)
        mem["HL"] = new("HL", [P, DK, T], F32R)
        mem["F16"] = at("F16", [P, DK, T], F32, ho)
        uo = top[0]
        mem["UH"] = new("UH", [P, FK, T], F32R)
        mem["UL"] = new("UL", [P, FK, T], F32R)

        def over(name, shape, dt, off):
            mem[name] = at(name, shape, dt, uo + off)

        over("XR", [P, 4, D], F32, 0)
        over("VS", [P, 3, P], F32, 16384)
        over("ATH", [P, 4, T], F32R, 0)
        over("ATL", [P, 4, T], F32R, 8192)
        over("MLH", [P, 8, T], F32R, 16384)
        over("MLL", [P, 8, T], F32R, 32768)
        over("SETS", [P, 2, 9, T], F32, 49152)
        over("FMT", [P, 3 * T], F32, 16384)
        over("T1", [P, 8, T], F32, 49152)
        over("CS1", [P, 2 * T], F32, 86016)
        over("MGH", [P, 8, T], F32R, 49152)
        over("MGL", [P, 8, T], F32R, 65536)
        over("QT", [P, 8, T], F32, 0)
        over("KD", [P, 4, T], F32, 16384)
        over("VV", [P, 4, 256], F32, 24576)
        over("QI", [P, 4, T], F32, 28672)
        over("KI", [P, T], F32, 36864)
        over("MASK", [P, 4, T], F32, 38912)
        over("WI", [P, 32], F32, 47104)
        over("RQ", [P, 64], F32, 47232)
        over("OH", [P, 8, T], F32R, 51328)
        over("OL", [P, 8, T], F32R, 67712)
        over("KT", [P, 2, T], F32, 51328)
        over("SCW", [P, 3, T], F32, 55424)
        over("CS2", [P, 2, T], F32, 84096)
        over("POSI", [P, T], I32, 0)
        over("CVH", [P, 8, T], F32R, 0)
        over("CVL", [P, 8, T], F32R, 16384)
        over("OUT", [P, 4, D], F32, 0)
        mem["RAW"] = new("RAW", [P, NRAW, DK, P])
        mem["WH"] = new("WH", [P, NSPL, DK, P], F32R)
        mem["WL"] = new("WL", [P, NSPL, DK, P], F32R)
        mem["C"] = new("C", [P, C_N])
        mem["TS"] = new("TS", [P, 9, T])
        mem["ADA"] = new("ADA", [P, 2, 512])
        mem["ASUM"] = new("ASUM", [P, 512])
        mem["RC"] = new("RC", [P, 8])
        mem["VT"] = new("VT", [P, 304])
        mem["MOD"] = new("MOD", [P, 128])
        mem["HG"] = new("HG", [P, 16])
        mem["CA"] = new("CA", [P, 8])
        mem["SM"] = new("SM", [P, 64])
        mem["M8"] = new("M8", [P, 8])
        mem["AVT"] = new("AVT", [P, 16])
        mem["IB"] = new("IB", [4, 1])
        mem["FB"] = new("FB", [4, 1])
        mem["PS"] = ctx.enter_context(nc.psum_tensor("PS", [P, 8, 512], F32))

        names = ["pe", "act", "dve", "pool", "c", "x", "vs", "cs", "fm", "pos", "out", "ada0", "ada1"] + [f"raw{i}" for i in range(NRAW)]
        sems = {n: ctx.enter_context(nc.semaphore(f"s_{n}")) for n in names}
        plan = program(nc, Queues(sems), mem, A, out, cst, cs_tab, fm_tab, None)
        q = Queues(sems)
        program(nc, q, mem, A, out, cst, cs_tab, fm_tab, plan)
        block = ctx.enter_context(nc.Block())

        @block.sync
        def _(e):
            q.run("sp", e)

        @block.gpsimd
        def _(e):
            q.run("pool", e)

        @block.scalar
        def _(e):
            q.run("act", e)

        @block.vector
        def _(e):
            q.run("dve", e)

        @block.tensor
        def _(e):
            q.run("pe", e)


_INS = ['x', 'ffn1_pre_g', 'ffn1_w_gate', 'ffn1_w_up', 'ffn1_w_down', 'ffn1_post_g', 'mix_pre_g', 'w_in', 'conv_w',
        'conv_b', 'mlstm_i_bias', 'mlstm_f_bias', 'mlstm_head_g', 'w_att_branch', 'w_mlstm_branch', 'w_out',
        'mix_post_g', 'ffn2_pre_g', 'ffn2_w_gate', 'ffn2_w_up', 'ffn2_w_down', 'ffn2_post_g', 'c_2', 'positions_2',
        'ada_w_2', 'ada_b_2', 'norm1_g_2', 'norm2_g_2', 'attn_w_in_2', 'attn_q_norm_g_2', 'attn_k_norm_g_2',
        'idx_k_ln_g_2', 'idx_k_ln_b_2', 'attn_w_out_2', 'conv_w_in_2', 'conv_w_2', 'conv_w_out_2', 'ffn_w_gate_2',
        'ffn_w_up_2', 'ffn_w_down_2']


def kernel(**inputs):
    import concourse.bacc as _bacc
    from concourse.bass_utils import run_bass_kernel_spmd as _run

    nc = _bacc.Bacc("TRN2", target_bir_lowering=False, num_devices=1)
    arrays, args = {}, {}
    for name in _INS:
        a = np.ascontiguousarray(inputs[name])
        arrays[f"in_{name}"] = a
        args[name] = nc.dram_tensor(f"in_{name}", a.shape, mybir.dt.from_np(a.dtype), kind="ExternalInput").ap()
    cst, cs_tab, fm_tab = constants()
    extra = []
    for name, a in (("const_tab", cst), ("const_rot", cs_tab), ("const_band", fm_tab)):
        arrays[name] = a
        extra.append(nc.dram_tensor(name, a.shape, F32, kind="ExternalInput").ap())
    out = nc.dram_tensor("out_x", (1, T, D), F32, kind="ExternalOutput").ap()
    build(nc, args, out, *extra)
    r = _run(nc, [arrays], core_ids=[0])
    return r.results[0]["out_x"]
```

```python
from contextlib import ExitStack

import numpy as np

import concourse.bass as bass
from concourse import mybir

F32 = mybir.dt.float32
F32R = mybir.dt.float32r
I32 = mybir.dt.int32
ALU = mybir.AluOpType
ACT = mybir.ActivationFunctionType
AX = mybir.AxisListType

P = 128
T = 512
D = 1024
DK = D // P
FF = 2816
FK = FF // P
EPS = 1e-6
NEG = -3.0e38
MASKED = -1.0e30

NRAW = 4
NSPL = 3

INV_2PI = 0.15915494309189535
PI_A = 6.28125
PI_B = 1.9350051879882812e-03
PI_C = 3.0199157663446332e-07
PI = 3.141592653589793
ROUND = 12582912.0
SIN_MAX = 3.1415925

C_ID, C_ONE, C_EPS, C_INVF, C_LOW, C_TRI, C_B64, C_R1, C_R2, C_SEL = (
    0, 128, 256, 257, 260, 388, 516, 644, 676, 804)
C_N = 1316


def constants():
    c = np.zeros((P, C_N), np.float32)
    fm = np.zeros((P, 3 * T), np.float32)
    i = np.arange(P)
    c[:, C_ID:C_ID + P] = np.eye(P)
    c[:, C_ONE:C_ONE + P] = 1.0
    t, s = 384 + i[:, None], np.arange(T)[None, :]
    d = t - s
    for g, ok in enumerate(((d >= 0) & (d <= 128), (d >= 0) & (d % 4 == 0), (d >= 0) & (d % 16 == 0))):
        fm[:, g * T:(g + 1) * T] = np.where(ok, 0.0, MASKED)
    c[:, C_LOW:C_LOW + P] = i[:, None] <= i[None, :]
    c[:, C_TRI:C_TRI + P] = np.where(i[None, :] <= i[:, None], 0.0, NEG)
    c[:, C_B64:C_B64 + P] = i[:, None] // 64 == i[None, :] // 64
    for m in range(16):
        c[m + 16, C_R1 + m] = -1.0
        c[m, C_R1 + m + 16] = 1.0
    for b in (0, 64):
        for m in range(32):
            c[b + m + 32, C_R2 + b + m] = -1.0
            c[b + m, C_R2 + b + m + 32] = 1.0
    for h in range(4):
        c[h, C_SEL + h * P:C_SEL + (h + 1) * P] = 1.0
    f2 = np.float32(10000.0) ** (-(np.arange(32, dtype=np.float32) * np.float32(2.0) / np.float32(64.0)))
    c[:, C_INVF] = f2[i % 32]
    c[:, C_EPS] = EPS
    f1 = np.float32(500000.0) ** (-(np.arange(16, dtype=np.float32) * np.float32(2.0) / np.float32(32.0)))
    ang = (np.arange(T, dtype=np.float32)[None, :] * f1[np.arange(32) % 16][:, None]).astype(np.float32)
    cs = np.concatenate([np.cos(ang), np.sin(ang)], axis=1).astype(np.float32)
    return c, cs, fm


class Ring:

    def __init__(self, aps):
        self.aps, self.free, self.n = list(aps), [None] * len(aps), 0

    def take(self):
        i = self.n % len(self.aps)
        self.n += 1
        return i, self.aps[i], self.free[i]


class Queues:

    def __init__(self, sems):
        self.sems = sems
        self.ops = {e: [] for e in ("pe", "act", "dve", "pool", "sp")}
        self.count = {s: 0 for s in sems}
        self.seen = {e: {} for e in self.ops}

    def put(self, eng, fn, a, k, w, sem, step):
        q, seen = self.ops[eng], self.seen[eng]
        for t in w:
            if t is not None and seen.get(t[0], 0) < t[1]:
                seen[t[0]] = t[1]
                q.append(("wait", self.sems[t[0]], t[1]))
        if sem is None:
            q.append(("op", fn, a, k, None, 0))
            return None
        self.count[sem] += step
        q.append(("op", fn, a, k, self.sems[sem], step))
        return (sem, self.count[sem])

    def now(self):
        return [(s, self.count[s]) for s in ("pe", "act", "dve", "pool")]

    def run(self, eng, e):
        for op in self.ops[eng]:
            if op[0] == "wait":
                e.wait_ge(op[1], op[2])
            else:
                ins = op[1](*op[2], **op[3])
                if op[4] is not None:
                    ins.then_inc(op[4], op[5])


class Split:

    def __init__(self, hi, lo):
        self.hi, self.lo, self.tok, self.hi_tok = hi, lo, {}, {}


def program(nc, q, mem, A, out, cst, cs_tab, fm_tab, plan):
    chunks = []
    V, S, G, PE, SP = nc.vector, nc.scalar, nc.gpsimd, nc.tensor, nc.sync

    def dve(fn, *a, w=(), **k):
        return q.put("dve", fn, a, k, w, "dve", 1)

    def act(fn, *a, w=(), **k):
        return q.put("act", fn, a, k, w, "act", 1)

    def pool(fn, *a, w=(), **k):
        return q.put("pool", fn, a, k, w, "pool", 1)

    def mm(o, l, r, start, stop, w=(), done=False):
        return q.put("pe", PE.matmul, (o, l, r), dict(start=start, stop=stop), w, "pe" if done else None, 1)

    def tr(o, i, ident, w=(), done=False):
        return q.put("pe", PE.transpose, (o, i, ident), {}, w, "pe" if done else None, 1)

    def load(o, i, sem, w=(), eng="sp"):
        fn = SP.dma_start if eng == "sp" else G.dma_start
        return q.put(eng, fn, (o, i), {}, w, sem, 16)

    C = mem["C"]
    ident, ones = C[:, C_ID:C_ID + P], C[:, C_ONE:C_ONE + P]
    eps = C[:, C_EPS:C_EPS + 1]
    X, HH, HL, F16 = mem["X"], mem["HH"], mem["HL"], mem["F16"]
    TS = mem["TS"]
    PS = mem["PS"]
    VT, MOD, SM = mem["VT"], mem["MOD"], mem["SM"]
    bfree = [None] * 8

    def bank(b):
        return PS[:, b, :]

    st = dict(use=0, dma=0, spl=0, hold=False, pool=False)
    raw_tok, spl_tok, pe_done = {}, {}, {}
    RAW, WH, WL = mem["RAW"], mem["WH"], mem["WL"]

    def issue_dma(j):
        pieces, nk = plan[j]
        r = j % NRAW
        for c0, ap in pieces:
            n = ap.shape[1]
            tok = load(RAW[:, r, 0:nk, c0:c0 + n], ap.rearrange("(k p) n -> p k n", p=P), f"raw{r}",
                       w=[spl_tok.get(j - NRAW)])
        raw_tok[j] = tok

    def issue_split(j):
        pieces, nk = plan[j]
        r, s = j % NRAW, j % NSPL
        wd = max(c0 + ap.shape[1] for c0, ap in pieces)
        prev = pe_done.get(j - NSPL)
        t = act(S.activation, WH[:, s, 0:nk, 0:wd], RAW[:, r, 0:nk, 0:wd], ACT.Copy, w=[raw_tok[j], prev])
        e, fn = (pool, G.tensor_tensor) if st["pool"] else (dve, V.tensor_tensor)
        spl_tok[j] = e(fn, WL[:, s, 0:nk, 0:wd], RAW[:, r, 0:nk, 0:wd],
                         WH[:, s, 0:nk, 0:wd].bitcast(F32), ALU.subtract, w=[t, raw_tok[j], prev])

    def advance(i):
        while True:
            j = st["dma"]
            if j < len(plan) and j <= i + NRAW and (j < NRAW or j - NRAW in spl_tok):
                issue_dma(j)
                st["dma"] += 1
                continue
            j = st["spl"]
            if not st["hold"] and j < st["dma"] and j < i + NSPL and (j < NSPL or j - NSPL in pe_done):
                issue_split(j)
                st["spl"] += 1
                continue
            break

    def use(pieces, nk):
        i = st["use"]
        st["use"] += 1
        chunks.append((pieces, nk))
        if plan is None:
            return i, WH[:, 0], WL[:, 0], None
        advance(i)
        s = i % NSPL
        return i, WH[:, s], WL[:, s], spl_tok[i]

    def wslice(w, r0, nk, c0, n):
        return [(0, w[r0:r0 + nk * P, c0:c0 + n])]

    background = []

    def pump():
        for g in list(background):
            try:
                next(g)
            except StopIteration:
                background.remove(g)

    def drain():
        while background:
            pump()

    busy = [False] * 8

    def grab(pool_):
        while True:
            for b in pool_:
                if not busy[b]:
                    busy[b] = True
                    pool_.remove(b)
                    pool_.append(b)
                    return b
            yield

    def release(b, t):
        bfree[b] = t
        busy[b] = False

    def fm(pieces, nk, x, kt0, b, first=True, last=True, n=P):
        i, wh, wl, wt = use(pieces, nk)
        o = PS[0:n, b, :]
        for k in range(nk):
            kk = kt0 + k
            w = [wt, x.tok.get(kk)] + ([bfree[b]] if first and k == 0 else [])
            end = last and k == nk - 1
            mm(o, wh[:, k, 0:n], x.hi[:, kk, :], first and k == 0, False, w=w)
            mm(o, wh[:, k, 0:n], x.lo[:, kk, :], False, False)
            t = mm(o, wl[:, k, 0:n], x.hi[:, kk, :], False, end, done=k == nk - 1)
            if k == nk - 1:
                pe_done[i] = t
            if k % 2:
                pump()
        ada_step()
        return t

    def fm_head(chs, x, each=None, after=None):
        used = [use(pieces, DK) for pieces, _ in chs]
        width = [max(c0 + ap.shape[1] for c0, ap in pieces) for pieces, _ in chs]
        for k in range(DK):
            if each:
                each(k)
            for (_, b), n, (i, wh, wl, wt) in zip(chs, width, used):
                w = [wt, x.hi_tok.get(k)] + ([bfree[b]] if k == 0 else [])
                mm(PS[0:n, b, :], wh[:, k, 0:n], x.hi[:, k, :], k == 0, False, w=w)
                mm(PS[0:n, b, :], wl[:, k, 0:n], x.hi[:, k, :], False, False)
            toks = []
            for (_, b), n, (i, wh, wl, wt) in zip(chs, width, used):
                t = mm(PS[0:n, b, :], wh[:, k, 0:n], x.lo[:, k, :], False, k == DK - 1, w=[x.tok.get(k)], done=k == DK - 1)
                toks.append(t)
                if k == DK - 1:
                    pe_done[i] = t
            if after:
                after(k)
        for _ in chs:
            ada_step()
        if plan is not None:
            advance(st["use"])
        return toks

    XR, VS = mem["XR"], mem["VS"]
    def rows(ap):
        if len(ap.shape) == 2:
            return ap.rearrange("a (r c) -> (a r) c", c=P)
        return ap.rearrange("a j (r c) -> (a j r) c", c=P)

    stage = [
        [("ffn1_pre_g", 8), ("c_2", 8)],
        [("ffn1_post_g", 8), ("mix_pre_g", 8), ("mix_post_g", 8), ("ffn2_pre_g", 8), ("ffn2_post_g", 8),
         ("mlstm_head_g", 8), ("conv_b", 16), ("attn_q_norm_g_2", 1), ("attn_k_norm_g_2", 1),
         ("idx_k_ln_g_2", 1), ("idx_k_ln_b_2", 1)],
        [("conv_w", 64), ("norm1_g_2", 16), ("norm2_g_2", 16), ("conv_w_2", 24)],
        [("ada_b_2", 96)],
    ]
    col, n_all, sizes, t_vs = {}, 0, [], [None] * 4

    def load_stage(g, eng):
        nonlocal n_all
        r = 0
        for name, n in stage[g]:
            col[name] = n_all + r
            if n == 1:
                for half in (0, 64):
                    t_vs[g] = load(VS[r:r + 1, g, half:half + 64], A[name], f"vs{g}", eng=eng)
            else:
                t_vs[g] = load(VS[r:r + n, g, :], rows(A[name]), f"vs{g}", eng=eng)
            r += n
        sizes.append((n_all, r))
        n_all += r

    load_stage(0, "sp")
    t_c = load(C[:, 0:C_LOW], cst[:, 0:C_LOW], "c")
    for tb in range(4):
        t_x = load(XR[:, tb, :], A["x"][0, tb * P:(tb + 1) * P, :], "x")
    for g in range(1, 4):
        load_stage(g, "pool")
    IB, FB = mem["IB"], mem["FB"]
    load(IB[:, :], A["mlstm_i_bias"].rearrange("a h -> h a"), "ib", eng="pool")
    t_ib = load(FB[32:36, :], A["mlstm_f_bias"].rearrange("a h -> h a"), "ib", eng="pool")
    t_c2 = load(C[:, C_LOW:C_N], cst[:, C_LOW:C_N], "c2", eng="pool")

    def vec(name, k=0):
        c = col[name] + k
        return VT[:, c:c + 1]

    if plan is not None:
        for j in range(NRAW):
            issue_dma(j)
        st["dma"], st["hold"] = NRAW, True

    CA, ADA, ASUM = mem["CA"], mem["ADA"], mem["ASUM"]
    ada = dict(n=0, sum=None, read=None, ca=None, mod=None)
    ada_in, ada_done = {}, {}

    def ada_load(m):
        if m < 192:
            c, k = (m // 8) % 12, m % 8
            ada_in[m] = load(ADA[:, m % 2, :], A["ada_w_2"][m // 96][k * P:(k + 1) * P, c * 512:(c + 1) * 512],
                             f"ada{m % 2}", w=[ada_done.get(m - 2)])

    def ada_step():
        m = ada["n"]
        if m > 192:
            return
        if m and m % 8 == 0:
            if busy[6]:
                return
            for j in range(4):
                t = mm(PS[:, 6, j:j + 1], ASUM[:, j * P:(j + 1) * P], ones[:, 0:1], True, True,
                       w=[ada["sum"], bfree[6]], done=j == 3)
            ada["read"] = t
            a = m // 2 - 4
            c = col["ada_b_2"] + a
            ada["mod"] = bfree[6] = dve(V.tensor_tensor, MOD[:, a:a + 4], PS[:, 6, 0:4], VT[:, c:c + 4], ALU.add, w=[t])
        if m < 192:
            k = m % 8
            w = [ada_in[m], ada["ca"], ada["read"], ada["sum"]]
            if k == 0:
                t = pool(G.tensor_scalar, ASUM[:, :], ADA[:, m % 2, :], CA[:, 0:1], None, ALU.mult, w=w)
            else:
                src = ADA[:, m % 2, :]
                t = pool(G.tensor_scalar, src, src, CA[:, k:k + 1], None, ALU.mult, w=w)
                t = pool(G.tensor_tensor, ASUM[:, :], ASUM[:, :], src, ALU.add, w=[t])
            ada["sum"] = ada_done[m] = t
            ada_load(m + 2)
        ada["n"] += 1

    for m in range(2):
        ada_load(m)

    sq = Ring([TS[:, 4, :], TS[:, 5, :]])
    nt = Ring([TS[:, i, :] for i in range(4)])
    acc, diag, RC = TS[:, 6, :], TS[:, 7, :], mem["RC"]
    ss = dict(tok=None, n=0, free=None, pre=None, rc=None)
    x_tok = [None] * DK
    RB, CB = 4, 5

    def sqrt_table():
        ss["pre"] = act(S.activation, RC[:, 4:5], eps, ACT.Sqrt, w=[t_c, ss["pre"]])

    def sumsq(src, w, eng="dve"):
        if ss["n"] == 0:
            t0 = act(S.activation, acc, src, ACT.Square, w=list(w) + [ss["free"]])
            ss["tok"] = t0
            sqrt_table()
        else:
            i, ap, fr = sq.take()
            t0 = act(S.activation, ap, src, ACT.Square, w=list(w) + [fr])
            if ss["n"] == DK - 1:
                ss["last"] = i, ap, t0
            else:
                e, fn = (pool, G.tensor_tensor) if eng == "pool" else (dve, V.tensor_tensor)
                ss["tok"] = sq.free[i] = e(fn, acc, acc, ap, ALU.add, w=[t0, ss["tok"]])
        ss["n"] += 1
        return t0

    def column_sums(src, first, last, w):
        for tb in range(4):
            t = q.put("pe", PE.matmul, (PS[:, CB, tb:tb + 1], src[:, tb * P:(tb + 1) * P], ones[:, 0:1]),
                      dict(start=first and tb == 0, stop=last, skip_group_check=True),
                      list(w) + ([bfree[CB]] if first else []), "pe" if tb == 3 else None, 1)
        return t

    def rstd_rows():
        i, ap, t = ss["last"]
        column_sums(acc, True, False, [ss["tok"], t_c])
        t = column_sums(ap, False, True, [t])
        ss["free"], ss["n"] = t, 0
        sq.free[i] = t
        t = act(S.activation, RC[:, 0:4], PS[:, CB, 0:4], ACT.Sqrt, bias=eps, scale=1.0 / D, w=[t, ss["rc"]])
        bfree[CB] = t
        t = dve(V.reciprocal, RC[:, 0:4], RC[:, 0:4], w=[t])
        w = [t] + q.now()
        for tb in range(4):
            t = dve(V.tensor_scalar, diag[:, tb * P:(tb + 1) * P], ident, RC[:, tb:tb + 1], None, ALU.mult, w=w)
        ss["rc"] = t
        if plan is not None and st["use"] < len(plan):
            advance(st["use"])
        return t

    def rstd_bank(t):
        return mm(bank(RB), ones, diag, True, True, w=[t, bfree[RB]], done=True)

    def finish_rstd():
        return rstd_bank(rstd_rows())

    H = Split(HH, HL)

    def normed(t_r, gain, shift=None, t_g=None):
        begun = {}

        def begin(k):
            i, ap, fr = nt.take()
            t = dve(V.scalar_tensor_tensor, ap, X[:, k, :], gain(k), bank(RB), ALU.mult, ALU.mult, w=[t_r, t_g, x_tok[k], fr])
            bfree[RB] = t
            if shift is None:
                t2 = act(S.activation, HH[:, k, :], ap, ACT.Copy, w=[t])
            else:
                t2 = act(S.activation, HH[:, k, :], ap, ACT.Identity, bias=shift(k), w=[t])
            H.hi_tok[k] = t2
            begun[k] = i, ap, t, t2

        def each(k):
            for j in ((0, 1) if k == 0 else (k + 1,)):
                if j < DK:
                    begin(j)
            i, ap, t, t2 = begun[k]
            hi = HH[:, k, :].bitcast(F32)
            if k % 2:
                if shift is not None:
                    t2 = act(S.activation, ap, ap, ACT.Identity, bias=shift(k), w=[t2])
                t3 = pool(G.tensor_tensor, HL[:, k, :], ap, hi, ALU.subtract, w=[t2, t])
            elif shift is None:
                t3 = dve(V.tensor_tensor, HL[:, k, :], ap, hi, ALU.subtract, w=[t2, t])
            else:
                t3 = dve(V.scalar_tensor_tensor, HL[:, k, :], ap, shift(k), hi, ALU.add, ALU.subtract, w=[t2, t])
            nt.free[i] = t3
            H.tok[k] = t3
        return each

    def scaled(k, src, w, gain):
        t = H.hi_tok[k] = act(S.activation, HH[:, k, :], src, ACT.Copy, scale=gain(k), w=w)
        t = H.tok[k] = dve(V.scalar_tensor_tensor, HL[:, k, :], src, gain(k), HH[:, k, :].bitcast(F32),
                           ALU.mult, ALU.subtract, w=[t] + list(w))
        return t

    def split_to(x, k, src, w, cols=slice(0, T)):
        hi, lo = x.hi[:, k, cols], x.lo[:, k, cols]
        t = act(S.activation, hi, src, ACT.Copy, w=w)
        t = dve(V.tensor_tensor, lo, src, hi.bitcast(F32), ALU.subtract, w=[t] + list(w))
        x.tok[k] = t
        return t

    HG = mem["HG"]

    def turn_vectors(g):
        c0, n = sizes[g]
        t = tr(PS[:, 7, c0:c0 + n], VS[0:n, g, :], C[0:n, C_ID:C_ID + n], w=[t_vs[g], t_c, bfree[7]], done=True)
        bfree[7] = dve(V.tensor_copy, VT[:, c0:c0 + n], PS[:, 7, c0:c0 + n], w=[t])
        return bfree[7]

    def turn_x(k):
        b = 1 + k % 4
        for tb in range(4):
            t = tr(PS[:, b, tb * P:(tb + 1) * P], XR[:, tb, k * P:(k + 1) * P], ident,
                   w=[t_x, t_c, bfree[b]], done=tb == 3)
        x_tok[k] = t

    t_v = turn_vectors(0)
    ada["ca"] = act(S.activation, CA[:, :], VT[:, col["c_2"]:col["c_2"] + 8], ACT.Silu, w=[t_v])
    for k in range(4):
        turn_x(k)
    if plan is not None:
        issue_split(0)
        st["spl"] = 1

    def first_tile(k):
        if k == 4 and plan is not None:
            st["hold"] = False
            advance(0)
        for j in ((0, 1) if k == 0 else (k + 1,)):
            if j < DK:
                b = 1 + j % 4
                bfree[b] = x_tok[j] = dve(V.tensor_copy, X[:, j, :], bank(b), w=[x_tok[j]])
        scaled(k, X[:, k, :], [x_tok[k], t_v], lambda j: vec("ffn1_pre_g", j))

    def first_sums(k):
        late_sums(k)
        if k < 4:
            turn_x(k + 4)

    def late_sums(k):
        for j in ([k - 1] if k else []) + ([k] if k == DK - 1 else []):
            sumsq(X[:, j, :], [x_tok[j]], "pool")

    U = Split(mem["UH"], mem["UL"])
    silu_r = Ring([TS[:, 0, :], TS[:, 1, :]])
    prod_r = Ring([TS[:, 2, :], TS[:, 3, :]])

    RS = TS[:, 8, :]

    def ffn_up(wg, wu, each, after=None, heads=2, scale=False, between=None):
        t = {}
        before = q.now()
        order = [(n, w) for n in range(FK) for w in range(2)]

        def chunk(n, w):
            return wslice((wg, wu)[w], 0, DK, n * P, P), (2 * n) % 4 + w

        for key, tok in zip(order, fm_head([chunk(*o) for o in order[:heads]], H, each, after)):
            t[key] = tok
        if scale:
            tr_ = rstd_rows()
            for n, w in order[heads:4]:
                c, b = chunk(n, w)
                t[n, w] = fm(c, DK, H, 0, b)
            tr_ = rstd_bank(tr_)
            t_rs = bfree[RB] = act(S.activation, RS, bank(RB), ACT.Copy, w=[tr_] + before)
        for i in range(2):
            silu_r.free[i], prod_r.free[i] = nt.free[i], nt.free[2 + i]
        for n in range(FK):
            for w in range(2):
                if (n, w) not in t:
                    c, b = chunk(n, w)
                    t[n, w] = fm(c, DK, H, 0, b)
            bg, bu = (2 * n) % 4, (2 * n) % 4 + 1
            i, s_ap, fr = silu_r.take()
            if scale:
                ts_ = bfree[bg] = dve(V.tensor_tensor, s_ap, bank(bg), RS, ALU.mult, w=[t[n, 0], fr, t_rs] + before)
                ts_ = act(S.activation, s_ap, s_ap, ACT.Silu, w=[ts_])
            else:
                ts_ = bfree[bg] = act(S.activation, s_ap, bank(bg), ACT.Silu, w=[t[n, 0], fr] + before)
            j, p_ap, fr = prod_r.take()
            if scale:
                tp = bfree[bu] = dve(V.tensor_tensor, p_ap, RS, bank(bu), ALU.mult, w=[t[n, 1], fr, t_rs])
                tp = dve(V.tensor_tensor, p_ap, p_ap, s_ap, ALU.mult, w=[ts_, tp])
            else:
                tp = bfree[bu] = dve(V.tensor_tensor, p_ap, s_ap, bank(bu), ALU.mult, w=[ts_, t[n, 1], fr])
            silu_r.free[i] = tp
            prod_r.free[j] = split_to(U, n, p_ap, [tp])
            if between and n == 3:
                between()
        for i in range(2):
            nt.free[i], nt.free[2 + i] = silu_r.free[i], prod_r.free[i]

    def ffn_down(wd, n, b):
        for c, nk in ((0, 8), (8, 8), (16, 6)):
            t = fm(wslice(wd, c * P, nk, n * P, P), nk, U, c, b, first=c == 0, last=c == 16)
        return t

    def keep_f(n, b, t, gain):
        t0 = act(S.activation, F16[:, n, :], bank(b), ACT.Copy, scale=gain(n), w=[t] + gk["hg"])
        bfree[b] = sumsq(bank(b), [t, t0])

    def residual_tile(t_r, k, on_pool):
        i, ap, fr = nt.take()
        t = dve(V.tensor_tensor, ap, F16[:, k, :], bank(RB), ALU.mult, w=[t_r, fr])
        bfree[RB] = t
        e, fn = (pool, G.tensor_tensor) if on_pool else (dve, V.tensor_tensor)
        nt.free[i] = x_tok[k] = e(fn, X[:, k, :], X[:, k, :], ap, ALU.add, w=[t])

    def residual(t_r):
        for k in range(DK + 2):
            if k < DK:
                residual_tile(t_r, k, k % 4 < 3)
            if k > 1:
                sumsq(X[:, k - 2, :], [x_tok[k - 2]])

    def ffn_first(each, after, heads, wg, wu, wd, post, between=None):
        ffn_up(wg, wu, each, after, heads, True, between)
        for n in range(DK):
            keep_f(n, n % 4, ffn_down(wd, n, n % 4), lambda k: HG[:, post + k:post + k + 1])

    def later_vectors():
        for g in range(1, 4):
            t = turn_vectors(g)
        gk["hg"] = []
        for j, name in enumerate(("ffn1_post_g", "ffn2_post_g")):
            gk["hg"].append(dve(V.tensor_scalar, HG[:, 8 * j:8 * j + 8], VT[:, col[name]:col[name] + 8], 0.5, None,
                                ALU.mult, w=[t]))

    gk = {}
    ffn_first(first_tile, first_sums, 1, A["ffn1_w_gate"][0], A["ffn1_w_up"][0], A["ffn1_w_down"][0], 0, later_vectors)
    t_r = finish_rstd()
    residual(t_r)

    t_r = finish_rstd()
    CS1, FMT = mem["CS1"], mem["FMT"]
    before = q.now()
    t_cs = load(CS1[0:32, :], cs_tab, "cs", w=before, eng="pool")
    t_fm = load(FMT[:, :], fm_tab, "fm", w=before, eng="pool")
    w_in = A["w_in"][0]
    SETS = mem["SETS"]
    set_free = [[], []]
    AT, ML, MG = Split(mem["ATH"], mem["ATL"]), Split(mem["MLH"], mem["MLL"]), Split(mem["MGH"], mem["MGL"])

    lb = Ring([0, 1])

    def lbank():
        return lb.take()[1]

    XB = [5, 6]
    def gates():
        ig, xf, nz, lf, cb = (TS[0:4, i, :] for i in range(5))
        t_ig = dve(V.tensor_scalar, ig, PS[0:4, gk["b"], :], IB[:, 0:1], None, ALU.add, w=[gk["t"], t_ib] + before)
        t = dve(V.tensor_scalar, xf, PS[32:36, gk["b"], :], FB[32:36, 0:1], None, ALU.add, w=[gk["t"], t_ib])
        bfree[gk["b"]] = t
        yield
        t1 = act(S.activation, nz, xf, ACT.Abs, w=[t])
        t1 = act(S.activation, nz, nz, ACT.Exp, scale=-1.0, w=[t1])
        t1 = act(S.activation, nz, nz, ACT.Ln, bias=C[0:4, C_ONE:C_ONE + 1], w=[t1])
        t = dve(V.scalar_tensor_tensor, lf, xf, 0.0, nz, ALU.min, ALU.subtract, w=[t1, t])
        t = dve(V.memset, xf, 1.0, w=[t])
        for _ in range(4):
            yield
        t = dve(V.tensor_tensor_scan, cb, xf, lf, 0.0, ALU.mult, ALU.add, w=[t])
        t_av = dve(V.tensor_tensor, ig, ig, cb, ALU.subtract, w=[t, t_ig])
        gk["mx"] = dve(V.tensor_tensor_scan, MX, ig, ig, 0.0, ALU.max, ALU.max, w=[t_av])
        t = dve(V.tensor_tensor, EM, cb, MX, ALU.add, w=[gk["mx"]])
        yield
        gk["em"] = act(S.activation, EM, EM, ACT.Exp, scale=-1.0, w=[t])
        for _ in range(8):
            yield
        b = yield from grab(XB)
        for sb in range(4):
            t = tr(PS[:, b, sb * 4:sb * 4 + 4], ig[:, sb * P:(sb + 1) * P], C[0:4, C_ID:C_ID + 4],
                   w=[t_av, bfree[b]], done=sb == 3)
        for sb in range(4):
            t = tr(PS[:, b, 16 + sb * 4:16 + sb * 4 + 4], EM[:, sb * P:(sb + 1) * P], C[0:4, C_ID:C_ID + 4],
                   w=[gk["em"]], done=sb == 3)
        t = dve(V.tensor_copy, AVT[:, :], PS[:, b, 0:32], w=[t])
        release(b, t)
        gk["avt"] = t

    MX, EM = TS[0:4, 7, :], TS[0:4, 8, :]
    AVT = mem["AVT"]
    gk["b"], q0_bank = 7, lbank()
    gk["t"], t_q0 = fm_head(
        [([(0, w_in[:, 8704:8736]), (32, w_in[:, 8708:8740])], gk["b"]), (wslice(w_in, 0, DK, 0, P), q0_bank)], H, normed(t_r, lambda k: vec("mix_pre_g", k)))
    for e in ("pe", "act", "dve", "pool"):
        q.ops[e].append(("wait", q.sems["c2"], t_c2[1]))
    background.append(gates())
    pump()
    nt.free[0:4] = [None] * 4

    rope_t = Ring([TS[:, 5, :], TS[:, 6, :]])

    def rope_first(dst, t, tok, key):
        x = yield from grab(XB)
        t2 = mm(PS[0:32, x, :], C[0:32, C_R1:C_R1 + 32], dst[0:32, :], True, True, w=[t, bfree[x]], done=True)
        i, ap, fr = rope_t.take()
        t3 = dve(V.tensor_tensor, ap[0:32, :], PS[0:32, x, :], CS1[0:32, T:2 * T], ALU.mult, w=[t2, fr, t_cs] + before)
        release(x, t3)
        t4 = dve(V.tensor_tensor, dst[0:32, :], dst[0:32, :], CS1[0:32, 0:T], ALU.mult, w=[t, t2])
        t4 = dve(V.tensor_tensor, dst[0:32, :], dst[0:32, :], ap[0:32, :], ALU.add, w=[t4, t3])
        rope_t.free[i] = t4
        tok[key] = [t, t4]

    def to_tokens(dst, t, tok, key):
        b = yield from grab(XB)
        for tb in range(4):
            t2 = tr(PS[:, b, tb * P:(tb + 1) * P], dst[:, tb * P:(tb + 1) * P], ident, w=[t, bfree[b]], done=tb == 3)
        t2 = act(S.activation, dst, bank(b), ACT.Copy, w=[t2])
        release(b, t2)
        tok[key] = [t2]

    def att_project(hd, s, tok):
        free = set_free[s]
        for g in range(3):
            for which, base in ((0, 0), (1, 1536), (2, 3072)):
                key = 2 * g + which if which < 2 else 6 + g
                dst = SETS[:, s, key, :]
                if hd == g == which == 0:
                    b, t = q0_bank, t_q0
                else:
                    b = lbank()
                    t = fm(wslice(w_in, 0, DK, base + (4 * g + hd) * P, P), DK, H, 0, b)
                t = act(S.activation, dst, bank(b), ACT.Copy, w=[t] + free)
                bfree[b] = t
                background.append((rope_first if which < 2 else to_tokens)(dst, t, tok, key))

    sm_n = [0]

    def small():
        c = sm_n[0] % 32
        sm_n[0] += 1
        return SM[:, 2 * c:2 * c + 1]

    pt_r = Ring([TS[:, 3, :], TS[:, 4, :]])
    att = dict(s_free=[bfree[2], bfree[3], bfree[4]], p_free=None)
    SCALE = float(P) ** -0.5

    def attention(hd, s, tok):
        while len(tok) < 9:
            yield
        start = q.now() if hd == 0 else []
        for tb in range(4):
            W = (tb + 1) * P
            ts = slice(tb * P, (tb + 1) * P)
            for g in range(3):
                t = mm(PS[:, 2 + g, 0:W], SETS[:, s, 2 * g, ts], SETS[:, s, 2 * g + 1, 0:W], True, True,
                       w=tok[2 * g] + tok[2 * g + 1] + att["s_free"], done=g == 2)
            pr = TS[:, 0:3, 0:W]
            t = dve(V.scalar_tensor_tensor, pr, PS[:, 2:5, 0:W], SCALE,
                    FMT[:, :].rearrange("p (g t) -> p g t", g=3)[:, :, T - W:T],
                    ALU.mult, ALU.add, w=[t, att["p_free"], t_fm] + start)
            att["s_free"] = [t]
            mx, l = small(), small()
            t = dve(V.tensor_reduce, mx, pr, AX.XY, ALU.max, negate=True, w=[t])
            for _ in range((1, 2, 2, 3)[tb]):
                yield
            t = act(S.activation, pr, pr, ACT.Exp, bias=mx, accum_out=l, w=[t])
            for _ in range((1, 1, 2, 2)[tb]):
                yield
            t = dve(V.reciprocal, l, l, w=[t])
            t_p = dve(V.tensor_scalar, pr, pr, l, None, ALU.mult, w=[t])
            for _ in range((1, 2, 2, 2)[tb]):
                yield
            blocks = [(g, sb) for g in range(3) for sb in range(tb + 1) if g > 0 or sb >= tb - 1]
            done = 0
            while done < len(blocks):
                part = blocks[done:done + 4]
                b = yield from grab(XB)
                for j, (g, sb) in enumerate(part):
                    t = tr(PS[:, b, j * P:(j + 1) * P], TS[:, g, sb * P:(sb + 1) * P], ident,
                           w=[t_p, bfree[b]], done=j == len(part) - 1)
                att["p_free"] = t
                i, ap, fr = pt_r.take()
                n = len(part) * P
                t = act(S.activation, ap[:, 0:n], PS[:, b, 0:n], ACT.Copy, w=[t, fr] + start)
                release(b, t)
                yield
                for j, (g, sb) in enumerate(part):
                    m = done + j
                    t2 = mm(PS[:, 7, 0:P], SETS[:, s, 6 + g, sb * P:(sb + 1) * P], ap[:, j * P:(j + 1) * P],
                            m == 0, m == len(blocks) - 1, w=[t, bfree[7]] + tok[6 + g], done=j == len(part) - 1)
                pt_r.free[i] = t2
                done += len(part)
            bfree[7] = split_to(AT, hd, PS[:, 7, 0:P], [t2], cols=ts)
        set_free[s] = [t2] + att["s_free"]

    raw_free = [None, None]

    def conv(s, cc, raw, dst, t, free, tok, key):
        wv = [vec("conv_w", j * 16 + cc) for j in range(4)]
        t2 = dve(V.tensor_scalar, dst, raw, wv[3], vec("conv_b", cc), ALU.mult, ALU.add, w=[t] + free)
        for d in range(1, 4):
            t2 = dve(V.scalar_tensor_tensor, dst[:, d:T], raw[:, 0:T - d], wv[3 - d], dst[:, d:T],
                     ALU.mult, ALU.add, w=[t2])
        raw_free[s] = t2
        for _ in range(3):
            yield
        tok[key] = [act(S.activation, dst, dst, ACT.Silu, w=[t2])]

    def ml_project(hd, s, tok):
        free = set_free[s]
        for which in range(2):
            for c in range(2):
                cc = which * 8 + hd * 2 + c
                dst = SETS[:, s, 2 * which + c, :]
                b = lbank()
                t = fm(wslice(w_in, 0, DK, 4608 + cc * P, P), DK, H, 0, b)
                raw = SETS[:, s, 8, :]
                t = bfree[b] = act(S.activation, raw, bank(b), ACT.Copy, w=[t, raw_free[s]] + free)
                background.append(conv(s, cc, raw, dst, t, free, tok, 2 * which + c))
        for c in range(2):
            b = lbank()
            dst = SETS[:, s, 4 + c, :]
            t = fm(wslice(w_in, 0, DK, 6656 + hd * 256 + c * P, P), DK, H, 0, b)
            t = act(S.activation, dst, bank(b), ACT.Copy, w=[t] + free)
            bfree[b] = t
            background.append(to_tokens(dst, t, tok, 4 + c))
        for c in range(2):
            b = lbank()
            t = fm(wslice(w_in, 0, DK, 7680 + hd * 256 + c * P, P), DK, H, 0, b)
            t = act(S.activation, SETS[:, s, 6 + c, :], bank(b), ACT.Sigmoid, w=[t] + free)
            bfree[b] = t
            tok[6 + c] = [t]

    sfree = [None] * 2

    def mlstm(hd, s, tok):
        while len(tok) < 8 or "avt" not in gk:
            yield
        start = q.now()
        sel = C[0:4, C_SEL + hd * P:C_SEL + (hd + 1) * P]
        b = yield from grab(XB)
        t = mm(bank(b), sel, MX, True, True, w=[gk["mx"], bfree[b]], done=True)
        gt = []
        for sb in range(4):
            c = sb * 4 + hd
            t2 = dve(V.tensor_scalar, TS[:, sb, sb * P:T], PS[:, b, sb * P:T], AVT[:, c:c + 1], 0.0,
                     ALU.subtract, ALU.max, w=[t, gk["avt"]] + start)
            gt.append(t2)
        release(b, t2)
        gt = [act(S.activation, TS[:, sb, sb * P:T], TS[:, sb, sb * P:T], ACT.Exp, scale=-1.0, w=[gt[sb]]) for sb in range(4)]
        yield
        wt = []
        for sb in range(4):
            z = sb % 2
            ns = slice(sb * P, T)
            for c in range(2):
                t = mm(PS[:, 2 + z, ns], SETS[:, s, 2 + c, sb * P:(sb + 1) * P], SETS[:, s, c, ns], c == 0, c == 1,
                       w=tok[c] + tok[2 + c] + [sfree[z]] + att["s_free"], done=c == 1)
            t = dve(V.scalar_tensor_tensor, TS[:, sb, ns], PS[:, 2 + z, ns], 1.0 / 16.0, TS[:, sb, ns],
                    ALU.mult, ALU.mult, w=[t, gt[sb]])
            sfree[z] = t
            dg = TS[:, sb, sb * P:(sb + 1) * P]
            wt.append(dve(V.tensor_tensor, dg, dg, C[:, C_LOW:C_LOW + P], ALU.mult, w=[t]))
            yield
        yield
        b = yield from grab(XB)
        for tb in range(4):
            for sb in range(tb + 1):
                td = mm(PS[:, b, tb:tb + 1], TS[:, sb, tb * P:(tb + 1) * P], ones[:, 0:1], sb == 0, sb == tb,
                        w=[wt[sb], bfree[b]], done=tb == 3 and sb == 3)
        dn, ms = SM[:, 64:68], SM[:, 72:76]
        t = dve(V.tensor_copy, dn, PS[:, b, 0:4], w=[td] + start)
        release(b, t)
        t = dve(V.scalar_tensor_tensor, dn, dn, -1.0, dn, ALU.mult, ALU.max, w=[t])
        t = dve(V.tensor_tensor, dn, dn, AVT[:, 16 + hd:32:4], ALU.max, w=[t, gk["avt"]])
        t_dn = dve(V.reciprocal, dn, dn, w=[t])
        nb, tn = [7, 4], []
        for c in range(2):
            for sb in range(4):
                ns = slice(sb * P, T)
                t1 = mm(PS[:, nb[c], ns], SETS[:, s, 4 + c, sb * P:(sb + 1) * P], TS[:, sb, ns], sb == 0, sb == 3,
                        w=tok[4 + c] + [bfree[nb[c]]] + att["s_free"], done=sb == 3)
            tn.append(t1)
            yield
        hm, sqt = [TS[:, 5, :], TS[:, 6, :]], [TS[:, 0, :], TS[:, 1, :]]
        tq = [act(S.activation, sqt[c], bank(nb[c]), ACT.Square, w=tn) for c in range(2)]
        t = dve(V.tensor_tensor, sqt[0], sqt[0], sqt[1], ALU.add, w=tq)
        for _ in range(2):
            yield
        b = yield from grab(XB)
        for tb in range(4):
            t2 = mm(PS[:, b, tb:tb + 1], sqt[0][:, tb * P:(tb + 1) * P], ones[:, 0:1], True, True, w=[t, bfree[b]], done=tb == 3)
        t = dve(V.tensor_tensor, ms, dn, PS[:, b, 0:4], ALU.mult, w=[t2, t_dn] + start)
        release(b, t)
        t = dve(V.tensor_tensor, ms, ms, dn, ALU.mult, w=[t])
        t = act(S.activation, ms, ms, ACT.Sqrt, bias=eps, scale=1.0 / 256.0, w=[t])
        yield
        t = dve(V.reciprocal, ms, ms, w=[t])
        t = dve(V.tensor_tensor, ms, ms, dn, ALU.mult, w=[t])
        dg = TS[:, 4, :]
        for tb in range(4):
            t2 = dve(V.tensor_scalar, dg[:, tb * P:(tb + 1) * P], ident, ms[:, tb:tb + 1], None, ALU.mult, w=[t] + start)
        yield
        b = yield from grab(XB)
        t = mm(bank(b), ones, dg, True, True, w=[t2, bfree[b]], done=True)
        rs_ = TS[:, 2, :]
        t_rs = act(S.activation, rs_, bank(b), ACT.Copy, w=[t] + tn)
        release(b, t_rs)
        yield
        for c in range(2):
            t2 = bfree[nb[c]] = dve(V.scalar_tensor_tensor, hm[c], bank(nb[c]), vec("mlstm_head_g", 2 * hd + c), rs_,
                                    ALU.mult, ALU.mult, w=[t_rs, tq[c]] + start)
            t2 = dve(V.tensor_tensor, hm[c], hm[c], SETS[:, s, 6 + c, :], ALU.mult, w=[t2] + tok[6 + c])
            k = 2 * hd + c
            for _ in range(3):
                yield
            t3 = act(S.activation, ML.hi[:, k, :], hm[c], ACT.Copy, w=[t2])
            yield
            t2 = ML.tok[k] = dve(V.tensor_tensor, ML.lo[:, k, :], hm[c], ML.hi[:, k, :].bitcast(F32), ALU.subtract, w=[t2, t3])
        set_free[s] = [t2, tn[1]]

    tok = None
    for n in range(8):
        todo, tok = tok, {}
        if todo is not None:
            background.append((attention if n <= 4 else mlstm)((n - 1) % 4, (n - 1) % 2, todo))
        (att_project if n < 4 else ml_project)(n % 4, n % 2, tok)
        drain()

    background.append(mlstm(3, 1, tok))
    wa, wm = A["w_att_branch"][0], A["w_mlstm_branch"][0]
    T1 = mem["T1"]
    before = q.now()
    gate_r = Ring([SETS[:, 0, 8, :], CS1[:, 0:T], CS1[:, T:2 * T]])
    t1_tok = []

    def gated_branch(n, gc, w, x, nk, b):
        t = fm(wslice(w_in, 0, DK, gc + n * P, P), DK, H, 0, b)
        i, ap, fr = gate_r.take()
        t = act(S.activation, ap, bank(b), ACT.Sigmoid, w=[t, fr] + before)
        bfree[b] = t
        b2 = lbank()
        t2 = fm(wslice(w, 0, nk, n * P, P), nk, x, 0, b2)
        return i, ap, t, b2, t2

    for n in range(DK):
        i, ap, t, b2, t2 = gated_branch(n, 8712, wa, AT, 4, lbank())
        t = dve(V.tensor_tensor, T1[:, n, :], ap, bank(b2), ALU.mult, w=[t, t2] + set_free[0] + before)
        gate_r.free[i] = bfree[b2] = t
        t1_tok.append(t)
    drain()
    before = q.now()
    gate_r = Ring([TS[:, i, :] for i in range(4)])
    for n in range(DK):
        i, ap, t, b2, t2 = gated_branch(n, 9736, wm, ML, 8, lbank())
        t = dve(V.tensor_tensor, ap, ap, bank(b2), ALU.mult, w=[t, t2])
        bfree[b2] = t
        t = dve(V.tensor_tensor, ap, ap, T1[:, n, :], ALU.add, w=[t, t1_tok[n]])
        gate_r.free[i] = split_to(MG, n, ap, [t] + before)
    w_out = A["w_out"][0]
    for n in range(DK):
        keep_f(n, n % 4, fm(wslice(w_out, 0, DK, n * P, P), DK, MG, 0, n % 4), lambda k: vec("mix_post_g", k))
    nt.free[0:4] = gate_r.free
    t_r = finish_rstd()

    def second_tile(k):
        for j in ((0, 1) if k == 0 else (k + 1,)):
            if j < DK:
                residual_tile(t_r, j, False)
        scaled(k, X[:, k, :], [x_tok[k]], lambda j: vec("ffn2_pre_g", j))

    ffn_first(second_tile, late_sums, 2, A["ffn2_w_gate"][0], A["ffn2_w_up"][0], A["ffn2_w_down"][0], 8)
    t_r = finish_rstd()
    residual(t_r)

    def mods(l, j, t):
        o = 96 + 16 * l + 8 * j
        sh, gt = 48 * l + 24 * j, 48 * l + 24 * j + 16
        g0 = col[("norm1_g_2", "norm2_g_2")[j]] + 8 * l
        t = dve(V.scalar_tensor_tensor, MOD[:, o:o + 8], MOD[:, sh + 8:sh + 16], 1.0, VT[:, g0:g0 + 8],
                ALU.add, ALU.mult, w=[t])
        return (t, lambda k: MOD[:, o + k:o + k + 1], lambda k: MOD[:, sh + k:sh + k + 1],
                lambda k: MOD[:, gt + k:gt + k + 1])

    while ada["n"] <= 192:
        ada_step()
    t_mod = ada["mod"]
    t_g, gain, shift, gate = mods(0, 0, t_mod)
    POSI = mem["POSI"]
    t_pos = load(POSI[:, :], A["positions_2"][0:1, :].to_broadcast([P, T]), "pos", w=q.now(), eng="pool")
    t_r = finish_rstd()
    w_att = A["attn_w_in_2"][0]
    head_banks = [2, 3]
    CS2 = mem["CS2"]
    cosT, sinT = CS2[:, 0, :], CS2[:, 1, :]
    angles = {}

    def angle_steps(before):
        pf, ang, kr, tmp = (mem["CST"][:, i, :] for i in range(4))
        t = dve(V.tensor_copy, pf, POSI[:, :], w=[t_pos] + before)
        yield
        t = dve(V.tensor_scalar, ang, pf, C[:, C_INVF:C_INVF + 1], None, ALU.mult, w=[t])
        yield
        t = dve(V.tensor_scalar, kr, ang, INV_2PI, ROUND, ALU.mult, ALU.add, w=[t])
        yield
        t = dve(V.tensor_scalar, kr, kr, ROUND, None, ALU.subtract, w=[t])
        yield
        for p in (PI_A, PI_B, PI_C):
            t = dve(V.scalar_tensor_tensor, ang, kr, -p, ang, ALU.mult, ALU.add, w=[t])
            yield
        t = angles["sin"] = dve(V.tensor_scalar, sinT, ang, SIN_MAX, -SIN_MAX, ALU.min, ALU.max, w=[t])
        yield
        t = dve(V.tensor_scalar, ang, ang, PI / 2, None, ALU.add, w=[t])
        yield
        t = dve(V.tensor_scalar, tmp, ang, PI, -2.0 * PI, ALU.is_gt, ALU.mult, w=[t])
        yield
        t = dve(V.tensor_tensor, ang, ang, tmp, ALU.add, w=[t])
        yield
        angles["cos"] = dve(V.tensor_scalar, cosT, ang, SIN_MAX, -SIN_MAX, ALU.min, ALU.max, w=[t])

    steps = angle_steps(q.now())
    tile = normed(t_r, gain, shift, t_g)

    def tile_and_angles(k):
        tile(k)
        for _ in range(2):
            next(steps, None)

    head_toks = fm_head(list(zip([wslice(w_att, 0, DK, 2048, 72), wslice(w_att, 0, DK, 1536, P)], head_banks)),
                        H, tile_and_angles)

    QT, KD, VV, QI, KI = mem["QT"], mem["KD"], mem["VV"], mem["QI"], mem["KI"]
    MASK, WI, SCW = mem["MASK"], mem["WI"], mem["SCW"]
    O = Split(mem["OH"], mem["OL"])
    B64 = C[:, C_B64:C_B64 + P]
    before = q.now()
    xr = Ring([TS[:, 0, :], TS[:, 1, :], ADA[:, 0, :], ADA[:, 1, :]])
    s2r = Ring([TS[:, 2, :], ASUM[:, :]])
    rr = Ring([TS[:, 3, :], TS[:, 4, :]])
    t_ki, t_qi, t_q, t_k, t_vv = {}, {}, {}, {}, {}

    def rope(x_ap, i, t_x_, dst, toks, key, n=P):
        t3 = pool(G.tensor_tensor, dst, x_ap, cosT[0:n], ALU.mult, w=[t_x_, t_cs2] + before)
        b = yield from grab(XB)
        t = mm(PS[0:n, b, :], C[0:n, C_R2:C_R2 + n], x_ap, True, True, w=[t_x_, bfree[b]], done=True)
        yield
        j, ap, fr = rr.take()
        t2 = dve(V.tensor_tensor, ap[0:n], PS[0:n, b, :], sinT[0:n], ALU.mult, w=[t, fr, t_cs2])
        release(b, t2)
        yield
        t3 = dve(V.tensor_tensor, dst, dst, ap[0:n], ALU.add, w=[t3, t2, t])
        rr.free[j] = xr.free[i] = t3
        xr_busy[i] = False
        toks[key] = t3

    xr_busy = [False] * 4

    def take_x():
        while xr_busy[xr.n % 4]:
            pump()
        i, x, fr = xr.take()
        xr_busy[i] = True
        return i, x, fr

    def project(c0, scale=1.0, head=None, n=P):
        if head is None:
            b = lbank()
            t = fm(wslice(w_att, 0, DK, c0, P), DK, H, 0, b)
        else:
            b, t = head_banks[head], head_toks[head]
        i, x, fr = take_x()
        t2 = act(S.activation, x[0:n], PS[0:n, b, :], ACT.Copy, scale=scale, w=[t, fr] + before)
        bfree[b] = t2
        return i, x, b, t, t2

    def index_key(i, xw, t):
        x, n = xw[0:64, :], 64
        B = B64[0:64, 0:64]
        xbk = yield from grab(XB)
        t2 = mm(PS[0:n, xbk, :], B, x, True, True, w=[t, bfree[xbk]], done=True)
        yield
        t0 = dve(V.scalar_tensor_tensor, x, PS[0:n, xbk, :], -1.0 / 64.0, x, ALU.mult, ALU.add, w=[t2, t])
        release(xbk, t0)
        xbk = yield from grab(XB)
        for tb in range(4):
            t2 = tr(PS[:, xbk, tb * 8:tb * 8 + 8], xw[64:72, tb * P:(tb + 1) * P], C[64:72, C_ID + 64:C_ID + 72],
                    w=[t, bfree[xbk]], done=tb == 3)
        t2 = dve(V.tensor_scalar, WI[:, :], PS[:, xbk, 0:32], float(8 ** -0.5 * 64 ** -0.5), None, ALU.mult, w=[t2] + before)
        release(xbk, t2)
        t_ki["wi"] = t2
        yield
        j, s2w, fr = s2r.take()
        s2 = s2w[0:64, :]
        t2 = act(S.activation, s2, x, ACT.Square, w=[t0, fr] + before)
        for _ in range(2):
            yield
        xbk = yield from grab(XB)
        t2 = mm(PS[0:n, xbk, :], B, s2, True, True, w=[t2, bfree[xbk]], done=True)
        t2 = act(S.activation, s2, PS[0:n, xbk, :], ACT.Sqrt, bias=eps[0:n], scale=1.0 / 64.0, w=[t2])
        release(xbk, t2)
        t2 = dve(V.reciprocal, s2, s2, w=[t2])
        t = dve(V.tensor_tensor, x, x, s2, ALU.mult, w=[t0, t2])
        s2r.free[j] = t
        t = dve(V.tensor_scalar, x, x, vec("idx_k_ln_g_2")[0:n], vec("idx_k_ln_b_2")[0:n], ALU.mult, ALU.add, w=[t])
        for _ in range(3):
            yield
        tk = {}
        yield from rope(x, i, t, KI[0:64, :], tk, 0, 64)
        t_ki[0] = dve(V.tensor_copy, KI[64:128, :], KI[0:64, :], w=[tk[0]])

    st["pool"] = True
    i, x, b, _, t_xi = project(2048, head=0, n=72)
    first_qi = project(1536, head=1)

    t_cs2 = act(S.activation, sinT, sinT, ACT.Sin, w=[angles["sin"], angles["cos"]])
    t_cs2 = act(S.activation, cosT, cosT, ACT.Sin, w=[angles["cos"]])
    before = q.now()
    background.append(index_key(i, x, t_xi))
    for c in range(4):
        i, x, b, _, t = project(1536 + c * P) if c else first_qi
        background.append(rope(x, i, t, QI[:, c, :], t_qi, c))
    t_mask = [None] * 4
    tri = C[:, C_TRI:C_TRI + P]
    rel = Ring([TS[:, 5, :], TS[:, 6, :]])
    sring = Ring([2, 3, 4])
    M8 = mem["M8"]
    GT, EQ = TS[:, 8, :], TS[:, 7, :]

    def indexer():
        while len(t_qi) < 4 or len(t_ki) < 2:
            yield
        t_mask[0] = dve(V.tensor_scalar, MASK[:, 0, 0:P], tri, MASKED, None, ALU.max, w=before)
        for tb in range(1, 4):
            W = (tb + 1) * P
            ts = slice(tb * P, (tb + 1) * P)
            sc, wk = SCW[:, 0, 0:W], SCW[:, 1, 0:W]
            relus = []
            for h in range(9):
                if h < 8:
                    b = sring.take()[1]
                    r = slice(64 * (h % 2), 64 * (h % 2) + 64)
                    t = mm(PS[:, b, 0:W], QI[r, h // 2, ts], KI[r, 0:W], True, True, w=[t_qi[h // 2], t_ki[0], bfree[b]], done=True)
                    j, ap, fr = rel.take()
                    t = act(S.activation, ap[:, 0:W], PS[:, b, 0:W], ACT.Relu, w=[t, fr] + before)
                    bfree[b] = t
                    relus.append((j, ap, t))
                if h > 0:
                    j, ap, t = relus[h - 1]
                    wi = WI[:, tb * 8 + h - 1:tb * 8 + h]
                    if h == 1:
                        ta = dve(V.tensor_scalar, sc, ap[:, 0:W], wi, None, ALU.mult, w=[t, t_ki["wi"]] + before)
                    else:
                        ta = dve(V.scalar_tensor_tensor, sc, ap[:, 0:W], wi, sc, ALU.mult, ALU.add, w=[t, ta])
                    rel.free[j] = ta
                    yield
            ta = dve(V.tensor_tensor, sc[:, W - P:W], sc[:, W - P:W], tri, ALU.add, w=[ta])
            src = sc
            for n in range(16):
                ta = dve(V.max, M8[:, :], src, w=[ta])
                if n < 15:
                    ta = dve(V.match_replace, wk, M8[:, :], src, -3.4e38, w=[ta])
                    src = wk
                if n % 2 or gk["slow"]:
                    yield
            cnt, need = small(), small()
            thr = M8[:, 7:8]
            gt, eq, pf_ = GT[:, 0:W], EQ[:, 0:W], wk
            ta = dve(V.tensor_scalar, gt, sc, thr, None, ALU.is_gt, ALU.add, accum_out=cnt, w=[ta] + before)
            tn_ = dve(V.tensor_scalar, need, cnt, -1.0, 128.0, ALU.mult, ALU.add, w=[ta])
            te_ = dve(V.tensor_scalar, eq, sc, thr, None, ALU.is_equal, w=[ta])
            te_ = dve(V.tensor_tensor_scan, pf_, eq, eq, 0.0, ALU.add, ALU.bypass, w=[te_])
            te_ = dve(V.scalar_tensor_tensor, eq, pf_, need, eq, ALU.is_le, ALU.mult, w=[te_, tn_])
            te_ = dve(V.tensor_tensor, gt, gt, eq, ALU.add, w=[te_])
            t_mask[tb] = dve(V.tensor_scalar, MASK[:, tb, 0:W], gt, -1.0, -MASKED, ALU.add, ALU.mult, w=[te_])
            yield

    gk["slow"] = False
    ix = indexer()
    background.append(ix)

    def q_tile(c, i, x, t, j, s2, t2):
        for tb in range(4):
            o = tb * 16 + 2 * c
            t2 = mm(PS[:, 7, o:o + 2], s2[:, tb * P:(tb + 1) * P], B64[:, 0:P:64], True, True, w=[t2, bfree[7]], done=tb == 3)
        s2r.free[j] = t_rq[0] = t2
        yield from rope(x, i, t, QT[:, c, :], t_q, c)

    def k_tile(c, i, x, t, j, s2, t2):
        xbk = yield from grab(XB)
        t2 = mm(bank(xbk), B64, s2, True, True, w=[t2, bfree[xbk]], done=True)
        yield
        t2 = act(S.activation, s2, bank(xbk), ACT.Sqrt, bias=eps, scale=1.0 / 64.0, w=[t2])
        release(xbk, t2)
        yield
        t2 = dve(V.reciprocal, s2, s2, w=[t2])
        t = dve(V.tensor_tensor, x, x, s2, ALU.mult, w=[t, t2])
        s2r.free[j] = t
        for _ in range(5):
            yield
        kt, tk = mem["KT"][:, c, :], {}
        yield from rope(x, i, t, kt, tk, 0)
        for j in range(2):
            src = kt[64 * j:64 * j + 64, :]
            dve(V.tensor_copy, KD[0:64, 2 * c + j, :], src, w=[tk[0]])
            t_k[2 * c + j] = dve(V.tensor_copy, KD[64:128, 2 * c + j, :], src, w=[tk[0]])

    def v_tile(c, x, i, t):
        b = yield from grab(XB)
        for tb in range(4):
            t2 = tr(PS[:, b, tb * P:(tb + 1) * P], x[:, tb * P:(tb + 1) * P], ident, w=[t, bfree[b]], done=tb == 3)
        t2 = act(S.activation, VV[:, :, c * P:(c + 1) * P], bank(b).rearrange("p (t n) -> p t n", t=4), ACT.Copy, w=[t2] + before)
        release(b, t2)
        xr.free[i] = t2
        xr_busy[i] = False
        t_vv[c] = t2

    t_rq = [None]
    for c in range(2):
        i, x, b, t, t2 = project(1280 + c * P)
        background.append(v_tile(c, x, i, t2))
    for fn, n, c0, gname in ((k_tile, 2, 1024, "attn_k_norm_g_2"), (q_tile, 8, 0, "attn_q_norm_g_2")):
        for c in range(n):
            i, x, b, t, t2 = project(c0 + c * P, vec(gname))
            j, s2, fr = s2r.take()
            t3 = act(S.activation, s2, bank(b), ACT.Square, w=[t, t2, fr] + before)
            bfree[b] = t3
            background.append(fn(c, i, x, t2, j, s2, t3))
    if ix in background:
        background.remove(ix)
    drain()
    gk["slow"] = True
    background.append(ix)
    st["pool"] = False
    RQ = mem["RQ"]
    t = act(S.activation, RQ[:, :], PS[:, 7, 0:64], ACT.Sqrt, bias=eps, scale=1.0 / 64.0, w=[t_rq[0]])
    bfree[7] = t
    t = dve(V.reciprocal, RQ[:, :], RQ[:, :], w=[t])
    t_rqs = dve(V.tensor_scalar, RQ[:, :], RQ[:, :], 0.125, None, ALU.mult, w=[t])

    pr_r = Ring([mem["F17"][:, i, :] for i in range(8)])
    PT = [F16[:, 4 * i:4 * i + 4, :].rearrange("p s (a b t) -> p s a b t", a=2, b=2) for i in range(2)]
    pt_free = [None, None]
    before = q.now()

    def probs(tb, g, i4):
        h = 4 * g + i4
        W = (tb + 1) * P
        r = slice(64 * (h % 2), 64 * (h % 2) + 64)
        b = sring.take()[1]
        t = mm(PS[:, b, 0:W], QT[r, h // 2, tb * P:(tb + 1) * P], KD[r, g, 0:W], True, True,
               w=[t_q[h // 2], t_k[g], bfree[b]], done=True)
        j, ap, fr = pr_r.take()
        pr = ap[:, 0:W]
        c = tb * 16 + h
        t = dve(V.scalar_tensor_tensor, pr, PS[:, b, 0:W], RQ[:, c:c + 1], MASK[:, tb, 0:W], ALU.mult, ALU.add,
                w=[t, fr, t_mask[tb], t_rqs] + before)
        bfree[b] = t
        mx, l = small(), small()
        t = dve(V.tensor_reduce, mx, pr, AX.X, ALU.max, negate=True, w=[t])
        t = act(S.activation, pr, pr, ACT.Exp, bias=mx, accum_out=l, w=[t])
        return j, ap, pr, l, t

    def scale_probs(on_pool, j, ap, pr, l, t):
        t = dve(V.reciprocal, l, l, w=[t])
        e, fn = (pool, G.tensor_scalar) if on_pool else (dve, V.tensor_scalar)
        return j, ap, e(fn, pr, pr, l, None, ALU.mult, w=[t])

    def turned(tb, g, i4, j, ap, t):
        b = xb2.take()[1]
        for sb in range(tb + 1):
            t2 = tr(PS[:, b, sb * P:(sb + 1) * P], ap[:, sb * P:(sb + 1) * P], ident, w=[t, bfree[b]], done=sb == tb)
        pr_r.free[j] = t2
        t2 = act(S.activation, PT[g % 2][:, 0:tb + 1, i4 % 2, i4 // 2, :],
                 PS[:, b, 0:(tb + 1) * P].rearrange("p (s t) -> p s t", t=P), ACT.Copy, w=[t2, pt_free[g % 2]] + before)
        bfree[b] = t2
        return t2

    def values(tb, g, t):
        for par in range(2):
            for sb in range(tb + 1):
                t2 = mm(PS[64 * par:64 * par + 64, 7, 0:256], VV[:, sb, g * 64:(g + 1) * 64],
                        PT[g % 2][:, sb, par, :, :].rearrange("p b t -> p (b t)"), sb == 0, sb == tb,
                        w=[t, t_vv[g // 2], bfree[7]], done=par == 1 and sb == tb)
        t = t2
        for i2 in range(2):
            t = split_to(O, 2 * g + i2, PS[:, 7, i2 * P:(i2 + 1) * P], [t2, t], cols=slice(tb * P, (tb + 1) * P))
        bfree[7] = t
        pt_free[g % 2] = t2

    xb2 = Ring([5, 6])
    items = [(tb, g, i4) for tb in range(4) for g in range(4) for i4 in range(4)]
    begun, ready, pending = {}, {}, []
    AHEAD, LATE = 5, 3
    for n in range(len(items) + AHEAD + LATE + 1):
        m = n - AHEAD
        if pending and pending[0][0] <= n:
            values(*pending.pop(0)[1])
        if 0 <= m < len(items):
            t = turned(*items[m], *ready.pop(m))
            if items[m][2] == 3:
                pending.append((n + LATE, (items[m][0], items[m][1], t)))
        if n < len(items):
            while t_mask[items[n][0]] is None:
                pump()
            begun[n] = probs(*items[n])
        if n - 1 in begun:
            ready[n - 1] = scale_probs(items[n - 1][0] < 3 or n % 2, *begun.pop(n - 1))
        if n % 2:
            pump()

    def gated(n, b, t, gate_):
        x_tok[n] = dve(V.scalar_tensor_tensor, X[:, n, :], bank(b), gate_(n), X[:, n, :], ALU.mult, ALU.add, w=[t, x_tok[n]])
        bfree[b] = x_tok[n]
        sumsq(X[:, n, :], [x_tok[n]])

    nt.free[0:4] = [t_mask[3]] * 4
    for n in range(DK):
        gated(n, n % 4, fm(wslice(A["attn_w_out_2"][0], 0, DK, n * P, P), DK, O, 0, n % 4), gate)

    def ffn_second(l):
        t_g, gain, shift, gate = mods(l, 1, t_mod)
        ffn_up(A["ffn_w_gate_2"][l], A["ffn_w_up_2"][l], normed(finish_rstd(), gain, shift, t_g))
        for n in range(DK):
            t = ffn_down(A["ffn_w_down_2"][l], n, n % 4)
            gated(n, n % 4, t, gate)

    ffn_second(0)

    t_g, gain, shift, gate = mods(1, 0, t_mod)
    t_r = finish_rstd()
    CV = Split(mem["CVH"], mem["CVL"])
    wc = A["conv_w_in_2"][0]
    def three(n):
        return [wslice(wc, 0, DK, j * D + n * P, P) for j in (1, 2, 0)]

    head_toks = fm_head(list(zip(three(0)[:2], (0, 1))), H, normed(t_r, gain, shift, t_g))
    head_toks.append(fm(three(0)[2], DK, H, 0, 2))
    before = q.now()
    zr = Ring([TS[:, 0, :], TS[:, 1, :]])
    yr = Ring([TS[:, 2, :], TS[:, 3, :]])
    for n in range(DK):
        bs = [0, 1, 2] if n % 2 == 0 else [3, 6, 7]
        tt = head_toks if n == 0 else [fm(c, DK, H, 0, b) for c, b in zip(three(n), bs)]
        i, z, fr = zr.take()
        t = act(S.activation, z, bank(bs[0]), ACT.Copy, w=[tt[0], fr] + before)
        bfree[bs[0]] = t
        t = dve(V.tensor_tensor, z, z, bank(bs[1]), ALU.mult, w=[t, tt[1]])
        bfree[bs[1]] = t
        j, y, fr = yr.take()
        w3 = [vec("conv_w_2", m * 8 + n) for m in range(3)]
        t = dve(V.tensor_scalar, y, z, w3[2], None, ALU.mult, w=[t, fr] + before)
        for d in (1, 2):
            t = dve(V.scalar_tensor_tensor, y[:, d:T], z[:, 0:T - d], w3[2 - d], y[:, d:T], ALU.mult, ALU.add, w=[t])
        zr.free[i] = t
        t = dve(V.tensor_tensor, y, y, bank(bs[2]), ALU.mult, w=[t, tt[2]])
        bfree[bs[2]] = t
        yr.free[j] = split_to(CV, n, y, [t])
    nt.free[0:4] = [yr.free[(DK - 1) % 2]] * 4
    for n in range(DK):
        gated(n, n % 4, fm(wslice(A["conv_w_out_2"][0], 0, DK, n * P, P), DK, CV, 0, n % 4), gate)
    ffn_second(1)

    OUT = mem["OUT"]
    before = q.now()
    for tb in range(4):
        for half in range(2):
            b = (2 * tb + half) % 4
            for j in range(4):
                k = half * 4 + j
                t = tr(PS[:, b, j * P:(j + 1) * P], X[:, k, tb * P:(tb + 1) * P], ident, w=[x_tok[k], bfree[b]], done=j == 3)
            t = dve(V.tensor_copy, OUT[:, tb, half * 512:(half + 1) * 512], bank(b), w=[t] + before)
            bfree[b] = t
        t_out = load(out[0, tb * P:(tb + 1) * P, :], OUT[:, tb, :], "out", w=[t])
    q.ops["sp"].append(("wait", q.sems["out"], t_out[1]))
    return chunks


def build(nc, A, out, cst, cs_tab, fm_tab):
    with ExitStack() as ctx:
        base = 16512
        top = [base]

        def at(name, shape, dt, off):
            return nc.alloc_sbuf_tensor_at(name, shape, dt, offset=off)

        def new(name, shape, dt=F32):
            n = 4
            for s in shape[1:]:
                n *= s
            off = top[0]
            top[0] += (n + 31) // 32 * 32
            return at(name, shape, dt, off)

        mem = {}
        mem["X"] = new("X", [P, DK, T])
        ho = top[0]
        mem["HH"] = new("HH", [P, DK, T], F32R)
        mem["HL"] = new("HL", [P, DK, T], F32R)
        mem["F16"] = at("F16", [P, DK, T], F32, ho)
        mem["F17"] = at("F17", [P, DK, T], F32, ho + 4 * DK * T)
        uo = top[0]
        mem["UH"] = new("UH", [P, FK, T], F32R)
        mem["UL"] = new("UL", [P, FK, T], F32R)

        def over(name, shape, dt, off):
            mem[name] = at(name, shape, dt, uo + off)

        over("XR", [P, 4, D], F32, 0)
        over("VS", [P, 4, P], F32, 16384)
        over("ATH", [P, 4, T], F32R, 0)
        over("ATL", [P, 4, T], F32R, 8192)
        over("MLH", [P, 8, T], F32R, 16384)
        over("MLL", [P, 8, T], F32R, 32768)
        over("SETS", [P, 2, 9, T], F32, 49152)
        over("FMT", [P, 3 * T], F32, 16384)
        over("T1", [P, 8, T], F32, 49152)
        over("CS1", [P, 2 * T], F32, 86016)
        over("MGH", [P, 8, T], F32R, 49152)
        over("MGL", [P, 8, T], F32R, 65536)
        over("CST", [P, 4, T], F32, 67968)
        over("QT", [P, 8, T], F32, 0)
        over("KD", [P, 4, T], F32, 16384)
        over("VV", [P, 4, 256], F32, 24576)
        over("QI", [P, 4, T], F32, 28672)
        over("KI", [P, T], F32, 36864)
        over("MASK", [P, 4, T], F32, 38912)
        over("WI", [P, 32], F32, 47104)
        over("RQ", [P, 64], F32, 47232)
        over("OH", [P, 8, T], F32R, 51584)
        over("OL", [P, 8, T], F32R, 67968)
        over("KT", [P, 2, T], F32, 51584)
        over("SCW", [P, 2, T], F32, 47488)
        over("CS2", [P, 2, T], F32, 84352)
        over("POSI", [P, T], I32, 0)
        over("CVH", [P, 8, T], F32R, 0)
        over("CVL", [P, 8, T], F32R, 16384)
        over("OUT", [P, 4, D], F32, 0)
        mem["RAW"] = new("RAW", [P, NRAW, DK, P])
        mem["WH"] = new("WH", [P, NSPL, DK, P], F32R)
        mem["WL"] = new("WL", [P, NSPL, DK, P], F32R)
        mem["C"] = new("C", [P, C_N])
        mem["TS"] = new("TS", [P, 9, T])
        mem["ADA"] = new("ADA", [P, 2, 512])
        mem["ASUM"] = new("ASUM", [P, 512])
        mem["RC"] = new("RC", [P, 8])
        mem["VT"] = new("VT", [P, 304])
        mem["MOD"] = new("MOD", [P, 128])
        mem["HG"] = new("HG", [P, 16])
        mem["CA"] = new("CA", [P, 8])
        mem["SM"] = new("SM", [P, 80])
        mem["M8"] = new("M8", [P, 8])
        mem["AVT"] = new("AVT", [P, 32])
        mem["IB"] = new("IB", [4, 1])
        mem["FB"] = new("FB", [36, 1])
        mem["PS"] = ctx.enter_context(nc.psum_tensor("PS", [P, 8, 512], F32))

        names = ["pe", "act", "dve", "pool", "c", "c2", "x", "vs0", "vs1", "vs2", "vs3", "ib", "cs", "fm", "pos", "out", "ada0", "ada1"] + [f"raw{i}" for i in range(NRAW)]
        sems = {n: ctx.enter_context(nc.semaphore(f"s_{n}")) for n in names}
        plan = program(nc, Queues(sems), mem, A, out, cst, cs_tab, fm_tab, None)
        q = Queues(sems)
        program(nc, q, mem, A, out, cst, cs_tab, fm_tab, plan)
        block = ctx.enter_context(nc.Block())

        @block.sync
        def _(e):
            q.run("sp", e)

        @block.gpsimd
        def _(e):
            q.run("pool", e)

        @block.scalar
        def _(e):
            q.run("act", e)

        @block.vector
        def _(e):
            q.run("dve", e)

        @block.tensor
        def _(e):
            q.run("pe", e)


_INS = ['x', 'ffn1_pre_g', 'ffn1_w_gate', 'ffn1_w_up', 'ffn1_w_down', 'ffn1_post_g', 'mix_pre_g', 'w_in', 'conv_w',
        'conv_b', 'mlstm_i_bias', 'mlstm_f_bias', 'mlstm_head_g', 'w_att_branch', 'w_mlstm_branch', 'w_out',
        'mix_post_g', 'ffn2_pre_g', 'ffn2_w_gate', 'ffn2_w_up', 'ffn2_w_down', 'ffn2_post_g', 'c_2', 'positions_2',
        'ada_w_2', 'ada_b_2', 'norm1_g_2', 'norm2_g_2', 'attn_w_in_2', 'attn_q_norm_g_2', 'attn_k_norm_g_2',
        'idx_k_ln_g_2', 'idx_k_ln_b_2', 'attn_w_out_2', 'conv_w_in_2', 'conv_w_2', 'conv_w_out_2', 'ffn_w_gate_2',
        'ffn_w_up_2', 'ffn_w_down_2']


def kernel(**inputs):
    import concourse.bacc as _bacc
    from concourse.bass_utils import run_bass_kernel_spmd as _run

    nc = _bacc.Bacc("TRN2", target_bir_lowering=False, num_devices=1)
    arrays, args = {}, {}
    for name in _INS:
        a = np.ascontiguousarray(inputs[name])
        arrays[f"in_{name}"] = a
        args[name] = nc.dram_tensor(f"in_{name}", a.shape, mybir.dt.from_np(a.dtype), kind="ExternalInput").ap()
    cst, cs_tab, fm_tab = constants()
    extra = []
    for name, a in (("const_tab", cst), ("const_rot", cs_tab), ("const_band", fm_tab)):
        arrays[name] = a
        extra.append(nc.dram_tensor(name, a.shape, F32, kind="ExternalInput").ap())
    out = nc.dram_tensor("out_x", (1, T, D), F32, kind="ExternalOutput").ap()
    build(nc, args, out, *extra)
    r = _run(nc, [arrays], core_ids=[0])
    return r.results[0]["out_x"]
```
